# Optimizing a Trainium2 kernel written in Bass

```python
import math
import jax, jax.numpy as jnp
from jax import lax
import numpy as np

D_MODEL = 1024
BATCH = 1
SEQ = 1024
DEPTH = 2

D_MIX = D_MODEL
MIX_CHUNK = 128
SPATIAL_CHUNK = 128
M_WIDTH = 3 * D_MODEL // 8
M_HEADS = 4
M_HEAD_DIM = M_WIDTH // M_HEADS
M_CONV = 4
M_BLOCK = 4
M_NBLOCKS = M_WIDTH // M_BLOCK
R_WIDTH = 3 * D_MODEL // 8
R_HEADS = 6
R_HEAD_DIM = R_WIDTH // R_HEADS
ROPE_THETA = 10000.0
G_WIDTH = D_MIX - M_WIDTH - R_WIDTH
G_GROUPS = 4
G_GROUP_DIM = G_WIDTH // G_GROUPS
D_FF = 4 * D_MODEL
EPS = 1e-6
IN_SIZES = (M_WIDTH, M_WIDTH, M_HEADS, M_HEADS, R_WIDTH, R_WIDTH, R_WIDTH, R_WIDTH, G_WIDTH, G_WIDTH)
N_IN = 2 * M_WIDTH + 2 * M_HEADS + 4 * R_WIDTH + 2 * G_WIDTH

kernel_name = "hybrid_mlstm_retention_gmlp_trunk"

def rmsnorm(x, g):
    xf = x.astype(jnp.float32)
    y = xf * lax.rsqrt(jnp.mean(jnp.square(xf), axis=-1, keepdims=True) + EPS)
    return (y * g.astype(jnp.float32)).astype(x.dtype)

def causal_depthwise_conv(x, w, b):
    k_w = w.shape[0]
    s = x.shape[1]
    xp = jnp.pad(x, ((0, 0), (k_w - 1, 0), (0, 0)))
    return sum(xp[:, j:j + s] * w[j] for j in range(k_w)) + b

def rotary(x):
    s, d = x.shape[1], x.shape[3]
    half = d // 2
    pos = jnp.arange(s, dtype=jnp.float32)
    freqs = ROPE_THETA ** (-jnp.arange(half, dtype=jnp.float32) / half)
    ang = pos[:, None] * freqs[None, :]
    cos = jnp.cos(ang)[None, :, None, :]
    sin = jnp.sin(ang)[None, :, None, :]
    xf = x.astype(jnp.float32)
    x1, x2 = xf[..., :half], xf[..., half:]
    return jnp.concatenate([x1 * cos - x2 * sin, x2 * cos + x1 * sin], axis=-1)

def to_chunks(x, chunk):
    b, s = x.shape[0], x.shape[1]
    xc = x.astype(jnp.float32).reshape((b, s // chunk, chunk) + x.shape[2:])
    perm = (0, 3, 1, 2) + tuple(range(4, xc.ndim))
    return xc.transpose(perm)

def from_chunks(x):
    b, h, nc, l, d = x.shape
    return x.transpose(0, 2, 3, 1, 4).reshape(b, nc * l, h, d)

def mlstm_chunkwise(q, k, v, i_pre, f_pre):
    d = q.shape[-1]
    l = MIX_CHUNK
    qc = to_chunks(q, l)
    kc = to_chunks(k, l) * (d ** -0.5)
    vc = to_chunks(v, l)
    ig = to_chunks(i_pre, l)
    logf = jax.nn.log_sigmoid(to_chunks(f_pre, l))
    bcum = jnp.cumsum(logf, axis=-1)
    b_end = bcum[..., -1]
    causal = jnp.tril(jnp.ones((l, l), dtype=bool))
    dmat = jnp.where(causal, bcum[..., :, None] - bcum[..., None, :] + ig[..., None, :], -jnp.inf)
    w_end = b_end[..., None] - bcum + ig
    a_c = jnp.max(w_end, axis=-1)
    e_end = jnp.exp(w_end - a_c[..., None])
    c_chunk = jnp.einsum('bhcl,bhcld,bhcle->bhcde', e_end, kc, vc)
    n_chunk = jnp.einsum('bhcl,bhcld->bhcd', e_end, kc)

    def step(carry, inp):
        c_st, n_st, m_st = carry
        be, ac, cc, nc = inp
        m_new = jnp.maximum(be + m_st, ac)
        s_old = jnp.exp(be + m_st - m_new)
        s_new = jnp.exp(ac - m_new)
        c_new = s_old[..., None, None] * c_st + s_new[..., None, None] * cc
        n_new = s_old[..., None] * n_st + s_new[..., None] * nc
        return (c_new, n_new, m_new), (c_st, n_st, m_st)

    bsz, h = qc.shape[0], qc.shape[1]
    init = (jnp.zeros((bsz, h, d, d), jnp.float32), jnp.zeros((bsz, h, d), jnp.float32),
            jnp.zeros((bsz, h), jnp.float32))
    xs = (jnp.moveaxis(b_end, 2, 0), jnp.moveaxis(a_c, 2, 0),
          jnp.moveaxis(c_chunk, 2, 0), jnp.moveaxis(n_chunk, 2, 0))
    _, (c_prev, n_prev, m_prev) = lax.scan(step, init, xs)
    c_prev = jnp.moveaxis(c_prev, 0, 2)
    n_prev = jnp.moveaxis(n_prev, 0, 2)
    m_prev = jnp.moveaxis(m_prev, 0, 2)

    inter_log = bcum + m_prev[..., None]
    m_t = jnp.maximum(inter_log, jnp.max(dmat, axis=-1))
    s_inter = jnp.exp(inter_log - m_t)
    wts = jnp.exp(dmat - m_t[..., None])
    scores = jnp.einsum('bhcld,bhcsd->bhcls', qc, kc) * wts
    num = (jnp.einsum('bhcls,bhcse->bhcle', scores, vc)
           + s_inter[..., None] * jnp.einsum('bhcld,bhcde->bhcle', qc, c_prev))
    den = jnp.sum(scores, axis=-1) + s_inter * jnp.einsum('bhcld,bhcd->bhcl', qc, n_prev)
    hout = num / jnp.maximum(jnp.abs(den), jnp.exp(-m_t))[..., None]
    return from_chunks(hout)

def retention_chunkwise(q, k, v):
    h, d = q.shape[2], q.shape[3]
    l = MIX_CHUNK
    qc = to_chunks(q, l)
    kc = to_chunks(k, l) * (d ** -0.5)
    vc = to_chunks(v, l)
    log_gamma = jnp.log(1.0 - 2.0 ** (-5.0 - jnp.arange(h, dtype=jnp.float32)))
    pos = jnp.arange(l, dtype=jnp.float32)
    causal = jnp.tril(jnp.ones((l, l), dtype=bool))
    rel = jnp.where(causal, pos[:, None] - pos[None, :], 0.0)
    decay = jnp.where(causal, jnp.exp(rel[None] * log_gamma[:, None, None]), 0.0)
    scores = jnp.einsum('bhcld,bhcsd->bhcls', qc, kc) * decay[None, :, None]
    intra = jnp.einsum('bhcls,bhcse->bhcle', scores, vc)
    zeta = jnp.exp((l - 1.0 - pos)[None, :] * log_gamma[:, None])
    kv_chunk = jnp.einsum('bhcld,bhcle,hl->bhcde', kc, vc, zeta)
    chunk_decay = jnp.exp(l * log_gamma)[None, :, None, None]

    def step(r_st, kv):
        return chunk_decay * r_st + kv, r_st

    bsz = qc.shape[0]
    _, r_prev = lax.scan(step, jnp.zeros((bsz, h, d, d), jnp.float32), jnp.moveaxis(kv_chunk, 2, 0))
    r_prev = jnp.moveaxis(r_prev, 0, 2)
    xi = jnp.exp((pos + 1.0)[None, :] * log_gamma[:, None])
    cross = jnp.einsum('bhcld,bhcde->bhcle', qc, r_prev) * xi[None, :, None, :, None]
    return from_chunks(intra + cross)

def chunked_spatial_gating(u, v, w_s, b_s):
    bsz, s, g, e = v.shape
    l = SPATIAL_CHUNK
    causal = jnp.tril(jnp.ones((l, l), dtype=bool))
    w = jnp.where(causal[None], w_s, 0.0).astype(v.dtype)
    vc = v.reshape(bsz, s // l, l, g, e)
    mixed = jnp.einsum('gts,bcsge->bctge', w, vc) + b_s.T.astype(v.dtype)[None, None, :, :, None]
    return u * mixed.reshape(bsz, s, g, e)

def hybrid_mixer(h, w_in, m_conv_w, m_conv_b, m_wq, m_wk, m_wv, m_i_bias, m_f_bias, m_norm_g,
                 m_skip, r_norm_g, g_norm_g, g_ws, g_bs, w_out):
    bsz, s, _ = h.shape
    dt = h.dtype
    proj = h @ w_in
    split_at = list(np.cumsum(IN_SIZES)[:-1])
    m_x, m_z, m_i, m_f, r_q, r_k, r_v, r_g, g_u, g_v = jnp.split(proj, split_at, axis=-1)

    x_c = jax.nn.silu(causal_depthwise_conv(m_x, m_conv_w, m_conv_b))
    xc_b = x_c.reshape(bsz, s, M_NBLOCKS, M_BLOCK)
    xm_b = m_x.reshape(bsz, s, M_NBLOCKS, M_BLOCK)
    q = jnp.einsum('bsni,nij->bsnj', xc_b, m_wq).reshape(bsz, s, M_HEADS, M_HEAD_DIM)
    k = jnp.einsum('bsni,nij->bsnj', xc_b, m_wk).reshape(bsz, s, M_HEADS, M_HEAD_DIM)
    v = jnp.einsum('bsni,nij->bsnj', xm_b, m_wv).reshape(bsz, s, M_HEADS, M_HEAD_DIM)
    hm = mlstm_chunkwise(q, k, v, m_i + m_i_bias, m_f + m_f_bias)
    hm = rmsnorm(hm, m_norm_g.reshape(M_HEADS, M_HEAD_DIM)).reshape(bsz, s, M_WIDTH).astype(dt)
    out_m = (hm + m_skip * x_c) * jax.nn.silu(m_z)

    rq = rotary(r_q.reshape(bsz, s, R_HEADS, R_HEAD_DIM))
    rk = rotary(r_k.reshape(bsz, s, R_HEADS, R_HEAD_DIM))
    hr = retention_chunkwise(rq, rk, r_v.reshape(bsz, s, R_HEADS, R_HEAD_DIM))
    hr = rmsnorm(hr, r_norm_g.reshape(R_HEADS, R_HEAD_DIM)).reshape(bsz, s, R_WIDTH).astype(dt)
    out_r = hr * jax.nn.silu(r_g)

    gu = jax.nn.gelu(g_u)
    gv = rmsnorm(jax.nn.gelu(g_v), g_norm_g)
    out_g = chunked_spatial_gating(gu.reshape(bsz, s, G_GROUPS, G_GROUP_DIM),
                                   gv.reshape(bsz, s, G_GROUPS, G_GROUP_DIM),
                                   g_ws, g_bs).reshape(bsz, s, G_WIDTH)

    return jnp.concatenate([out_m, out_r, out_g], axis=-1) @ w_out

def setup_inputs(seed: int = 0) -> dict:
    key = jax.random.key(seed)
    ks = jax.random.split(key, 24)
    f32 = jnp.float32

    def nrm(k, shape, scale):
        return jax.random.normal(k, shape, f32) * scale

    def gain(k, shape):
        return 1.0 + 0.05 * jax.random.normal(k, shape, f32)

    x = jax.random.normal(ks[0], (BATCH, SEQ, D_MODEL), f32)
    norm_mix_g = gain(ks[1], (DEPTH, D_MODEL))
    w_in = nrm(ks[2], (DEPTH, D_MODEL, N_IN), D_MODEL ** -0.5)
    m_conv_w = nrm(ks[3], (DEPTH, M_CONV, M_WIDTH), M_CONV ** -0.5)
    m_conv_b = nrm(ks[4], (DEPTH, M_WIDTH), 0.02)
    m_wq = nrm(ks[5], (DEPTH, M_NBLOCKS, M_BLOCK, M_BLOCK), M_BLOCK ** -0.5)
    m_wk = nrm(ks[6], (DEPTH, M_NBLOCKS, M_BLOCK, M_BLOCK), M_BLOCK ** -0.5)
    m_wv = nrm(ks[7], (DEPTH, M_NBLOCKS, M_BLOCK, M_BLOCK), M_BLOCK ** -0.5)
    m_i_bias = nrm(ks[8], (DEPTH, M_HEADS), 0.1)
    m_f_bias = (jnp.linspace(3.0, 6.0, M_HEADS, dtype=f32)[None, :]
                + nrm(ks[9], (DEPTH, M_HEADS), 0.1))
    m_norm_g = gain(ks[10], (DEPTH, M_WIDTH))
    m_skip = gain(ks[11], (DEPTH, M_WIDTH))
    r_norm_g = gain(ks[12], (DEPTH, R_WIDTH))
    g_norm_g = gain(ks[13], (DEPTH, G_WIDTH))
    g_ws = nrm(ks[14], (DEPTH, G_GROUPS, SPATIAL_CHUNK, SPATIAL_CHUNK), SPATIAL_CHUNK ** -0.5)
    g_bs = gain(ks[15], (DEPTH, G_GROUPS, SPATIAL_CHUNK))
    w_out = nrm(ks[16], (DEPTH, D_MIX, D_MODEL), D_MIX ** -0.5)
    norm_ff_g = gain(ks[17], (DEPTH, D_MODEL))
    w_ff1 = nrm(ks[18], (DEPTH, D_MODEL, D_FF), D_MODEL ** -0.5)
    w_ff2 = nrm(ks[19], (DEPTH, D_FF, D_MODEL), D_FF ** -0.5)
    final_norm_g = gain(ks[20], (D_MODEL,))
    return {"x": x, "norm_mix_g": norm_mix_g, "w_in": w_in, "m_conv_w": m_conv_w,
            "m_conv_b": m_conv_b, "m_wq": m_wq, "m_wk": m_wk, "m_wv": m_wv,
            "m_i_bias": m_i_bias, "m_f_bias": m_f_bias, "m_norm_g": m_norm_g,
            "m_skip": m_skip, "r_norm_g": r_norm_g, "g_norm_g": g_norm_g,
            "g_ws": g_ws, "g_bs": g_bs, "w_out": w_out, "norm_ff_g": norm_ff_g,
            "w_ff1": w_ff1, "w_ff2": w_ff2, "final_norm_g": final_norm_g}

def reference(x, norm_mix_g, w_in, m_conv_w, m_conv_b, m_wq, m_wk, m_wv, m_i_bias, m_f_bias,
              m_norm_g, m_skip, r_norm_g, g_norm_g, g_ws, g_bs, w_out, norm_ff_g, w_ff1, w_ff2,
              final_norm_g):
    for layer in range(DEPTH):
        h = rmsnorm(x, norm_mix_g[layer])
        x = x + hybrid_mixer(h, w_in[layer], m_conv_w[layer], m_conv_b[layer], m_wq[layer],
                             m_wk[layer], m_wv[layer], m_i_bias[layer], m_f_bias[layer],
                             m_norm_g[layer], m_skip[layer], r_norm_g[layer], g_norm_g[layer],
                             g_ws[layer], g_bs[layer], w_out[layer])
        h2 = rmsnorm(x, norm_ff_g[layer])
        x = x + jnp.square(jax.nn.relu(h2 @ w_ff1[layer])) @ w_ff2[layer]
    return rmsnorm(x, final_norm_g)


_drawn_inputs = setup_inputs


def setup_inputs(seed=0):
    import zlib

    import numpy as np

    out = dict(_drawn_inputs(seed))
    spreads = {}
    factors = {'m_conv_b': 3.446,
     'm_i_bias': 64.0,
     'm_skip': 4.267,
     'g_norm_g': 4.142,
     'g_bs': 2.912,
     'm_norm_g': 4.19,
     'r_norm_g': 4.275}
    for name, (base, spread) in spreads.items():
        noise = np.random.default_rng([zlib.crc32(name.encode()), seed]).standard_normal(out[name].shape)
        drawn = base * np.exp(spread * noise) if base else spread * noise
        out[name] = __import__('jax').numpy.asarray(drawn.astype(out[name].dtype))
    for name, factor in factors.items():
        out[name] = (out[name] * factor).astype(out[name].dtype)
    return out
```

```python
from contextlib import ExitStack

import concourse.bass as bass
from concourse import mybir
from concourse.alu_op_type import AluOpType as ALU

F32 = mybir.dt.float32
F32R = mybir.dt.float32r
ACT = mybir.ActivationFunctionType
AX_X = mybir.AxisListType.X

P = 128
D = 1024
S = 1024
DEPTH = 2
KT = D // P
T = 512
HALVES = S // T
L = 128
NC = T // L
MW = RW = 384
MT = MW // P
MH, MD = 4, 96
RH, RD = 6, 64
GW, GG, GD = 256, 4, 64
GT = GW // P
FF = 4096
FG = 4
GROUPS = FF // P // FG
EPS = 1e-6
BIG = 1.0e30

RING = 3
RAW = 2
U_GATE, U_GV, U_GU, U_MX, U_Z, U_RG, U_RQ, U_RK, U_RV, U_OUT = 0, 1, 3, 5, 8, 11, 14, 17, 21, 24
PADS = (20, 32)
HALF_UNITS = [u for u in range(33) if u not in PADS]
GROUP_UNITS = list(range(8))

PIECES = [(h, t) for h in range(MH) for t in range(MT) if max(MD * h, P * t) < min(MD * h + MD, P * t + P)]

SMALL = {}
_n = 0
for _name, _w in (("g_mix", KT), ("g_ff", KT), ("conv_w", 4 * MT), ("conv_b", MT), ("skip", MT), ("m_norm", MT),
                  ("r_norm", MT), ("i_bias", 1), ("f_bias", 1), ("wq", 4 * MT), ("wk", 4 * MT), ("wv", 4 * MT),
                  ("bs", GT * L), ("g_norm", GW), ("ws", GG * L)):
    SMALL[_name] = (_n, _n + _w)
    _n += _w
N_SMALL = _n

CONST = {}
_n = 0
for _name, _w in (("upper", L), ("causal", L), ("blocks", L), ("eye", P), ("swap", P), ("ones", P),
                  ("decay", 2 * MT * L), ("xi", MT * L), ("gl", MT), ("zeta", RH), ("sel", MH * P),
                  ("eye4", 4), ("zero", L), ("final_g", KT), ("eps", 1), ("one", 1)):
    CONST[_name] = (_n, _n + _w)
    _n += _w
N_CONST = _n

SECTIONS = ("pre", "half", "norm", "group")
TIMES = {"pre": 1, "half": HALVES, "norm": 1, "group": GROUPS}
RAISED = {
    "x_loaded": (0, 0, 0, 0, 0),
    "const_loaded": (0, 0, 0, 0, 0),
    "small_loaded": (0, 16, 0, 0, 0),
    "rope_loaded": (0, 0, 32, 0, 0),
    "raw0_full": (0, 0, 16 * 16, 0, 16 * 4),
    "raw1_full": (0, 0, 16 * 15, 0, 16 * 4),
    "hi_done": (0, 0, 33, 0, 9),
    "w_ready": (3, 0, 33, 0, 9),
    "pa_full": (0, 0, 40, 4, 8),
    "pa_taken": (4, 0, 40, 4, 8),
    "pv_full": (8, 0, 72, 0, 16),
    "pv_taken": (4, 0, 72, 0, 16),
    "sq_ready": (0, 0, 8, 16, 0),
    "sq_free": (0, 0, 7, 14, 0),
    "rstd_ready": (0, 0, 1, 2, 0),
    "h_ready": (0, 0, 8, 16, 0),
    "hh_done": (0, 0, 8, 16, 0),
    "hl_ready": (1, 0, 8, 16, 0),
    "layer_ready": (0, 1, 0, 0, 0),
    "conv_done": (0, 0, 3, 0, 0),
    "xc_ready": (0, 0, 3, 0, 0),
    "softplus_ready": (0, 0, 1, 0, 0),
    "rows_ready": (0, 0, 1, 0, 0),
    "rows_exp": (0, 0, 1, 0, 0),
    "sold_ready": (0, 0, 1, 0, 0),
    "gvn_ready": (0, 0, 1, 0, 0),
    "rqk_ready": (0, 0, 6, 0, 0),
    "e_ready": (0, 0, 4, 0, 0),
    "ss_ready": (0, 0, 9, 0, 0),
    "rs_ready": (0, 0, 9, 0, 0),
    "mn_ready": (0, 0, 4, 0, 0),
    "rn_ready": (0, 0, 4, 0, 0),
    "y_ready": (0, 0, 6, 0, 0),
    "oh_done": (0, 0, 10, 0, 0),
    "o_ready": (0, 0, 10, 0, 0),
    "sq_done": (0, 0, 0, 0, 8),
    "dh_done": (0, 0, 0, 0, 8),
    "hid_ready": (2, 0, 0, 0, 8),
    "dve_step": (0, 16, 72, 0, 0),
    "act_step": (0, 0, 11, 0, 0),
    "out_ready": (0, 0, 0, 0, 0),
    "stored": (0, 0, 0, 0, 0),
}


class Count:

    def __init__(self, sems):
        self.sems, self.mine, self.last = sems, {}, None
        self.section, self.base = None, None

    def enter(self, section, *regs):
        self.section, self.regs, self.mine, self.bases = section, regs, {}, {}

    def value(self, name, k):
        start, *per = RAISED[name]
        if self.section is None:
            return k
        if self.section == "end":
            return start + DEPTH * sum(n * TIMES[s] for s, n in zip(SECTIONS, per)) + k
        whole = sum(n * TIMES[s] for s, n in zip(SECTIONS, per))
        at = SECTIONS.index(self.section)
        fixed = start + sum(n * TIMES[s] for s, n in zip(SECTIONS[:at], per[:at])) + k
        v = self.regs[0] * whole + fixed if whole else fixed
        if len(self.regs) > 1 and per[at]:
            v = self.regs[1] * per[at] + v
        return v

    def at(self, name, k):
        return self.sems[name], self.value(name, k)

    def up(self, name, n=1):
        self.mine[name] = self.mine.get(name, 0) + n
        self.last = (name, self.mine[name])
        return self.sems[name], n

    def own(self):
        return self.at(*self.last)

    def leave(self):
        at = 1 + SECTIONS.index(self.section)
        for name, n in self.mine.items():
            assert RAISED[name][at] == n, f"{name} is raised {n} times in {self.section}"


def schedule():
    steps = [("norm",), ("gates", 0), ("gv",), ("gu", 0), ("gu", 1)]
    steps += [("mx", t) for t in range(MT)]
    steps += [("z", t) for t in range(MT)]
    steps += [("rg", t) for t in range(MT)]
    steps += [("gate_math",), ("rqk", 0), ("gate_tok",), ("g_norm",), ("rqk", 1), ("rot", 0), ("g_mix",),
              ("mq", 0), ("rqk", 2), ("rot", 1), ("ms", 0), ("rqk", 3), ("rot", 2), ("mn", 0), ("rqk", 4), ("rot", 3),
              ("mt", 0), ("mq", 1), ("rqk", 5), ("rot", 4), ("ms", 1), ("rv", 0), ("rot", 5), ("rv", 1), ("mn", 1),
              ("rv", 2), ("rv", 3), ("mt", 1), ("mq", 2),
              ("rs", 0), ("ms", 2), ("rn", 0), ("mn", 2), ("rs", 1), ("rt", 0), ("mt", 2), ("mq", 3), ("rn", 1),
              ("ms", 3), ("rs", 2), ("rt", 1), ("mn", 3), ("rn", 2), ("mt", 3), ("rs", 3), ("rt", 2), ("rn", 3), ("rt", 3)]
    steps += [("out", m) for m in range(KT)]
    return steps


def units_of(step):
    kind, *a = step
    if kind == "gates":
        return [U_GATE]
    if kind == "gv":
        return [U_GV, U_GV + 1]
    if kind == "rqk":
        return [U_RQ + a[0]]
    if kind == "rv":
        return [U_RV, U_RV + 1, U_RV + 2] if a[0] == 0 else []
    first = {"gu": U_GU, "mx": U_MX, "z": U_Z, "rg": U_RG, "out": U_OUT}
    return [first[kind] + a[0]] if kind in first else []


def groups_of(step):
    return {"norm": (1, 0), "gv": (NC, 0), "gate_math": (0, 0), "g_norm": (0, 0), "gate_tok": (0, 1), "rot": (0, 1),
            "g_mix": (0, GT), "mq": (3, 1), "ms": (0, 2), "mn": (0, 3), "mt": (0, 1), "rt": (0, 1), "rs": (0, 3),
            "rn": (0, 2), "out": (0, 1)}.get(step[0], (1, 0))


def places(steps):
    at, out = [0, 0], {}
    for s in steps:
        out[s] = tuple(at)
        at = [x + y for x, y in zip(at, groups_of(s))]
    return out


PA_PADS, PV_PADS = 1, 3
AHEAD = 2


def splits_before(steps):
    order = [(i, u) for i, s in enumerate(steps) for u in units_of(s)]
    out = [[] for _ in steps]
    for n, (i, u) in enumerate(order):
        at = order[max(n - AHEAD, 0)][0] if n >= AHEAD else 0
        out[at].append(u)
    return out


def trunk(nc, x_t, wmix, wff, small_d, const_d, rope_d, out):
    ctx = ExitStack()
    with ctx:
        base = nc.sbuf_base
        ctx.enter_context(nc.sbuf_tensor("arena", [P, (nc.sbuf_bytes_remaining - 512) // 4], F32))
        origin = [base + (-base) % 32]

        def place(name, shape, dt=F32, at=None):
            size = 4
            for n in shape[1:]:
                size *= n
            size += (-size) % 32
            off = origin[0] if at is None else at
            if at is None:
                origin[0] += size
            return nc.alloc_sbuf_tensor_at(name, shape, dt, offset=off), off

        xT, _ = place("xT", [P, KT, S])
        hh, hh_at = place("hh", [P, KT, S], F32R)
        hl, hl_at = place("hl", [P, KT, S], F32R)
        raw, _ = place("raw", [P, RAW, KT * P])
        wh, _ = place("wh", [P, RING, KT, P], F32R)
        wl, _ = place("wl", [P, RING, KT, P], F32R)
        small, _ = place("small", [P, N_SMALL])
        const, _ = place("const", [P, N_CONST])
        bdq, _ = place("bdq", [P, len(PIECES), MD])
        bdk, _ = place("bdk", [P, len(PIECES), MD])
        bdv, _ = place("bdv", [P, MT, P])
        cst, _ = place("cst", [MD, MH, MD + 1])
        rst, _ = place("rst", [P, MT, P])
        hist, _ = place("hist", [P, MT, 3])
        mrow, _ = place("mrow", [MH, T])
        tok, _ = place("tok", [P, 80])
        mp, _ = place("mp", [MH, NC + 1])
        sold, _ = place("sold", [MH, NC])
        soldd, _ = place("soldd", [MH, MH, NC])
        dn, _ = place("dn", [P, 8])
        ms_, _ = place("msum", [P, 8])
        mrs, _ = place("mrs", [P, 8])
        rss_, _ = place("rsum", [P, 8])
        rrs, _ = place("rrs", [P, 8])
        pool_at = origin[0]
        gu, g_at = place("gu", [P, GT, T])
        gv, _ = place("gv", [P, NC, GW])
        rv, _ = place("rv", [P, NC, RW], at=g_at)
        xc, _ = place("xc", [P, MT, T])
        zt, _ = place("zt", [P, MT, T])
        rg, _ = place("rg", [P, MT, T])
        mxp, _ = place("mxp", [P, MT, T + 3])
        rqk, rqk_at = place("rqk", [P, 2 * MT, T])
        hidh, _ = place("hidh", [P, FG, S], F32R, at=pool_at)
        hidl, _ = place("hidl", [P, FG, S], F32R, at=pool_at + 4 * FG * S)
        assert pool_at + 8 * FG * S <= rqk_at
        sq, _ = place("sq", [P, 2, T], at=rqk_at)
        hf, _ = place("hf", [P, 2, T], at=rqk_at + 8 * T)
        rstd, _ = place("rstd", [P, T], at=rqk_at + 16 * T)
        chunk_at = origin[0]
        qT, q_at = place("qT", [MD, MH, L])
        kT, k_at = place("kT", [MD, MH, L])
        et, _ = place("et", [P, MH, L])
        ktok, _ = place("ktok", [P, MW])
        vx, _ = place("vx", [P, MH, MD + 1])
        num, _ = place("num", [P, MH, MD + 1])
        mn, _ = place("mn", [P, MW])
        my, _ = place("my", [P, MT, L])
        relu, _ = place("relu", [P, 2, T], at=chunk_at)
        sqh, _ = place("sqh", [P, 2, T], at=chunk_at + 8 * T)
        gy, _ = place("gy", [P, 2, T], at=q_at)
        assert chunk_at + 16 * T <= origin[0]
        assert origin[0] <= nc.sbuf_usable_end, (origin[0], nc.sbuf_usable_end)
        oh, ol = hh[:, :, T:S], hl[:, :, T:S]

        def slot(name, shape, at, k, half):
            return place(name, shape, at=at + 4 * (k * S + half * T))[0]

        ra = slot("ra", [MH, T], hh_at, 0, 1)
        rsint = slot("rsint", [MH, T], hh_at, 1, 1)
        reend = slot("reend", [MH, T], hh_at, 2, 1)
        rem = slot("rem", [MH, T], hl_at, 0, 1)
        rbc = slot("rbc", [MH, T], hl_at, 1, 1)
        rtmp = slot("rtmp", [MH, T], hl_at, 2, 1)
        cos = slot("cos", [P, T], hh_at, 3, 1)
        sin = slot("sin", [P, T], hh_at, 4, 1)
        rot = slot("rot", [P, T], hh_at, 5, 1)
        rig = slot("rig", [MH, T], hl_at, 3, 1)
        rxf = slot("rxf", [MH, T], hl_at, 4, 1)
        rsc = [slot(f"rsc{p}", [P, MT, L], hh_at, p, 0) for p in range(2)]
        rqx = slot("rqx", [P, MT, L], hh_at, 2, 0)
        rkt = slot("rkt", [P, RW], hh_at, 3, 0)
        ro = slot("ro", [P, RW], hh_at, 4, 0)
        rn = slot("rn", [P, RW], hh_at, 5, 0)
        ry = slot("ry", [P, MT, L], hh_at, 6, 0)

        pa = [ctx.enter_context(nc.psum_tensor(f"pa{i}", [P, 512], F32)) for i in range(4)]
        pv = [ctx.enter_context(nc.psum_tensor(f"pv{i}", [P, 512], F32)) for i in range(4)]

        sems = {n: ctx.enter_context(nc.semaphore(n)) for n in RAISED}

        def sm(name, k=None):
            a, b = SMALL[name]
            return small[:, a:b] if k is None else small[:, a + k:a + k + 1]

        def cn(name):
            a, b = CONST[name]
            return const[:, a:b]

        eye, ones = cn("eye"), cn("ones")
        decay = cn("decay").rearrange("p (e t l) -> p e t l", e=2, t=MT)
        xi = cn("xi").rearrange("p (t l) -> p t l", t=MT)
        sel = cn("sel").rearrange("p (h l) -> p h l", h=MH)
        ws = sm("ws").rearrange("p (g t) -> p g t", g=GG)
        atok = tok[:, 0:64].rearrange("p (c q h) -> p c q h", c=NC, q=4)
        soldb = tok[:, 64:80].rearrange("p (h c) -> p h c", h=MH)
        steps = schedule()
        ahead = splits_before(steps)
        before = places(steps)

        def nth(ring, step, j=1):
            return before[step]["pa pv".split().index(ring)] + j

        numbered = {}
        for names, kinds in (("ss", ("g_norm", "mn", "rn")), ("o", ("g_mix", "mt", "rt")), ("y", ("g_mix", "mt"))):
            k = 0
            for st in steps:
                if st[0] in kinds:
                    numbered[names, st] = k
                    k += GT if st[0] == "g_mix" else 1
        ends = {}
        for st in steps:
            for u in units_of(st):
                if st[0] == "rv":
                    ends[u] = ("pa_full", nth("pa", ("rv", NC - 1)))
                elif st[0] == "out":
                    ends[u] = ("pv_full", nth("pv", st))
                else:
                    ends[u] = ("pa_full", nth("pa", st, groups_of(st)[0]))
        group_ends = {u: ("pa_full", 2 * (u + 1)) if u < FG else ("pv_full", 4 * (u - FG + 1)) for u in GROUP_UNITS}
        block = ctx.enter_context(nc.Block())

        def raw_wait(sp, n, order, i):
            sp.wait_ge(*n.at("w_ready", 0 if i < RAW else order[i - RAW] + 1))

        @block.sync
        def _(sp):
            n = Count(sems)
            sp.dma_start(const[:, :], const_d).then_inc(*n.up("const_loaded", 16))
            for h in range(HALVES):
                sp.dma_start(xT[:, :, T * h:T * h + T], x_t[:, :, T * h:T * h + T]).then_inc(*n.up("x_loaded", 16))
            with sp.Fori(0, DEPTH) as layer:
                n.enter("pre", layer)
                sp.wait_ge(*n.at("hl_ready", 0))
                sp.dma_start(small[:, :], small_d[bass.ds(layer, 1), :, :].rearrange("a p n -> (a p) n")
                             ).then_inc(*n.up("small_loaded", 16))
                n.leave()
                with sp.Fori(0, HALVES) as half:
                    n.enter("half", layer, half)
                    for i, u in enumerate(HALF_UNITS):
                        raw_wait(sp, n, HALF_UNITS, i)
                        sp.dma_start(raw[:, i % RAW, :],
                                     wmix[bass.ds(layer, 1), i, :, :].rearrange("a p n -> (a p) n")
                                     ).then_inc(*n.up(f"raw{i % RAW}_full", 16))
                        if u == U_MX:
                            sp.wait_ge(*n.at("hl_ready", KT))
                            for j, dst in enumerate((cos, sin)):
                                sp.dma_start(dst[:, :], rope_d[bass.ds(half, 1), j, :, :].rearrange(
                                    "a p n -> (a p) n")).then_inc(*n.up("rope_loaded", 16))
                    n.leave()
                with sp.Fori(0, GROUPS) as group:
                    n.enter("group", layer, group)
                    for i in GROUP_UNITS:
                        raw_wait(sp, n, GROUP_UNITS, i)
                        sp.dma_start(raw[:, i % RAW, :],
                                     wff[bass.ds(layer * GROUPS + group, 1), i, :, :].rearrange(
                                         "a p n -> (a p) n")).then_inc(*n.up(f"raw{i % RAW}_full", 16))
                    n.leave()
            n.enter("end")
            for h in range(HALVES):
                for j in range(0, KT, 4):
                    sp.wait_ge(*n.at("out_ready", KT * h + j + 4))
                    sp.dma_start(out[:, j:j + 4, T * h:T * h + T], xT[:, j:j + 4, T * h:T * h + T]
                                 ).then_inc(*n.up("stored", 16))
            sp.wait_ge(*n.at("stored", 16 * 4))

        @block.tensor
        def _(pe):
            n = Count(sems)
            rings = {}

            def bank(ring, taken=-4):
                k = rings[ring] = rings.get(ring, 0) + 1
                pe.wait_ge(*n.at(f"{ring}_taken", max(k - 4, taken)))
                return (pa if ring == "pa" else pv)[(k - 1) % 4]

            def norm_sums(first, pads=0):
                ps = bank("pa")
                for k in range(KT):
                    pe.wait_ge(*n.at("sq_ready", first + k + 1))
                    ins = pe.matmul(ps[:, :], ones, sq[:, k % 2, :], start=(k == 0), stop=(k == KT - 1))
                    if k < KT - 1:
                        ins.then_inc(*n.up("sq_free"))
                ins.then_inc(*n.up("pa_full", 1 + pads))

            def feature_tile(u, ring, hready=False):
                ps = bank(ring)
                pe.wait_ge(*n.at("w_ready", u + 1))
                for k in range(KT):
                    if hready:
                        pe.wait_ge(*n.at("hl_ready", k + 1))
                    pe.matmul(ps[:, :], wh[:, u % RING, k, :], hh[:, k, 0:T], start=(k == 0), stop=False)
                    pe.matmul(ps[:, :], wh[:, u % RING, k, :], hl[:, k, 0:T], start=False, stop=False)
                    ins = pe.matmul(ps[:, :], wl[:, u % RING, k, :], hh[:, k, 0:T], start=False, stop=(k == KT - 1))
                ins.then_inc(*n.up(f"{ring}_full"))
                return ins

            pe.sem_inc(sems["pv_full"], RAISED["pv_full"][0])
            pe.wait_ge(sems["const_loaded"], 16)
            with pe.Fori(0, DEPTH) as layer:
                with pe.Fori(0, HALVES) as half:
                    n.enter("half", layer, half)
                    rings.clear()
                    for step in steps:
                        kind, *a = step
                        c = a[0] if a else 0
                        tk = slice(L * c, L * c + L)
                        if kind == "norm":
                            norm_sums(0)
                        elif kind in ("gates", "gu", "mx", "z", "rg", "rqk"):
                            feature_tile(units_of(step)[0], "pa", kind == "gates")
                        elif kind in ("gv", "rv"):
                            u, cols = (U_GV, GT) if kind == "gv" else (U_RV, MT)
                            for cc in (range(NC) if kind == "gv" else [c]):
                                tt = slice(L * cc, L * cc + L)
                                ps = bank("pa")
                                pe.wait_ge(*n.at("w_ready", u + cols))
                                s0 = u % RING
                                o = ps[:, 0:cols * P].rearrange("p (u n) -> p u n", u=cols)
                                for k in range(KT):
                                    pe.matmul(o, hh[:, k, tt], wh[:, s0:s0 + cols, k, :], start=(k == 0), stop=False)
                                    pe.matmul(o, hh[:, k, tt], wl[:, s0:s0 + cols, k, :], start=False, stop=False)
                                    ins = pe.matmul(o, hl[:, k, tt], wh[:, s0:s0 + cols, k, :], start=False,
                                                    stop=(k == KT - 1))
                                ins.then_inc(*n.up("pa_full"))
                        elif kind == "gate_tok":
                            ps = bank("pv")
                            pe.wait_ge(*n.at("sold_ready", 1))
                            pe.matmul(ps[:, 64:80], ones[0:MH, :], soldd[:, :, :], start=True, stop=True)
                            for cc in range(NC):
                                for q, row in enumerate((ra, rsint, reend, rem)):
                                    at = 4 * (4 * cc + q)
                                    ins = pe.transpose(ps[:, at:at + 4], row[:, L * cc:L * cc + L], eye[0:MH, 0:MH])
                            ins.then_inc(*n.up("pv_full"))
                        elif kind == "rot":
                            ps = bank("pv")
                            pe.wait_ge(*n.at("pa_taken", nth("pa", ("rqk", c))))
                            pe.matmul(ps[:, :], cn("swap"), rqk[:, c, :], start=True, stop=True
                                      ).then_inc(*n.up("pv_full"))
                        elif kind == "g_mix":
                            for t in range(GT):
                                ps = bank("pv")
                                pe.wait_ge(*n.at("gvn_ready", 1))
                                for cc in range(NC):
                                    for g in (2 * t, 2 * t + 1):
                                        q = GD * (g % 2)
                                        ins = pe.matmul(ps[q:q + GD, L * cc:L * cc + L],
                                                        gv[:, cc, GD * g:GD * g + GD], ws[:, g, :],
                                                        start=True, stop=True)
                                ins.then_inc(*n.up("pv_full"))
                        elif kind == "mq":
                            if c == 0:
                                pe.wait_ge(*n.at("xc_ready", MT))
                                pe.wait_ge(*n.at("layer_ready", 0))
                            for bd in (bdq, bdk):
                                ps = bank("pa")
                                for h in range(MH):
                                    ts = [i for i, (hd, _) in enumerate(PIECES) if hd == h]
                                    for i in ts:
                                        ins = pe.matmul(ps[0:MD, L * h:L * h + L], bd[:, i, :],
                                                        xc[:, PIECES[i][1], tk],
                                                        start=(i == ts[0]), stop=(i == ts[-1]))
                                ins.then_inc(*n.up("pa_full"))
                            ps = bank("pa")
                            for t in range(MT):
                                ins = pe.matmul(ps[:, P * t:P * t + P], mxp[:, t, 3 + L * c:3 + L * c + L],
                                                bdv[:, t, :], start=True, stop=True)
                            ins.then_inc(*n.up("pa_full", 1 + PA_PADS * (c == NC - 1)))
                            ps = bank("pv")
                            for h in range(MH):
                                ts = [i for i, (hd, _) in enumerate(PIECES) if hd == h]
                                for i in ts:
                                    ins = pe.matmul(ps[:, MD * h:MD * h + MD], xc[:, PIECES[i][1], tk],
                                                    bdk[:, i, :], start=(i == ts[0]), stop=(i == ts[-1]))
                            ins.then_inc(*n.up("pv_full"))
                        elif kind == "ms":
                            ps = bank("pv")
                            for h in range(MH):
                                ins = pe.matmul(ps[:, L * h:L * h + L], sel[0:MH, h, :], mrow[:, tk],
                                                start=True, stop=True)
                            ins.then_inc(*n.up("pv_full"))
                            ps = bank("pv")
                            pe.wait_ge(*n.at("pa_taken", nth("pa", ("mq", c), 3)))
                            for h in range(MH):
                                ins = pe.matmul(ps[:, L * h:L * h + L], kT[:, h, :], qT[:, h, :],
                                                start=True, stop=True)
                            ins.then_inc(*n.up("pv_full"))
                        elif kind == "mn":
                            w = MD + 1
                            ps = bank("pv", nth("pv", ("mn", c - 1), 3) if c else -4)
                            for h in range(MH):
                                ins = pe.matmul(ps[:, w * h:w * h + w], qT[:, h, :], cst[:, h, :],
                                                start=True, stop=True)
                            ins.then_inc(*n.up("pv_full"))
                            ps = bank("pv", nth("pv", ("ms", c), 2))
                            for h in range(MH):
                                ins = pe.matmul(ps[:, w * h:w * h + w], et[:, h, :], vx[:, h, :],
                                                start=True, stop=True)
                            ins.then_inc(*n.up("pv_full"))
                            ps = bank("pv", nth("pv", ("mq", c)))
                            for h in range(MH):
                                ins = pe.matmul(ps[0:MD, w * h:w * h + w], ktok[:, MD * h:MD * h + MD], vx[:, h, :],
                                                start=True, stop=True)
                            ins.then_inc(*n.up("pv_full"))
                        elif kind in ("mt", "rt"):
                            ps = bank("pv")
                            src, name = (mn, "mn_ready") if kind == "mt" else (rn, "rn_ready")
                            pe.wait_ge(*n.at(name, c + 1))
                            for t in range(MT):
                                ins = pe.transpose(ps[:, P * t:P * t + P], src[:, P * t:P * t + P], eye)
                            ins.then_inc(*n.up("pv_full"))
                        elif kind == "rs":
                            if c == 0:
                                pe.wait_ge(*n.at("rqk_ready", 2 * MT))
                            for p in range(2):
                                ps = bank("pv")
                                for t in range(MT):
                                    ins = pe.matmul(ps[:, L * t:L * t + L], rqk[RD * p:RD * p + RD, MT + t, tk],
                                                    rqk[RD * p:RD * p + RD, t, tk], start=True, stop=True)
                                ins.then_inc(*n.up("pv_full"))
                            ps = bank("pv")
                            for t in range(MT):
                                ins = pe.transpose(ps[:, P * t:P * t + P], rqk[:, MT + t, tk], eye)
                            ins.then_inc(*n.up("pv_full"))
                        elif kind == "rn":
                            ps = bank("pv", max(nth("pv", ("rs", c), 3), nth("pv", ("rn", c - 1), 2) if c else 0))
                            pe.wait_ge(*n.at("pa_taken", nth("pa", ("rv", c))))
                            for t in range(MT):
                                pe.matmul(ps[:, P * t:P * t + P], rqx[:, t, :], rst[:, t, :], start=True, stop=False)
                                for p in range(2):
                                    q = P * t + RD * p
                                    ins = pe.matmul(ps[:, q:q + RD], rsc[p][:, t, :], rv[:, c, q:q + RD],
                                                    start=False, stop=(p == 1))
                            ins.then_inc(*n.up("pv_full"))
                            ps = bank("pv")
                            for t in range(MT):
                                ins = pe.matmul(ps[:, P * t:P * t + P], rkt[:, P * t:P * t + P],
                                                rv[:, c, P * t:P * t + P], start=True, stop=True)
                            ins.then_inc(*n.up("pv_full"))
                        elif kind == "out":
                            u = units_of(step)[0]
                            ps = bank("pv")
                            pe.wait_ge(*n.at("w_ready", u + 1))
                            if c == 0:
                                pe.wait_ge(*n.at("o_ready", 10))
                            for k in range(KT):
                                pe.matmul(ps[:, :], wh[:, u % RING, k, :], oh[:, k, :], start=(k == 0), stop=False)
                                pe.matmul(ps[:, :], wh[:, u % RING, k, :], ol[:, k, :], start=False, stop=False)
                                ins = pe.matmul(ps[:, :], wl[:, u % RING, k, :], oh[:, k, :], start=False,
                                                stop=(k == KT - 1))
                            ins.then_inc(*n.up("pv_full", 1 + PV_PADS * (c == KT - 1)))
                    n.leave()
                n.enter("norm", layer)
                rings.clear()
                for h in range(HALVES):
                    norm_sums(KT * h, 2 * h)
                n.leave()
                with pe.Fori(0, GROUPS) as group:
                    n.enter("group", layer, group)
                    rings.clear()
                    for u in GROUP_UNITS:
                        pe.wait_ge(*n.at("w_ready", u + 1))
                        s0 = u % RING
                        for m in ([0] if u < FG else range(2)):
                            for h in range(HALVES):
                                th = slice(T * h, T * h + T)
                                if u < FG:
                                    ps = bank("pa")
                                    if u == 0:
                                        pe.wait_ge(*n.at("hl_ready", 0))
                                    for k in range(KT):
                                        a, b = wh[:, s0, k, :], wl[:, s0, k, :]
                                        pe.matmul(ps[:, :], a, hh[:, k, th], start=(k == 0), stop=False)
                                        pe.matmul(ps[:, :], a, hl[:, k, th], start=False, stop=False)
                                        ins = pe.matmul(ps[:, :], b, hh[:, k, th], start=False, stop=(k == KT - 1))
                                    ins.then_inc(*n.up("pa_full"))
                                else:
                                    ps = bank("pv")
                                    for k in range(FG):
                                        if u == FG and m == 0:
                                            pe.wait_ge(*n.at("hid_ready", 2 * k + h + 1))
                                        a, b = (w[:, s0, 2 * k + m, :] for w in (wh, wl))
                                        pe.matmul(ps[:, :], a, hidh[:, k, th], start=(k == 0), stop=False)
                                        pe.matmul(ps[:, :], a, hidl[:, k, th], start=False, stop=False)
                                        ins = pe.matmul(ps[:, :], b, hidh[:, k, th], start=False, stop=(k == FG - 1))
                                    ins.then_inc(*n.up("pv_full"))
                    n.leave()
            n.enter("end")
            rings.clear()
            for h in range(HALVES):
                norm_sums(KT * h)

        @block.scalar
        def _(act):
            n = Count(sems)
            eps, one = cn("eps"), cn("one")

            def round_unit(order, slot_ends, u):
                i = order.index(u)
                last = i == len(order) - 1
                act.wait_ge(*n.at(f"raw{i % RAW}_full", 16 * (i // RAW + 1)))
                if u >= RING:
                    act.wait_ge(*n.at(*slot_ends[u - RING if u - RING in order else u - 2 * RING]))
                else:
                    act.wait_ge(*n.at("pv_full", (-4, 0, -5)[u]))
                act.activation(wh[:, u % RING, :, :].rearrange("p k n -> p (k n)"), raw[:, i % RAW, :], ACT.Copy
                               ).then_inc(*n.up("hi_done", 1 if last is False and u + 1 in order else 2))

            def inv_rms(dst, src, width, name, wait_own=True):
                act.activation(dst, src, ACT.Ln, bias=eps, scale=1.0 / width).then_inc(*n.up("act_step"))
                act.wait_ge(*n.own())
                act.activation(dst, dst, ACT.Exp, scale=-0.5).then_inc(*n.up(name))

            def norm(first, number, rfirst, pads=0):
                th = slice(0, T) if n.section == "half" else slice(rfirst * T, rfirst * T + T)
                act.wait_ge(*n.at("pa_full", number))
                act.activation(rstd[:, :], pa[(number - 1) % 4][:, :], ACT.Ln, bias=eps, scale=1.0 / D
                               ).then_inc(*n.up("pa_taken", 1 + pads))
                act.wait_ge(*n.own())
                act.activation(rstd[:, :], rstd[:, :], ACT.Exp, scale=-0.5).then_inc(*n.up("rstd_ready"))
                if n.section != "end":
                    for k in range(KT):
                        act.wait_ge(*n.at("h_ready", first + k + 1))
                        act.activation(hh[:, k, th], hf[:, k % 2, :], ACT.Copy).then_inc(*n.up("hh_done"))

            def take(step, dst, func, j=1, rows=slice(0, P), cols=slice(0, 512), shape=None, pads=0, **kw):
                k = nth("pa", step, j)
                act.wait_ge(*n.at("pa_full", k))
                src = pa[(k - 1) % 4][rows, cols]
                if shape:
                    src = src.rearrange(shape[0], **shape[1])
                act.activation(dst, src, func, **kw).then_inc(*n.up("pa_taken", 1 + pads))

            for name in ("pa_taken",):
                act.sem_inc(sems[name], RAISED[name][0])
            act.wait_ge(sems["const_loaded"], 16)
            with act.Fori(0, DEPTH) as layer:
                with act.Fori(0, HALVES) as half:
                    n.enter("half", layer, half)
                    for i, step in enumerate(steps):
                        for u in ahead[i]:
                            round_unit(HALF_UNITS, ends, u)
                        kind, *a = step
                        c = a[0] if a else 0
                        tk = slice(L * c, L * c + L)
                        if kind == "norm":
                            norm(0, 1, 0)
                        elif kind == "gates":
                            k = nth("pa", step)
                            act.wait_ge(*n.at("small_loaded", 0))
                            act.wait_ge(*n.at("pa_full", k))
                            ps = pa[(k - 1) % 4]
                            act.activation(rig[:, :], ps[0:MH, :], ACT.Identity, bias=sm("i_bias")[0:MH, :])
                            act.activation(rxf[:, :], ps[32:32 + MH, :], ACT.Identity, bias=sm("f_bias")[32:32 + MH, :]
                                           ).then_inc(*n.up("pa_taken"))
                        elif kind == "gv":
                            for cc in range(NC):
                                take(step, gv[:, cc, :], ACT.Gelu_apprx_tanh, j=cc + 1, cols=slice(0, GW))
                        elif kind == "gu":
                            take(step, gu[:, c, :], ACT.Gelu_apprx_tanh)
                        elif kind == "mx":
                            take(step, mxp[:, c, 3:3 + T], ACT.Copy)
                        elif kind == "z":
                            take(step, zt[:, c, :], ACT.Silu)
                            act.wait_ge(*n.at("conv_done", c + 1))
                            act.activation(xc[:, c, :], xc[:, c, :], ACT.Silu).then_inc(*n.up("xc_ready"))
                        elif kind == "rg":
                            take(step, rg[:, c, :], ACT.Silu)
                        elif kind == "gate_math":
                            act.wait_ge(*n.at("pa_taken", nth("pa", ("gates", 0))))
                            act.activation(rtmp[:, :], rxf[:, :], ACT.Abs).then_inc(*n.up("act_step"))
                            act.wait_ge(*n.own())
                            act.activation(rtmp[:, :], rtmp[:, :], ACT.Exp, scale=-1.0).then_inc(*n.up("act_step"))
                            act.wait_ge(*n.own())
                            act.activation(rtmp[:, :], rtmp[:, :], ACT.Ln, bias=one[0:MH, :]
                                           ).then_inc(*n.up("softplus_ready"))
                        elif kind == "gate_tok":
                            act.wait_ge(*n.at("rows_ready", 1))
                            for row in (rsint, reend, rem):
                                act.activation(row[:, :], row[:, :], ACT.Exp)
                            act.activation(sold[:, :], sold[:, :], ACT.Exp).then_inc(*n.up("rows_exp"))
                        elif kind in ("g_norm", "mn", "rn"):
                            k, w, src, dst = {"g_norm": (NC, GW, ms_, mrs), "mn": (MH, MD, ms_, mrs),
                                              "rn": (RH, RD, rss_, rrs)}[kind]
                            act.wait_ge(*n.at("ss_ready", numbered["ss", step] + 1))
                            inv_rms(dst[:, 0:k], src[:, 0:k], w, "rs_ready")
                        elif kind == "rqk":
                            take(step, rqk[:, c, :], ACT.Copy)
                        elif kind == "rv":
                            take(step, rv[:, c, :], ACT.Copy, cols=slice(0, RW))
                        elif kind == "mq":
                            if c == 0:
                                act.wait_ge(*n.at("o_ready", GT))
                            for j, (dst, scale) in enumerate(((qT, 1.0), (kT, MD ** -0.5))):
                                take(step, dst[:, :, :], ACT.Copy, j=j + 1, rows=slice(0, MD),
                                     shape=("p (h l) -> p h l", {"h": MH}), scale=scale)
                            take(step, vx[:, :, 0:MD], ACT.Copy, j=3, cols=slice(0, MW),
                                 shape=("p (h d) -> p h d", {"h": MH}), pads=PA_PADS * (c == NC - 1))
                        elif kind == "ms":
                            act.wait_ge(*n.at("pv_taken", nth("pv", step)))
                            act.activation(et[:, :, :], et[:, :, :], ACT.Exp).then_inc(*n.up("e_ready"))
                        if kind == "g_mix":
                            for t in range(GT):
                                act.wait_ge(*n.at("y_ready", numbered["y", step] + t + 1))
                                act.activation(oh[:, 2 * MT + t, :], gy[:, t, :], ACT.Copy).then_inc(*n.up("oh_done"))
                        elif kind == "mt":
                            act.wait_ge(*n.at("y_ready", numbered["y", step] + 1))
                            act.activation(oh[:, 0:MT, tk], my[:, :, :], ACT.Copy).then_inc(*n.up("oh_done"))
                        elif kind == "rt":
                            act.wait_ge(*n.at("pv_taken", nth("pv", step)))
                            act.activation(oh[:, MT:2 * MT, tk], ry[:, :, :], ACT.Copy).then_inc(*n.up("oh_done"))
                    n.leave()
                n.enter("norm", layer)
                for h in range(HALVES):
                    norm(KT * h, h + 1, h, 2 * h)
                n.leave()
                with act.Fori(0, GROUPS) as group:
                    n.enter("group", layer, group)
                    for u in (0, 1):
                        round_unit(GROUP_UNITS, group_ends, u)

                    def round_square(e):
                        act.wait_ge(*n.at("sq_done", e + 1))
                        h = e % HALVES
                        act.activation(hidh[:, e // HALVES, T * h:T * h + T], sqh[:, e % 2, :], ACT.Copy
                                       ).then_inc(*n.up("dh_done"))

                    for u in range(FG):
                        round_unit(GROUP_UNITS, group_ends, u + 2)
                        for e in (2 * u, 2 * u + 1):
                            act.wait_ge(*n.at("pa_full", e + 1))
                            act.activation(relu[:, e % 2, :], pa[e % 4][:, :], ACT.Relu).then_inc(*n.up("pa_taken"))
                            if e:
                                round_square(e - 1)
                    round_square(2 * FG - 1)
                    for u in (FG + 2, FG + 3):
                        round_unit(GROUP_UNITS, group_ends, u)
                    n.leave()
            n.enter("end")
            for h in range(HALVES):
                norm(KT * h, h + 1, h)

        @block.vector
        def _(dve):
            n = Count(sems)

            def rest_unit(order, u):
                i = order.index(u)
                dve.wait_ge(*n.at("hi_done", u + 1))
                dve.tensor_tensor(wl[:, u % RING, :, :].rearrange("p k n -> p (k n)"), raw[:, i % RAW, :],
                                  wh[:, u % RING, :, :].bitcast(F32).rearrange("p k n -> p (k n)"), ALU.subtract
                                  ).then_inc(*n.up("w_ready", 1 if u + 1 in order else 2))

            def norm(cols, th, g, first, number):
                for k in range(KT):
                    if k >= 2:
                        dve.wait_ge(*n.at("sq_free", first // KT * (KT - 1) + k - 1))
                    dve.tensor_tensor(sq[:, k % 2, :], xT[:, k, cols], xT[:, k, cols], ALU.mult
                                      ).then_inc(*n.up("sq_ready"))
                dve.wait_ge(*n.at("rstd_ready", number))
                for k in range(KT + 1):
                    if k < KT:
                        if n.section == "end":
                            dve.scalar_tensor_tensor(xT[:, k, cols], xT[:, k, cols], g[:, k:k + 1], rstd[:, :],
                                                     ALU.mult, ALU.mult).then_inc(*n.up("out_ready"))
                            continue
                        go()
                        dve.scalar_tensor_tensor(hf[:, k % 2, :], xT[:, k, cols], g[:, k:k + 1], rstd[:, :],
                                                 ALU.mult, ALU.mult).then_inc(*n.up("h_ready"))
                    if k >= 1 and n.section != "end":
                        dve.wait_ge(*n.at("hh_done", first + k))
                        dve.tensor_tensor(hl[:, k - 1, th], hf[:, (k - 1) % 2, :], hh[:, k - 1, th].bitcast(F32),
                                          ALU.subtract).then_inc(*n.up("hl_ready"))

            def step_done(ins):
                ins.then_inc(*n.up("dve_step"))
                dve.wait_ge(*n.own())

            def go():
                dve.wait_ge(*n.own())

            def full(step, j=1):
                k = nth("pv", step, j)
                dve.wait_ge(*n.at("pv_full", k))
                return pv[(k - 1) % 4]

            def rest_output(step, dst, src, j=0):
                dve.wait_ge(*n.at("oh_done", numbered["o", step] + j + 1))
                dve.tensor_tensor(ol[:, dst[0], dst[1]], src, oh[:, dst[0], dst[1]].bitcast(F32), ALU.subtract
                                  ).then_inc(*n.up("o_ready"))

            for name in ("w_ready", "pv_taken", "hl_ready", "hid_ready"):
                dve.sem_inc(sems[name], RAISED[name][0])
            dve.wait_ge(sems["const_loaded"], 16)
            dve.wait_ge(sems["x_loaded"], 16 * HALVES)
            with dve.Fori(0, DEPTH) as layer:
                n.enter("pre", layer)
                dve.wait_ge(*n.at("small_loaded", 16))
                for bd in (bdq, bdk):
                    dve.memset(bd[:, :, :], 0.0)
                for buf in (bdv, cst, rst, hist):
                    dve.memset(buf[:, :, :], 0.0)
                dve.memset(mp[:, :], 0.0)
                step_done(dve.memset(vx[:, :, MD:MD + 1], 1.0))
                blocks = cn("blocks")
                for bd, name in ((bdq, "wq"), (bdk, "wk")):
                    w = sm(name).rearrange("p (t j) -> p t j", j=4)
                    for i, (h, t) in enumerate(PIECES):
                        lo, hi = max(MD * h, P * t), min(MD * h + MD, P * t + P)
                        nb = (hi - lo) // 4
                        dve.tensor_tensor(
                            bd[:, i, lo - MD * h:hi - MD * h].rearrange("p (n j) -> p n j", j=4),
                            blocks[:, lo - P * t:hi - P * t].rearrange("p (n j) -> p n j", j=4),
                            w[:, t:t + 1, :].broadcast_to([P, nb, 4]), ALU.mult).then_inc(*n.up("dve_step"))
                w = sm("wv").rearrange("p (t j) -> p t j", j=4)
                for t in range(MT):
                    dve.tensor_tensor(bdv[:, t, :].rearrange("p (n j) -> p n j", j=4),
                                      blocks.rearrange("p (n j) -> p n j", j=4),
                                      w[:, t:t + 1, :].broadcast_to([P, P // 4, 4]), ALU.mult
                                      ).then_inc(*n.up("dve_step"))
                dve.tensor_tensor(ws, ws, cn("causal").rearrange("p (a l) -> p a l", a=1).broadcast_to([P, GG, L]),
                                  ALU.mult).then_inc(*n.up("layer_ready"))
                n.leave()
                with dve.Fori(0, HALVES) as half:
                    n.enter("half", layer, half)
                    dve.wait_ge(*n.at("pv_taken", 0))
                    for i, step in enumerate(steps):
                        for u in ahead[i]:
                            rest_unit(HALF_UNITS, u)
                        kind, *a = step
                        c = a[0] if a else 0
                        tk = slice(L * c, L * c + L)
                        xcols = bass.ds(half * T, T)
                        if kind == "norm":
                            norm(xcols, slice(0, T), sm("g_mix"), 0, 1)
                        elif kind == "mx":
                            dve.wait_ge(*n.at("pa_taken", nth("pa", step)))
                            go()
                            dve.tensor_copy(mxp[:, c, 0:3], hist[:, c, :]).then_inc(*n.up("dve_step"))
                            go()
                            step_done(dve.tensor_copy(hist[:, c, :], mxp[:, c, T:T + 3]))
                            w = sm("conv_w")
                            step_done(dve.tensor_scalar(xc[:, c, :], mxp[:, c, 0:T], w[:, 4 * c:4 * c + 1],
                                                        sm("conv_b", c), ALU.mult, ALU.add))
                            for j in range(1, 4):
                                ins = dve.scalar_tensor_tensor(xc[:, c, :], mxp[:, c, j:j + T],
                                                               w[:, 4 * c + j:4 * c + j + 1], xc[:, c, :],
                                                               ALU.mult, ALU.add)
                                if j < 3:
                                    step_done(ins)
                            ins.then_inc(*n.up("conv_done"))
                        elif kind == "gate_math":
                            go()
                            v3 = lambda r: r[:, :].rearrange("h (c l) -> h c l", c=NC)
                            dve.wait_ge(*n.at("softplus_ready", 1))
                            step_done(dve.scalar_tensor_tensor(rtmp[:, :], rxf[:, :], 0.0, rtmp[:, :],
                                                               ALU.min, ALU.subtract))
                            for cc in range(NC):
                                t = slice(L * cc, L * cc + L)
                                ins = dve.tensor_tensor_scan(rbc[:, t], rtmp[:, t], cn("zero")[0:MH, :], 0.0,
                                                             ALU.add, ALU.add)
                            step_done(ins)
                            dve.tensor_copy(mp[:, 0:1], mp[:, NC:NC + 1]).then_inc(*n.up("dve_step"))
                            step_done(dve.tensor_tensor(ra[:, :], rig[:, :], rbc[:, :], ALU.subtract))
                            for cc in range(NC):
                                t, e = slice(L * cc, L * cc + L), L * cc + L - 1
                                step_done(dve.tensor_tensor_scan(mrow[:, t], ra[:, t], ra[:, t], mp[:, cc:cc + 1],
                                                                 ALU.max, ALU.max))
                                step_done(dve.tensor_tensor(mp[:, cc + 1:cc + 2], mrow[:, e:e + 1], rbc[:, e:e + 1],
                                                            ALU.add))
                            ends_m = v3(mrow)[:, :, L - 1:L]
                            dve.tensor_tensor(v3(rsint), mp[:, 0:NC].rearrange("h (c a) -> h c a", a=1).broadcast_to(
                                [MH, NC, L]), v3(mrow), ALU.subtract)
                            dve.tensor_tensor(v3(reend), v3(ra), ends_m.broadcast_to([MH, NC, L]), ALU.subtract)
                            dve.scalar_tensor_tensor(rem[:, :], rbc[:, :], -1.0, mrow[:, :], ALU.mult, ALU.subtract)
                            dve.tensor_tensor(sold[:, :], mp[:, 0:NC], ends_m.rearrange("h c a -> h (c a)"),
                                              ALU.subtract).then_inc(*n.up("rows_ready"))
                        elif kind == "gate_tok":
                            dve.wait_ge(*n.at("rows_exp", 1))
                            dve.tensor_tensor(
                                soldd[:, :, :], sold[:, :].rearrange("h (a c) -> h a c", a=1).broadcast_to([MH, MH, NC]),
                                cn("eye4")[0:MH, :].rearrange("h (g a) -> h g a", a=1).broadcast_to([MH, MH, NC]),
                                ALU.mult).then_inc(*n.up("sold_ready"))
                            ps = full(step)
                            go()
                            dve.tensor_copy(tok[:, :], ps[:, 0:80]).then_inc(*n.up("pv_taken"))
                        elif kind == "g_norm":
                            dve.wait_ge(*n.at("pa_taken", nth("pa", ("gv",), NC)))
                            for b in range(2):
                                s2 = et[:, :, :].rearrange("p h l -> p (h l)").rearrange("p (c n) -> p c n", c=2)
                                go()
                                step_done(dve.tensor_tensor(s2, gv[:, 2 * b:2 * b + 2, :], gv[:, 2 * b:2 * b + 2, :],
                                                            ALU.mult))
                                dve.tensor_reduce(ms_[:, 2 * b:2 * b + 2], s2, AX_X, ALU.add
                                                  ).then_inc(*n.up("ss_ready" if b else "dve_step"))
                            dve.wait_ge(*n.at("rs_ready", numbered["ss", step] + 1))
                            for cc in range(NC):
                                ins = dve.scalar_tensor_tensor(gv[:, cc, :], gv[:, cc, :], mrs[:, cc:cc + 1],
                                                               sm("g_norm"), ALU.mult, ALU.mult)
                            ins.then_inc(*n.up("gvn_ready"))
                        elif kind == "rot":
                            if c == 0:
                                dve.wait_ge(*n.at("rope_loaded", 32))
                            ps = full(step)
                            go()
                            dve.tensor_tensor(rot[:, :], ps[:, :], sin[:, :], ALU.mult).then_inc(*n.up("pv_taken"))
                            step_done(dve.tensor_tensor(rqk[:, c, :], rqk[:, c, :], cos[:, :], ALU.mult))
                            dve.tensor_tensor(rqk[:, c, :], rqk[:, c, :], rot[:, :], ALU.add
                                              ).then_inc(*n.up("rqk_ready"))
                        elif kind == "g_mix":
                            bs = sm("bs").rearrange("p (t a l) -> p t a l", t=GT, a=1)
                            go()
                            for t in range(GT):
                                ps = full(step, t + 1)
                                y = gy[:, t, :].rearrange("p (c l) -> p c l", c=NC)
                                dve.tensor_tensor(y, ps[:, :].rearrange("p (c l) -> p c l", c=NC),
                                                  bs[:, t, :, :].broadcast_to([P, NC, L]), ALU.add
                                                  ).then_inc(*n.up("pv_taken"))
                                dve.wait_ge(*n.own())
                                dve.tensor_tensor(gy[:, t, :], gy[:, t, :], gu[:, t, :], ALU.mult
                                                  ).then_inc(*n.up("y_ready"))
                            for t in range(GT):
                                rest_output(step, (2 * MT + t, slice(0, T)), gy[:, t, :], t)
                        elif kind == "mq":
                            ps = full(step)
                            heads = lambda ap: ap.rearrange("p (h d) -> p h d", h=MH)
                            go()
                            dve.scalar_tensor_tensor(
                                heads(ktok[:, :]), heads(ps[:, 0:MW]), MD ** -0.5,
                                atok[:, c, 2, :].rearrange("p (h a) -> p h a", a=1).broadcast_to([P, MH, MD]),
                                ALU.mult, ALU.mult).then_inc(*n.up("pv_taken"))
                        elif kind == "ms":
                            ps = full(step)
                            go()
                            for h in range(MH):
                                ins = dve.scalar_tensor_tensor(et[:, h, :], ps[:, L * h:L * h + L],
                                                               atok[:, c, 0, h:h + 1], cn("upper"), ALU.add, ALU.min)
                            ins.then_inc(*n.up("pv_taken"))
                            dve.wait_ge(*n.at("e_ready", c + 1))
                            ps = full(step, 2)
                            dve.tensor_tensor(et[:, :, :], ps[:, :].rearrange("p (h l) -> p h l", h=MH), et[:, :, :],
                                              ALU.mult).then_inc(*n.up("pv_taken"))
                        elif kind == "mn":
                            w = MH * (MD + 1)
                            heads = lambda ap: ap.rearrange("p (h d) -> p h d", h=MH)
                            wide = lambda ap, m=P, d=MD + 1: ap.rearrange("p (h a) -> p h a", a=1).broadcast_to([m, MH, d])
                            ps = full(step)
                            go()
                            dve.tensor_tensor(num[:, :, :], heads(ps[:, 0:w]), wide(atok[:, c, 1, :]), ALU.mult
                                              ).then_inc(*n.up("pv_taken"))
                            ps = full(step, 2)
                            dve.wait_ge(*n.own())
                            dve.tensor_tensor(num[:, :, :], heads(ps[:, 0:w]), num[:, :, :], ALU.add
                                              ).then_inc(*n.up("pv_taken"))
                            step_done(dve.tensor_tensor(cst[:, :, :], cst[:, :, :], soldb[0:MD, :, c:c + 1].broadcast_to(
                                [MD, MH, MD + 1]), ALU.mult))
                            ps = full(step, 3)
                            dve.tensor_tensor(cst[:, :, :], heads(ps[0:MD, 0:w]), cst[:, :, :], ALU.add
                                              ).then_inc(*n.up("pv_taken"))
                            step_done(dve.scalar_tensor_tensor(dn[:, 0:MH], num[:, :, MD], -1.0, num[:, :, MD],
                                                               ALU.mult, ALU.max))
                            step_done(dve.tensor_tensor(dn[:, 0:MH], dn[:, 0:MH], atok[:, c, 3, :], ALU.max))
                            step_done(dve.reciprocal(dn[:, 4:4 + MH], dn[:, 0:MH]))
                            step_done(dve.tensor_tensor(num[:, :, 0:MD], num[:, :, 0:MD], wide(dn[:, 4:4 + MH], d=MD),
                                                        ALU.mult))
                            step_done(dve.tensor_tensor(heads(mn[:, :]), num[:, :, 0:MD], num[:, :, 0:MD], ALU.mult))
                            dve.tensor_reduce(ms_[:, 0:MH], heads(mn[:, :]), AX_X, ALU.add
                                              ).then_inc(*n.up("ss_ready"))
                            dve.wait_ge(*n.at("rs_ready", numbered["ss", step] + 1))
                            dve.tensor_tensor(heads(mn[:, :]), num[:, :, 0:MD], wide(mrs[:, 0:MH], d=MD), ALU.mult
                                              ).then_inc(*n.up("mn_ready"))
                        elif kind == "mt":
                            ps = full(step)
                            go()
                            for t in range(MT):
                                ins = dve.tensor_scalar(my[:, t, :], ps[:, P * t:P * t + P], sm("m_norm", t), None,
                                                        ALU.mult)
                            ins.then_inc(*n.up("pv_taken"))
                            dve.wait_ge(*n.own())
                            for t in range(MT):
                                ins = dve.scalar_tensor_tensor(my[:, t, :], xc[:, t, tk], sm("skip", t), my[:, t, :],
                                                               ALU.mult, ALU.add)
                            step_done(ins)
                            dve.tensor_tensor(my[:, :, :], my[:, :, :], zt[:, :, tk], ALU.mult
                                              ).then_inc(*n.up("y_ready"))
                            rest_output(step, (slice(0, MT), tk), my[:, :, :])
                        elif kind == "rs":
                            for p in range(2):
                                ps = full(step, p + 1)
                                if p == 0:
                                    go()
                                    dve.tensor_tensor(rqx[:, :, :], rqk[:, 0:MT, tk], xi, ALU.mult)
                                dve.tensor_tensor(rsc[p][:, :, :], ps[:, 0:MT * L].rearrange("p (t l) -> p t l", t=MT),
                                                  decay[:, p, :, :], ALU.mult).then_inc(*n.up("pv_taken"))
                            ps = full(step, 3)
                            dve.tensor_tensor(
                                rkt[:, :].rearrange("p (h d) -> p h d", h=RH),
                                ps[:, 0:RW].rearrange("p (h d) -> p h d", h=RH),
                                cn("zeta").rearrange("p (h a) -> p h a", a=1).broadcast_to([P, RH, RD]), ALU.mult
                                ).then_inc(*n.up("pv_taken"))
                        elif kind == "rn":
                            heads = lambda ap: ap.rearrange("p (h d) -> p h d", h=RH)
                            ps = full(step)
                            go()
                            dve.tensor_copy(ro[:, :], ps[:, 0:RW]).then_inc(*n.up("pv_taken"))
                            step_done(dve.tensor_tensor(rst[:, :, :], rst[:, :, :], cn("gl").rearrange(
                                "p (t a) -> p t a", a=1).broadcast_to([P, MT, P]), ALU.mult))
                            ps = full(step, 2)[:, 0:RW].rearrange("p (t n) -> p t n", t=MT)
                            for p in range(2):
                                q = slice(RD * p, RD * p + RD)
                                ins = dve.tensor_tensor(rst[q, :, q], ps[q, :, q], rst[q, :, q], ALU.add)
                            ins.then_inc(*n.up("pv_taken"))
                            step_done(dve.tensor_tensor(rn[:, :], ro[:, :], ro[:, :], ALU.mult))
                            dve.tensor_reduce(rss_[:, 0:RH], heads(rn[:, :]), AX_X, ALU.add).then_inc(*n.up("ss_ready"))
                            dve.wait_ge(*n.at("rs_ready", numbered["ss", step] + 1))
                            dve.tensor_tensor(heads(rn[:, :]), heads(ro[:, :]), rrs[:, 0:RH].rearrange(
                                "p (h a) -> p h a", a=1).broadcast_to([P, RH, RD]), ALU.mult
                                ).then_inc(*n.up("rn_ready"))
                        elif kind == "rt":
                            ps = full(step)
                            go()
                            for t in range(MT):
                                ins = dve.scalar_tensor_tensor(ry[:, t, :], ps[:, P * t:P * t + P], sm("r_norm", t),
                                                               rg[:, t, tk], ALU.mult, ALU.mult)
                            ins.then_inc(*n.up("pv_taken"))
                            rest_output(step, (slice(MT, 2 * MT), tk), ry[:, :, :])
                        elif kind == "out":
                            ps = full(step)
                            go()
                            dve.tensor_tensor(xT[:, c, xcols], ps[:, :], xT[:, c, xcols], ALU.add
                                              ).then_inc(*n.up("pv_taken", 1 + PV_PADS * (c == KT - 1)))
                    n.leave()
                n.enter("norm", layer)
                dve.wait_ge(*n.at("pv_taken", 0))
                for h in range(HALVES):
                    th = slice(T * h, T * h + T)
                    norm(th, th, sm("g_ff"), KT * h, h + 1)
                n.leave()
                with dve.Fori(0, GROUPS) as group:
                    n.enter("group", layer, group)
                    for u in (0, 1):
                        rest_unit(GROUP_UNITS, u)

                    def rest_square(e):
                        dve.wait_ge(*n.at("dh_done", e + 1))
                        th = slice(T * (e % HALVES), T * (e % HALVES) + T)
                        dve.tensor_tensor(hidl[:, e // HALVES, th], sqh[:, e % 2, :],
                                          hidh[:, e // HALVES, th].bitcast(F32), ALU.subtract
                                          ).then_inc(*n.up("hid_ready"))

                    for u in range(FG):
                        rest_unit(GROUP_UNITS, u + 2)
                        for e in (2 * u, 2 * u + 1):
                            dve.wait_ge(*n.at("pa_taken", e + 1))
                            dve.wait_ge(*n.at("hid_ready", e - 1))
                            dve.tensor_tensor(sqh[:, e % 2, :], relu[:, e % 2, :], relu[:, e % 2, :], ALU.mult
                                              ).then_inc(*n.up("sq_done"))
                            if e:
                                rest_square(e - 1)
                    rest_square(2 * FG - 1)
                    for q in range(KT // 2):
                        if q < 2:
                            rest_unit(GROUP_UNITS, FG + 2 + q)
                        for j in range(4):
                            m, th = 2 * q + j // 2, slice(T * (j % 2), T * (j % 2) + T)
                            k = 4 * q + j
                            dve.wait_ge(*n.at("pv_full", k + 1))
                            dve.tensor_tensor(xT[:, m, th], pv[k % 4][:, :], xT[:, m, th], ALU.add
                                              ).then_inc(*n.up("pv_taken"))
                    n.leave()
            n.enter("end")
            dve.wait_ge(*n.at("pv_taken", 0))
            for h in range(HALVES):
                th = slice(T * h, T * h + T)
                norm(th, th, cn("final_g"), KT * h, h + 1)


def _unit(w):
    return w.reshape(KT, P, P).transpose(1, 0, 2).reshape(P, KT * P)


def _constants(np):
    c = np.zeros((P, N_CONST), np.float32)

    def put(name, v):
        a, b = CONST[name]
        v = np.asarray(v, np.float32)
        v = v.reshape(v.shape[0], -1)
        c[:v.shape[0], a:b] = v

    i = np.arange(P)
    put("upper", np.where(i[:, None] <= i[None, :], 0.0, -BIG))
    put("causal", i[:, None] <= i[None, :])
    put("blocks", i[:, None] // 4 == i[None, :] // 4)
    put("eye", np.eye(P))
    put("ones", np.ones((P, P)))
    put("swap", i[:, None] == (i[None, :] ^ 32))
    lg = np.log(1.0 - 2.0 ** (-5.0 - np.arange(RH)))
    heads = np.stack([2 * np.arange(MT) + p for p in range(2)])
    rel = np.maximum(i[None, :] - i[:, None], 0)
    put("decay", np.stack([[np.where(i[:, None] <= i[None, :], np.exp(rel * lg[h]), 0.0) * RD ** -0.5 for h in r]
                           for r in heads]).transpose(2, 0, 1, 3))
    mine = heads[i // RD]
    put("xi", np.exp(lg[mine][:, :, None] * (i + 1.0)))
    put("gl", np.exp(L * lg[mine]))
    put("zeta", np.exp((L - 1.0 - i)[:, None] * lg[None, :]) * RD ** -0.5)
    put("sel", -np.repeat(np.eye(MH)[:, :, None], P, 2))
    put("eye4", np.eye(MH))
    put("eps", np.full((P, 1), EPS))
    put("one", np.ones((P, 1)))
    return c


def _rope(np):
    half = RD // 2
    pos = np.arange(S, dtype=np.float32)
    freq = np.float32(10000.0) ** (-np.arange(half, dtype=np.float32) / np.float32(half))
    ang = (pos[:, None] * freq[None, :].astype(np.float32)).astype(np.float32)
    i = np.arange(P) % RD
    cos, sin = np.cos(ang)[:, i % half].T, np.sin(ang)[:, i % half].T
    sin = np.where(i[:, None] < half, -sin, sin)
    return np.stack([cos, sin]).reshape(2, P, HALVES, T).transpose(2, 0, 1, 3).astype(np.float32)


def kernel(**inputs):
    import numpy as np
    import concourse.bacc as bacc
    from concourse.bass_utils import run_bass_kernel_spmd

    a = {k: np.asarray(v) for k, v in inputs.items()}
    w_in, w_out = a["w_in"], a["w_out"]
    at = np.cumsum([0, MW, MW, MH, MH, RW, RW, RW, RW, GW, GW])
    o_mx, o_z, o_i, o_f, o_rq, o_rk, o_rv, o_rg, o_gu, o_gv = at[:-1]
    wmix = np.zeros((DEPTH, len(HALF_UNITS), P, KT * P), np.float32)
    for l in range(DEPTH):
        gates = np.zeros((D, P), np.float32)
        gates[:, 0:MH] = w_in[l][:, o_i:o_i + MH]
        gates[:, 32:32 + MH] = w_in[l][:, o_f:o_f + MH]
        tiles = [gates]
        for o, nt in ((o_gv, GT), (o_gu, GT), (o_mx, MT), (o_z, MT), (o_rg, MT), (o_rq, MT), (o_rk, MT), (o_rv, MT)):
            tiles += [w_in[l][:, o + P * t:o + P * t + P] for t in range(nt)]
        tiles += [w_out[l][:, P * t:P * t + P] for t in range(KT)]
        for i, w in enumerate(tiles):
            wmix[l, i] = _unit(w)
    wff = np.zeros((DEPTH * GROUPS, 8, P, KT * P), np.float32)
    for l in range(DEPTH):
        for g in range(GROUPS):
            for j in range(FG):
                f = (g * FG + j) * P
                wff[l * GROUPS + g, j] = _unit(a["w_ff1"][l][:, f:f + P])
            rows = a["w_ff2"][l][g * FG * P:(g + 1) * FG * P].reshape(FG, P, 4, 2 * P)
            wff[l * GROUPS + g, FG:] = rows.transpose(2, 1, 0, 3).reshape(4, P, KT * P)
    small = np.zeros((DEPTH, P, N_SMALL), np.float32)

    def put(name, v, r0=0):
        c0, c1 = SMALL[name]
        v = v.reshape(DEPTH, v.shape[1], -1)
        small[:, r0:r0 + v.shape[1], c0:c1] = v

    def tiles_of(v):
        return v.reshape(DEPTH, -1, P).transpose(0, 2, 1)

    put("g_mix", tiles_of(a["norm_mix_g"]))
    put("g_ff", tiles_of(a["norm_ff_g"]))
    put("conv_w", a["m_conv_w"].reshape(DEPTH, 4, MT, P).transpose(0, 3, 2, 1))
    put("conv_b", tiles_of(a["m_conv_b"]))
    put("skip", tiles_of(a["m_skip"]))
    put("m_norm", tiles_of(a["m_norm_g"]))
    put("r_norm", tiles_of(a["r_norm_g"]))
    put("i_bias", a["m_i_bias"][:, :, None])
    put("f_bias", a["m_f_bias"][:, :, None], 32)
    for name, key in (("wq", "m_wq"), ("wk", "m_wk"), ("wv", "m_wv")):
        put(name, a[key].reshape(DEPTH, MT, P, 4).transpose(0, 2, 1, 3))
    bs = a["g_bs"].reshape(DEPTH, GT, 2, 1, L)
    put("bs", np.broadcast_to(bs, (DEPTH, GT, 2, GD, L)).transpose(0, 2, 3, 1, 4).reshape(DEPTH, P, -1))
    put("g_norm", np.broadcast_to(a["g_norm_g"][:, None, :], (DEPTH, P, GW)))
    put("ws", a["g_ws"].transpose(0, 3, 1, 2))
    const = _constants(np)
    const[:, CONST["final_g"][0]:CONST["final_g"][1]] = a["final_norm_g"].reshape(KT, P).T
    x_t = a["x"][0].T.reshape(KT, P, S).transpose(1, 0, 2)

    nc = bacc.Bacc("TRN2", target_bir_lowering=False, num_devices=1,
                   dynamic_dma_scratch_size=1024)
    arrays, args = {}, []
    for name, v in (("x_t", x_t), ("wmix", wmix), ("wff", wff), ("small", small), ("const", const),
                    ("rope", _rope(np))):
        v = np.ascontiguousarray(v)
        arrays[name] = v
        args.append(nc.dram_tensor(name, v.shape, mybir.dt.from_np(v.dtype), kind="ExternalInput").ap())
    args.append(nc.dram_tensor("y_t", (P, KT, S), F32, kind="ExternalOutput").ap())
    trunk(nc, *args)
    r = run_bass_kernel_spmd(nc, [arrays], core_ids=[0])
    y = r.results[0]["y_t"]
    return np.ascontiguousarray(y.transpose(2, 1, 0).reshape(1, S, D))
```

```python
from contextlib import ExitStack

import concourse.bass as bass
from concourse import mybir
from concourse.alu_op_type import AluOpType as ALU

F32 = mybir.dt.float32
F32R = mybir.dt.float32r
ACT = mybir.ActivationFunctionType
AX_X = mybir.AxisListType.X

P = 128
D = 1024
S = 1024
DEPTH = 2
KT = D // P
T = 512
HALVES = S // T
L = 128
NC = T // L
MW = RW = 384
MT = MW // P
MH, MD = 4, 96
RH, RD = 6, 64
GW, GG, GD = 256, 4, 64
GT = GW // P
FF = 4096
FG = 4
GROUPS = FF // P // FG
EPS = 1e-6
BIG = 1.0e30

RING = 3
RAW = 2
U_GATE, U_MX, U_GV, U_GU, U_Z, U_RQ, U_RG, U_RV, U_OUT = 0, 1, 4, 6, 8, 11, 17, 21, 24
PADS = (20, 32)
HALF_UNITS = [u for u in range(33) if u not in PADS]
LAYER_UNITS = len(HALF_UNITS) + 8 * (FF // P // FG)
GROUP_UNITS = list(range(8))

PIECES = [(h, t) for h in range(MH) for t in range(MT) if max(MD * h, P * t) < min(MD * h + MD, P * t + P)]

SMALL = {}
_n = 0
for _name, _w in (("g_mix", KT), ("g_ff", KT), ("conv_w", 4 * MT), ("conv_b", MT), ("skip", MT), ("m_norm", MT),
                  ("r_norm", MT), ("i_bias", 1), ("f_bias", 1), ("wq", 4 * MT), ("wk", 4 * MT), ("wv", 4 * MT),
                  ("bs", GT * L), ("g_norm", GW), ("ws", GG * L)):
    SMALL[_name] = (_n, _n + _w)
    _n += _w
N_SMALL = _n

CONST = {}
_n = 0
for _name, _w in (("upper", L), ("causal", L), ("blocks", L), ("eye", P), ("swap", P), ("ones", P),
                  ("decay", 2 * MT * L), ("xi", MT * L), ("gl", MT), ("zeta", RH), ("sel", MH * P),
                  ("eye4", 4), ("zero", L), ("final_g", KT), ("eps", 1), ("one", 1)):
    CONST[_name] = (_n, _n + _w)
    _n += _w
N_CONST = _n

SECTIONS = ("pre", "half", "norm", "group")
TIMES = {"pre": 1, "half": HALVES, "norm": 1, "group": GROUPS}
RAISED = {
    "x0_loaded": (0, 0, 0, 0, 0),
    "x1_loaded": (0, 0, 0, 0, 0),
    "x2_loaded": (0, 0, 0, 0, 0),
    "const_loaded": (0, 0, 0, 0, 0),
    "small_loaded": (0, 16, 0, 0, 0),
    "rope_loaded": (0, 0, 32, 0, 0),
    "raw0_full": (0, 0, 16 * 16, 0, 16 * 4),
    "raw1_full": (0, 0, 16 * 15, 0, 16 * 4),
    "hi_done": (0, 0, 33, 0, 9),
    "w_ready": (3, 0, 33, 0, 9),
    "pa_full": (0, 4, 40, 4, 8),
    "pa_taken": (4, 4, 40, 4, 8),
    "pv_full": (8, 0, 72, 0, 16),
    "pv_taken": (4, 0, 72, 0, 16),
    "sq_ready": (0, 8, 8, 0, 0),
    "sq_added": (0, 7, 7, 0, 0),
    "sqb_ready": (0, 0, 0, 8, 0),
    "sqb_added": (0, 0, 0, 7, 0),
    "rstd_ready": (0, 1, 1, 1, 0),
    "h_ready": (0, 8, 8, 8, 0),
    "hh_done": (0, 8, 8, 8, 0),
    "hl_ready": (1, 8, 8, 8, 0),
    "layer_ready": (0, 1, 0, 0, 0),
    "conv_done": (0, 0, 3, 0, 0),
    "xc_ready": (0, 0, 3, 0, 0),
    "rg_ready": (0, 0, 1, 0, 0),
    "softplus_ready": (0, 0, 1, 0, 0),
    "rows_ready": (0, 0, 1, 0, 0),
    "rows_exp": (0, 0, 1, 0, 0),
    "sold_ready": (0, 0, 1, 0, 0),
    "gvn_ready": (0, 0, 1, 0, 0),
    "rqk_ready": (0, 0, 6, 0, 0),
    "e_ready": (0, 0, 4, 0, 0),
    "ss_ready": (0, 0, 9, 0, 0),
    "rs_ready": (0, 0, 9, 0, 0),
    "mn_ready": (0, 0, 4, 0, 0),
    "rn_ready": (0, 0, 4, 0, 0),
    "y_ready": (0, 0, 6, 0, 0),
    "oh_done": (0, 0, 10, 0, 0),
    "o_ready": (0, 0, 10, 0, 0),
    "sq_done": (0, 0, 0, 0, 8),
    "dh_done": (0, 0, 0, 0, 8),
    "hid_ready": (2, 0, 0, 0, 8),
    "dve_step": (0, 16, 72, 0, 0),
    "act_step": (0, 0, 11, 0, 0),
    "out_ready": (0, 0, 0, 0, 0),
    "stored": (0, 0, 0, 0, 0),
}


class Count:

    def __init__(self, sems, carried=None):
        self.carried = carried
        self.sems, self.mine, self.last = sems, {}, None
        self.section, self.base = None, None

    def enter(self, section, *regs):
        self.section, self.regs = section, regs
        self.last = ("pv_taken", 0)
        self.mine = {self.carried: 1} if self.carried and section in ("half", "group") else {}

    def value(self, name, k):
        start, *per = RAISED[name]
        if self.section is None:
            return k
        if self.section == "end":
            return start + DEPTH * sum(n * TIMES[s] for s, n in zip(SECTIONS, per)) + k
        whole = sum(n * TIMES[s] for s, n in zip(SECTIONS, per))
        at = SECTIONS.index(self.section)
        fixed = start + sum(n * TIMES[s] for s, n in zip(SECTIONS[:at], per[:at])) + k
        v = self.regs[0] * whole + fixed if whole else fixed
        if len(self.regs) > 1 and per[at]:
            v = self.regs[1] * per[at] + v
        return v

    def at(self, name, k):
        return self.sems[name], self.value(name, k)

    def up(self, name, n=1):
        self.mine[name] = self.mine.get(name, 0) + n
        self.last = (name, self.mine[name])
        return self.sems[name], n

    def own(self):
        return self.at(*self.last)

    def leave(self):
        at = 1 + SECTIONS.index(self.section)
        for name, n in self.mine.items():
            n -= name == self.carried
            assert RAISED[name][at] == n, f"{name} is raised {n} times in {self.section}"


def schedule():
    order = """gates0 gate_math mx0 mx1 mx2 gate_tok gv gu0 gu1 z0 xs0 xs1 xs2 z1 mq0 z2
        ms0 g_norm rqk0 mn0 g_mix rqk1 rot0 mt0 mq1 rqk2 rot1 ms1 rqk3 rot2 mn1 rqk4 rot3 mt1 mq2 rqk5 rot4 ms2 rg0
        rot5 mn2 rg1 rs0 mt2 mq3 rg2 rgs ms3 rv0 mn3 rn0 rv1 mt3 rs1 rt0 rv2 rn1 rv3 rs2 rt1 rn2 rs3 na0 rt2 na1
        rn3 na2 rt3 na3 na4 out0 na5 na6 na7 out1 nsum nh0 nh1 out2 nh2 nh3 out3 nh4 nh5 out4 nh6 nh7 out5 out6 out7"""
    steps = [(s[:-1], int(s[-1])) if s[-1].isdigit() else (s,) for s in order.split()]
    return steps


def units_of(step):
    kind, *a = step
    if kind == "gates":
        return [U_GATE]
    if kind == "gv":
        return [U_GV, U_GV + 1]
    if kind == "rqk":
        return [U_RQ + a[0]]
    if kind == "rv":
        return [U_RV, U_RV + 1, U_RV + 2] if a[0] == 0 else []
    first = {"gu": U_GU, "mx": U_MX, "z": U_Z, "rg": U_RG, "out": U_OUT}
    return [first[kind] + a[0]] if kind in first else []


def groups_of(step):
    return {"nsum": (1, 0), "na": (0, 0), "nh": (0, 0), "gv": (NC, 0), "gate_math": (0, 0), "g_norm": (0, 0), "gate_tok": (0, 1), "rot": (0, 1),
            "g_mix": (0, GT), "mq": (3, 1), "ms": (0, 2), "mn": (0, 3), "mt": (0, 1), "rt": (0, 1), "rs": (0, 3),
            "rn": (0, 2), "out": (0, 1), "xs": (0, 0), "rgs": (0, 0)}.get(step[0], (1, 0))


def places(steps):
    at, out = [0, 0], {}
    for s in steps:
        out[s] = tuple(at)
        at = [x + y for x, y in zip(at, groups_of(s))]
    return out


PA_PADS, PV_PADS = 1, 3
AHEAD = 2


def splits_before(steps):
    free = steps.index(("rv", NC - 1)) + 1
    order = [(i, u) for i, s in enumerate(steps) for u in units_of(s)]
    out = [[] for _ in steps]
    for n, (i, u) in enumerate(order):
        at = order[max(n - AHEAD, 0)][0] if n >= AHEAD else 0
        if u >= U_OUT:
            at = max(at, free)
        out[at].append(u)
    return out


def trunk(nc, x_t, units_d, small_d, const_d, rope_d, out):
    ctx = ExitStack()
    with ctx:
        base = nc.sbuf_base
        ctx.enter_context(nc.sbuf_tensor("arena", [P, (nc.sbuf_bytes_remaining - 512) // 4], F32))
        origin = [base + (-base) % 32]

        def place(name, shape, dt=F32, at=None):
            size = 4
            for n in shape[1:]:
                size *= n
            size += (-size) % 32
            off = origin[0] if at is None else at
            if at is None:
                origin[0] += size
            return nc.alloc_sbuf_tensor_at(name, shape, dt, offset=off), off

        xT, _ = place("xT", [P, KT, S])
        hh, hh_at = place("hh", [P, KT, S], F32R)
        hl, hl_at = place("hl", [P, KT, S], F32R)
        raw, _ = place("raw", [P, RAW, KT * P])
        wh, _ = place("wh", [P, RING, KT, P], F32R)
        wl, _ = place("wl", [P, RING, KT, P], F32R)
        small, _ = place("small", [P, N_SMALL])
        const, _ = place("const", [P, N_CONST])
        bdq, _ = place("bdq", [P, len(PIECES), MD])
        bdk, _ = place("bdk", [P, len(PIECES), MD])
        bdv, _ = place("bdv", [P, MT, P])
        cst, _ = place("cst", [MD, MH, MD + 1])
        rst, _ = place("rst", [P, MT, P])
        hist, _ = place("hist", [P, MT, 3])
        mrow, _ = place("mrow", [MH, T])
        tok, _ = place("tok", [P, 80])
        mp, _ = place("mp", [MH, NC + 1])
        sold, _ = place("sold", [MH, NC])
        soldd, _ = place("soldd", [MH, MH, NC])
        dn, _ = place("dn", [P, 8])
        ms_, _ = place("msum", [P, 8])
        mrs, _ = place("mrs", [P, 8])
        rss_, _ = place("rsum", [P, 8])
        rrs, _ = place("rrs", [P, 8])
        pool_at = origin[0]
        gu, g_at = place("gu", [P, GT, T])
        gv, _ = place("gv", [P, NC, GW])
        rv, _ = place("rv", [P, NC, RW], at=g_at)
        xc, _ = place("xc", [P, MT, T])
        zt, _ = place("zt", [P, MT, T])
        rg, _ = place("rg", [P, MT, T])
        mxp, _ = place("mxp", [P, MT, T + 3])
        rqk, rqk_at = place("rqk", [P, 2 * MT, T])
        hidh, _ = place("hidh", [P, FG, S], F32R, at=pool_at)
        hidl, _ = place("hidl", [P, FG, S], F32R, at=pool_at + 4 * FG * S)
        assert pool_at + 8 * FG * S <= rqk_at
        sq = [place(f"sq{b}", [P, 2, T], at=rqk_at + 8 * T * b)[0] for b in range(2)]
        rstd = [place(f"rstd{b}", [P, T], at=rqk_at + 16 * T + 4 * T * b)[0] for b in range(2)]
        chunk_at = origin[0]
        qT, q_at = place("qT", [MD, MH, L])
        kT, k_at = place("kT", [MD, MH, L])
        et, _ = place("et", [P, MH, L])
        ktok, _ = place("ktok", [P, MW])
        vx, _ = place("vx", [P, MH, MD + 1])
        num, _ = place("num", [P, MH, MD + 1])
        mn, _ = place("mn", [P, MW])
        my, _ = place("my", [P, MT, L])
        gy, _ = place("gy", [P, 2, T], at=origin[0])
        hf, _ = place("hf", [P, 2, T], at=origin[0])
        gsq, _ = place("gsq", [P, T], at=origin[0] + 8 * T)
        rsc = [place(f"rsc{p}", [P, MT, L])[0] for p in range(2)]
        rqx, _ = place("rqx", [P, MT, L])
        rkt, _ = place("rkt", [P, RW])
        ro, _ = place("ro", [P, RW])
        rn, _ = place("rn", [P, RW])
        ry, _ = place("ry", [P, MT, L])
        relu, _ = place("relu", [P, 2, T], at=chunk_at)
        sqh, _ = place("sqh", [P, 2, T], at=chunk_at + 8 * T)
        assert chunk_at + 16 * T <= origin[0]
        assert origin[0] <= nc.sbuf_usable_end, (origin[0], nc.sbuf_usable_end)
        oh, ol = hh[:, :, T:S], hl[:, :, T:S]

        def slot(name, shape, at, k, half):
            return place(name, shape, at=at + 4 * (k * S + half * T))[0]

        ra = slot("ra", [MH, T], hh_at, 0, 1)
        rsint = slot("rsint", [MH, T], hh_at, 1, 1)
        reend = slot("reend", [MH, T], hh_at, 2, 1)
        rem = slot("rem", [MH, T], hl_at, 0, 1)
        rbc = slot("rbc", [MH, T], hl_at, 1, 1)
        rtmp = slot("rtmp", [MH, T], hl_at, 2, 1)
        cos = slot("cos", [P, T], hh_at, 3, 1)
        sin = slot("sin", [P, T], hh_at, 4, 1)
        rot = slot("rot", [P, T], hh_at, 5, 1)
        rig = slot("rig", [MH, T], hl_at, 3, 1)
        rxf = slot("rxf", [MH, T], hl_at, 4, 1)
        pa = [ctx.enter_context(nc.psum_tensor(f"pa{i}", [P, 512], F32)) for i in range(4)]
        pv = [ctx.enter_context(nc.psum_tensor(f"pv{i}", [P, 512], F32)) for i in range(4)]

        sems = {n: ctx.enter_context(nc.semaphore(n)) for n in RAISED}

        def sm(name, k=None):
            a, b = SMALL[name]
            return small[:, a:b] if k is None else small[:, a + k:a + k + 1]

        def cn(name):
            a, b = CONST[name]
            return const[:, a:b]

        eye, ones = cn("eye"), cn("ones")
        decay = cn("decay").rearrange("p (e t l) -> p e t l", e=2, t=MT)
        xi = cn("xi").rearrange("p (t l) -> p t l", t=MT)
        sel = cn("sel").rearrange("p (h l) -> p h l", h=MH)
        ws = sm("ws").rearrange("p (g t) -> p g t", g=GG)
        atok = tok[:, 0:64].rearrange("p (c q h) -> p c q h", c=NC, q=4)
        soldb = tok[:, 64:80].rearrange("p (h c) -> p h c", h=MH)
        steps = schedule()
        ahead = splits_before(steps)
        before = places(steps)

        def nth(ring, step, j=1):
            return before[step]["pa pv".split().index(ring)] + j

        numbered = {}
        for names, kinds in (("ss", ("g_norm", "mn", "rn")), ("o", ("g_mix", "mt", "rt")), ("y", ("g_mix", "mt")),):
            k = 0
            for st in steps:
                if st[0] in kinds:
                    numbered[names, st] = k
                    k += GT if st[0] == "g_mix" else 1
        ends = {}
        for st in steps:
            for u in units_of(st):
                if st[0] == "rv":
                    ends[u] = ("pa_full", nth("pa", ("rv", NC - 1)))
                elif st[0] == "out":
                    ends[u] = ("pv_full", nth("pv", st))
                else:
                    ends[u] = ("pa_full", nth("pa", st, groups_of(st)[0]))
        group_ends = {u: ("pa_full", 2 * (u + 1)) if u < FG else ("pv_full", 4 * (u - FG + 1)) for u in GROUP_UNITS}
        block = ctx.enter_context(nc.Block())

        def unit_at(index):
            return units_d[bass.ds(index, 1), :, :].rearrange("a p n -> (a p) n")

        @block.sync
        def _(sp):
            n = Count(sems)

            def load_unit(n, order, i, index):
                sp.wait_ge(*n.at("w_ready", 0 if i < RAW else order[i - RAW] + 1))
                sp.dma_start(raw[:, i % RAW, :], unit_at(index)).then_inc(*n.up(f"raw{i % RAW}_full", 16))

            def load_next(n, order, index):
                last = max(i for i in range(len(order)) if i % RAW == 0)
                sp.wait_ge(*n.at("w_ready", order[last] + 1))
                sp.dma_start(raw[:, 0, :], unit_at(index)).then_inc(*n.up("raw0_full", 16))

            for j in range(2):
                q = slice(KT // 2 * j, KT // 2 * (j + 1))
                sp.dma_start(xT[:, q, 0:T], x_t[:, q, 0:T]).then_inc(*n.up(f"x{j}_loaded", 16))
            sp.dma_start(const[:, :], const_d).then_inc(*n.up("const_loaded", 16))
            sp.dma_start(raw[:, 0, :], units_d[0, :, :]).then_inc(*n.up("raw0_full", 16))
            with sp.Fori(0, DEPTH) as layer:
                n.enter("pre", layer)
                sp.wait_ge(*n.at("hl_ready", 0))
                sp.dma_start(small[:, :], small_d[bass.ds(layer, 1), :, :].rearrange("a p n -> (a p) n")
                             ).then_inc(*n.up("small_loaded", 16))
                n.leave()
                for half in range(HALVES):
                    n.enter("half", layer, half)
                    for i, u in enumerate(HALF_UNITS):
                        if i:
                            load_unit(n, HALF_UNITS, i, layer * LAYER_UNITS + i)
                        if u == U_MX:
                            sp.wait_ge(*n.at("pv_full", 0))
                            for j, dst in enumerate((cos, sin)):
                                sp.dma_start(dst[:, :], rope_d[half, j, :, :]).then_inc(*n.up("rope_loaded", 16))
                    load_next(n, HALF_UNITS, layer * LAYER_UNITS + half * len(HALF_UNITS))
                    n.leave()
                with sp.Fori(0, GROUPS) as group:
                    n.enter("group", layer, group)
                    first = group * len(GROUP_UNITS) + (layer * LAYER_UNITS + len(HALF_UNITS))
                    for i in GROUP_UNITS[1:]:
                        load_unit(n, GROUP_UNITS, i, first + i)
                    load_next(n, GROUP_UNITS, first + len(GROUP_UNITS))
                    n.leave()
            n.enter("end")
            for h in range(HALVES):
                for j in range(0, KT, 4):
                    sp.wait_ge(*n.at("out_ready", KT * h + j + 4))
                    sp.dma_start(out[:, j:j + 4, T * h:T * h + T], xT[:, j:j + 4, T * h:T * h + T]
                                 ).then_inc(*n.up("stored", 16))
            sp.wait_ge(*n.at("stored", 16 * 4))

        @block.tensor
        def _(pe):
            n = Count(sems)
            rings = {}

            def bank(ring, taken=-4):
                k = rings[ring] = rings.get(ring, 0) + 1
                pe.wait_ge(*n.at(f"{ring}_taken", max(k - 4, taken)))
                return (pa if ring == "pa" else pv)[(k - 1) % 4]

            def norm_sum(name, k, b, pads=0):
                ps = bank("pa")
                pe.wait_ge(*n.at(name, k))
                pe.matmul(ps[:, :], ones, rstd[b][:, :], start=True, stop=True).then_inc(*n.up("pa_full", 1 + pads))

            def feature_tile(u, ring, hready=False):
                ps = bank(ring)
                pe.wait_ge(*n.at("w_ready", u + 1))
                for k in range(KT):
                    if hready:
                        pe.wait_ge(*n.at("hl_ready", k + 1 - KT))
                    pe.matmul(ps[:, :], wh[:, u % RING, k, :], hh[:, k, 0:T], start=(k == 0), stop=False)
                    pe.matmul(ps[:, :], wh[:, u % RING, k, :], hl[:, k, 0:T], start=False, stop=False)
                    ins = pe.matmul(ps[:, :], wl[:, u % RING, k, :], hh[:, k, 0:T], start=False, stop=(k == KT - 1))
                ins.then_inc(*n.up(f"{ring}_full"))
                return ins

            pe.sem_inc(sems["pv_full"], RAISED["pv_full"][0])
            pe.wait_ge(sems["const_loaded"], 16)
            with pe.Fori(0, DEPTH) as layer:
                n.enter("pre", layer)
                rings.clear()
                norm_sum("sq_added", KT - 1, 0, 3)
                n.leave()
                for half in range(HALVES):
                    n.enter("half", layer, half)
                    rings.clear()
                    for step in steps:
                        kind, *a = step
                        c = a[0] if a else 0
                        tk = slice(L * c, L * c + L)
                        if kind == "nsum":
                            norm_sum("sq_added", KT - 1, 0, PA_PADS)
                        elif kind in ("gates", "gu", "mx", "z", "rg", "rqk"):
                            feature_tile(units_of(step)[0], "pa", kind == "gates")
                        elif kind in ("gv", "rv"):
                            u, cols = (U_GV, GT) if kind == "gv" else (U_RV, MT)
                            for cc in (range(NC) if kind == "gv" else [c]):
                                tt = slice(L * cc, L * cc + L)
                                ps = bank("pa")
                                pe.wait_ge(*n.at("w_ready", u + cols))
                                s0 = u % RING
                                o = ps[:, 0:cols * P].rearrange("p (u n) -> p u n", u=cols)
                                for k in range(KT):
                                    pe.matmul(o, hh[:, k, tt], wh[:, s0:s0 + cols, k, :], start=(k == 0), stop=False)
                                    pe.matmul(o, hh[:, k, tt], wl[:, s0:s0 + cols, k, :], start=False, stop=False)
                                    ins = pe.matmul(o, hl[:, k, tt], wh[:, s0:s0 + cols, k, :], start=False,
                                                    stop=(k == KT - 1))
                                ins.then_inc(*n.up("pa_full"))
                        elif kind == "gate_tok":
                            ps = bank("pv")
                            pe.wait_ge(*n.at("sold_ready", 1))
                            pe.matmul(ps[:, 64:80], ones[0:MH, :], soldd[:, :, :], start=True, stop=True)
                            for cc in range(NC):
                                for q, row in enumerate((ra, rsint, reend, rem)):
                                    at = 4 * (4 * cc + q)
                                    ins = pe.transpose(ps[:, at:at + 4], row[:, L * cc:L * cc + L], eye[0:MH, 0:MH])
                            ins.then_inc(*n.up("pv_full"))
                        elif kind == "rot":
                            ps = bank("pv")
                            pe.wait_ge(*n.at("pa_taken", nth("pa", ("rqk", c))))
                            pe.matmul(ps[:, :], cn("swap"), rqk[:, c, :], start=True, stop=True
                                      ).then_inc(*n.up("pv_full"))
                        elif kind == "g_mix":
                            for t in range(GT):
                                ps = bank("pv")
                                pe.wait_ge(*n.at("gvn_ready", 1))
                                for cc in range(NC):
                                    for g in (2 * t, 2 * t + 1):
                                        q = GD * (g % 2)
                                        ins = pe.matmul(ps[q:q + GD, L * cc:L * cc + L],
                                                        gv[:, cc, GD * g:GD * g + GD], ws[:, g, :],
                                                        start=True, stop=True)
                                ins.then_inc(*n.up("pv_full"))
                        elif kind == "mq":
                            if c == 0:
                                pe.wait_ge(*n.at("xc_ready", MT))
                                pe.wait_ge(*n.at("layer_ready", 0))
                            for bd in (bdq, bdk):
                                ps = bank("pa")
                                for h in range(MH):
                                    ts = [i for i, (hd, _) in enumerate(PIECES) if hd == h]
                                    for i in ts:
                                        ins = pe.matmul(ps[0:MD, L * h:L * h + L], bd[:, i, :],
                                                        xc[:, PIECES[i][1], tk],
                                                        start=(i == ts[0]), stop=(i == ts[-1]))
                                ins.then_inc(*n.up("pa_full"))
                            ps = bank("pa")
                            for t in range(MT):
                                ins = pe.matmul(ps[:, P * t:P * t + P], mxp[:, t, 3 + L * c:3 + L * c + L],
                                                bdv[:, t, :], start=True, stop=True)
                            ins.then_inc(*n.up("pa_full"))
                            ps = bank("pv")
                            for h in range(MH):
                                ts = [i for i, (hd, _) in enumerate(PIECES) if hd == h]
                                for i in ts:
                                    ins = pe.matmul(ps[:, MD * h:MD * h + MD], xc[:, PIECES[i][1], tk],
                                                    bdk[:, i, :], start=(i == ts[0]), stop=(i == ts[-1]))
                            ins.then_inc(*n.up("pv_full"))
                        elif kind == "ms":
                            ps = bank("pv")
                            for h in range(MH):
                                ins = pe.matmul(ps[:, L * h:L * h + L], sel[0:MH, h, :], mrow[:, tk],
                                                start=True, stop=True)
                            ins.then_inc(*n.up("pv_full"))
                            ps = bank("pv")
                            pe.wait_ge(*n.at("pa_taken", nth("pa", ("mq", c), 3)))
                            for h in range(MH):
                                ins = pe.matmul(ps[:, L * h:L * h + L], kT[:, h, :], qT[:, h, :],
                                                start=True, stop=True)
                            ins.then_inc(*n.up("pv_full"))
                        elif kind == "mn":
                            w = MD + 1
                            ps = bank("pv", nth("pv", ("mn", c - 1), 3) if c else -4)
                            for h in range(MH):
                                ins = pe.matmul(ps[:, w * h:w * h + w], qT[:, h, :], cst[:, h, :],
                                                start=True, stop=True)
                            ins.then_inc(*n.up("pv_full"))
                            ps = bank("pv", nth("pv", ("ms", c), 2))
                            for h in range(MH):
                                ins = pe.matmul(ps[:, w * h:w * h + w], et[:, h, :], vx[:, h, :],
                                                start=True, stop=True)
                            ins.then_inc(*n.up("pv_full"))
                            ps = bank("pv", nth("pv", ("mq", c)))
                            for h in range(MH):
                                ins = pe.matmul(ps[0:MD, w * h:w * h + w], ktok[:, MD * h:MD * h + MD], vx[:, h, :],
                                                start=True, stop=True)
                            ins.then_inc(*n.up("pv_full"))
                        elif kind in ("mt", "rt"):
                            ps = bank("pv")
                            src, name = (mn, "mn_ready") if kind == "mt" else (rn, "rn_ready")
                            pe.wait_ge(*n.at(name, c + 1))
                            for t in range(MT):
                                ins = pe.transpose(ps[:, P * t:P * t + P], src[:, P * t:P * t + P], eye)
                            ins.then_inc(*n.up("pv_full"))
                        elif kind == "rs":
                            if c == 0:
                                pe.wait_ge(*n.at("rqk_ready", 2 * MT))
                            for p in range(2):
                                ps = bank("pv")
                                for t in range(MT):
                                    ins = pe.matmul(ps[:, L * t:L * t + L], rqk[RD * p:RD * p + RD, MT + t, tk],
                                                    rqk[RD * p:RD * p + RD, t, tk], start=True, stop=True)
                                ins.then_inc(*n.up("pv_full"))
                            ps = bank("pv")
                            for t in range(MT):
                                ins = pe.transpose(ps[:, P * t:P * t + P], rqk[:, MT + t, tk], eye)
                            ins.then_inc(*n.up("pv_full"))
                        elif kind == "rn":
                            ps = bank("pv", max(nth("pv", ("rs", c), 3), nth("pv", ("rn", c - 1), 2) if c else 0))
                            pe.wait_ge(*n.at("pa_taken", nth("pa", ("rv", c))))
                            for t in range(MT):
                                pe.matmul(ps[:, P * t:P * t + P], rqx[:, t, :], rst[:, t, :], start=True, stop=False)
                                for p in range(2):
                                    q = P * t + RD * p
                                    ins = pe.matmul(ps[:, q:q + RD], rsc[p][:, t, :], rv[:, c, q:q + RD],
                                                    start=False, stop=(p == 1))
                            ins.then_inc(*n.up("pv_full"))
                            ps = bank("pv")
                            for t in range(MT):
                                ins = pe.matmul(ps[:, P * t:P * t + P], rkt[:, P * t:P * t + P],
                                                rv[:, c, P * t:P * t + P], start=True, stop=True)
                            ins.then_inc(*n.up("pv_full"))
                        elif kind == "out":
                            u = units_of(step)[0]
                            ps = bank("pv")
                            pe.wait_ge(*n.at("w_ready", u + 1))
                            if c == 0:
                                pe.wait_ge(*n.at("o_ready", 10))
                            for k in range(KT):
                                pe.matmul(ps[:, :], wh[:, u % RING, k, :], oh[:, k, :], start=(k == 0), stop=False)
                                pe.matmul(ps[:, :], wh[:, u % RING, k, :], ol[:, k, :], start=False, stop=False)
                                ins = pe.matmul(ps[:, :], wl[:, u % RING, k, :], oh[:, k, :], start=False,
                                                stop=(k == KT - 1))
                            ins.then_inc(*n.up("pv_full", 1 + PV_PADS * (c == KT - 1)))
                    n.leave()
                n.enter("norm", layer)
                rings.clear()
                norm_sum("sqb_added", KT - 1, 1, 3)
                n.leave()
                with pe.Fori(0, GROUPS) as group:
                    n.enter("group", layer, group)
                    rings.clear()
                    for u in GROUP_UNITS:
                        pe.wait_ge(*n.at("w_ready", u + 1))
                        s0 = u % RING
                        for m in ([0] if u < FG else range(2)):
                            for h in range(HALVES):
                                th = slice(T * h, T * h + T)
                                if u < FG:
                                    ps = bank("pa")
                                    for k in range(KT):
                                        if u == 0 and (h or k == 0):
                                            pe.wait_ge(*n.at("hl_ready", k + 1 - KT if h else -KT))
                                        a, b = wh[:, s0, k, :], wl[:, s0, k, :]
                                        pe.matmul(ps[:, :], a, hh[:, k, th], start=(k == 0), stop=False)
                                        pe.matmul(ps[:, :], a, hl[:, k, th], start=False, stop=False)
                                        ins = pe.matmul(ps[:, :], b, hh[:, k, th], start=False, stop=(k == KT - 1))
                                    ins.then_inc(*n.up("pa_full"))
                                else:
                                    ps = bank("pv")
                                    for k in range(FG):
                                        if u == FG and m == 0:
                                            pe.wait_ge(*n.at("hid_ready", 2 * k + h + 1))
                                        a, b = (w[:, s0, 2 * k + m, :] for w in (wh, wl))
                                        pe.matmul(ps[:, :], a, hidh[:, k, th], start=(k == 0), stop=False)
                                        pe.matmul(ps[:, :], a, hidl[:, k, th], start=False, stop=False)
                                        ins = pe.matmul(ps[:, :], b, hidh[:, k, th], start=False, stop=(k == FG - 1))
                                    ins.then_inc(*n.up("pv_full"))
                    n.leave()
            n.enter("end")
            rings.clear()
            for h in range(HALVES):
                norm_sum("sq_added", (KT - 1) * (h + 1), h)

        @block.scalar
        def _(act):
            n = Count(sems, "hi_done")
            later = Count(sems)
            eps, one = cn("eps"), cn("one")

            def round_unit(order, slot_ends, u):
                i = order.index(u)
                act.wait_ge(*n.at(f"raw{i % RAW}_full", 16 * (i // RAW + 1)))
                if u >= RING:
                    act.wait_ge(*n.at(*slot_ends[u - RING if u - RING in order else u - 2 * RING]))
                elif u:
                    act.wait_ge(*n.at("pv_full", (0, -PV_PADS - 2)[u - 1]))
                act.activation(wh[:, u % RING, :, :].rearrange("p k n -> p (k n)"), raw[:, i % RAW, :], ACT.Copy
                               ).then_inc(*n.up("hi_done", 1 if u + 1 in order else 2))

            def round_next(order, slot_ends):
                act.wait_ge(*n.at("raw0_full", 16 * (1 + (len(order) + 1) // RAW)))
                act.wait_ge(*n.at(*slot_ends[max(u for u in order if u % RING == 0)]))
                act.activation(wh[:, 0, :, :].rearrange("p k n -> p (k n)"), raw[:, 0, :], ACT.Copy
                               ).then_inc(*n.up("hi_done"))

            def inv_rms(dst, src, width, name, wait_own=True):
                act.activation(dst, src, ACT.Ln, bias=eps, scale=1.0 / width).then_inc(*n.up("act_step"))
                act.wait_ge(*n.own())
                act.activation(dst, dst, ACT.Exp, scale=-0.5).then_inc(*n.up(name))

            def square(n, k, b, cols, first=0, names=("sq_ready", "sq_added")):
                if k >= 3:
                    act.wait_ge(*n.at(names[1], first * (KT - 1) + k - 2))
                act.activation(sq[b][:, k % 2, :] if k else rstd[b][:, :], xT[:, k, cols], ACT.Square
                               ).then_inc(*n.up(names[0]))

            def inv_norm(k, b, pads=0):
                act.wait_ge(*n.at("pa_full", k))
                act.activation(rstd[b][:, :], pa[(k - 1) % 4][:, :], ACT.Ln, bias=eps, scale=1.0 / D
                               ).then_inc(*n.up("pa_taken", 1 + pads))
                act.wait_ge(*n.own())
                act.activation(rstd[b][:, :], rstd[b][:, :], ACT.Exp, scale=-0.5).then_inc(*n.up("rstd_ready"))

            def round_h(k, th):
                act.wait_ge(*n.at("h_ready", k + 1))
                act.activation(hh[:, k, th], hf[:, k % 2, :], ACT.Copy).then_inc(*n.up("hh_done"))

            def take(step, dst, func, j=1, rows=slice(0, P), cols=slice(0, 512), shape=None, pads=0, **kw):
                k = nth("pa", step, j)
                act.wait_ge(*n.at("pa_full", k))
                src = pa[(k - 1) % 4][rows, cols]
                if shape:
                    src = src.rearrange(shape[0], **shape[1])
                act.activation(dst, src, func, **kw).then_inc(*n.up("pa_taken", 1 + pads))

            act.sem_inc(sems["pa_taken"], RAISED["pa_taken"][0])
            act.wait_ge(sems["x1_loaded"], 16)
            act.dma_start(xT[:, :, T:S], x_t[:, :, T:S]).then_inc(sems["x2_loaded"], 16)
            round_unit(HALF_UNITS, ends, 0)
            act.preload_act_table_set("natural_log_exp_and_others")
            with act.Fori(0, DEPTH) as layer:
                n.enter("pre", layer)
                act.wait_ge(*n.at("pv_taken", 0))
                for k in range(KT):
                    if k % (KT // 2) == 0:
                        act.wait_ge(sems[f"x{k // (KT // 2)}_loaded"], 16)
                    square(n, k, 0, slice(0, T))
                act.wait_ge(sems["const_loaded"], 16)
                inv_norm(1, 0, 3)
                for k in range(KT):
                    round_h(k, slice(0, T))
                n.leave()
                for half in range(HALVES):
                    later.enter("norm", layer)
                    n.enter("half", layer, half)
                    for i, step in enumerate(steps):
                        for u in ahead[i]:
                            if u:
                                round_unit(HALF_UNITS, ends, u)
                        if step == ("out", KT - 1):
                            round_next(HALF_UNITS, ends)
                        kind, *a = step
                        c = a[0] if a else 0
                        tk = slice(L * c, L * c + L)
                        other = slice(T, S) if half == 0 else slice(0, T)
                        if kind == "na":
                            if c == 0:
                                act.wait_ge(*n.at("pv_taken", nth("pv", ("rs", NC - 1), 3)))
                                act.wait_ge(sems["x2_loaded"], 16)
                            square(n, c, 0, other)
                        elif kind == "nsum":
                            inv_norm(nth("pa", step), 0, PA_PADS)
                        elif kind == "nh":
                            round_h(c, slice(0, T))
                        elif kind == "out":
                            if half == HALVES - 1:
                                act.wait_ge(*n.at("pv_taken", nth("pv", step)))
                                square(later, c, 1, slice(T, S), names=("sqb_ready", "sqb_added"))
                        elif kind == "gates":
                            k = nth("pa", step)
                            act.wait_ge(*n.at("small_loaded", 0))
                            act.wait_ge(*n.at("pa_full", k))
                            ps = pa[(k - 1) % 4]
                            act.activation(rig[:, :], ps[0:MH, :], ACT.Identity, bias=sm("i_bias")[0:MH, :])
                            act.activation(rxf[:, :], ps[32:32 + MH, :], ACT.Identity, bias=sm("f_bias")[32:32 + MH, :]
                                           ).then_inc(*n.up("pa_taken"))
                        elif kind == "gv":
                            for cc in range(NC):
                                take(step, gv[:, cc, :], ACT.Gelu_apprx_tanh, j=cc + 1, cols=slice(0, GW))
                        elif kind == "gu":
                            take(step, gu[:, c, :], ACT.Gelu_apprx_tanh)
                        elif kind == "mx":
                            take(step, mxp[:, c, 3:3 + T], ACT.Copy)
                        elif kind == "z":
                            take(step, zt[:, c, :], ACT.Silu)
                        elif kind == "rg":
                            take(step, rg[:, c, :], ACT.Copy)
                        elif kind == "xs":
                            act.wait_ge(*n.at("conv_done", c + 1))
                            act.activation(xc[:, c, :], xc[:, c, :], ACT.Silu).then_inc(*n.up("xc_ready"))
                        elif kind == "rgs":
                            act.wait_ge(*n.at("pa_taken", nth("pa", ("rg", MT - 1))))
                            act.activation(rg[:, :, :], rg[:, :, :], ACT.Silu).then_inc(*n.up("rg_ready"))
                            act.preload_act_table_set("natural_log_exp_and_others")
                        elif kind == "gate_math":
                            act.wait_ge(*n.at("pa_taken", nth("pa", ("gates", 0))))
                            act.activation(rtmp[:, :], rxf[:, :], ACT.Abs).then_inc(*n.up("act_step"))
                            act.wait_ge(*n.own())
                            act.activation(rtmp[:, :], rtmp[:, :], ACT.Exp, scale=-1.0).then_inc(*n.up("act_step"))
                            act.wait_ge(*n.own())
                            act.activation(rtmp[:, :], rtmp[:, :], ACT.Ln, bias=one[0:MH, :]
                                           ).then_inc(*n.up("softplus_ready"))
                        elif kind == "gate_tok":
                            act.wait_ge(*n.at("rows_ready", 1))
                            for row in (rsint, reend, rem):
                                act.activation(row[:, :], row[:, :], ACT.Exp)
                            act.activation(sold[:, :], sold[:, :], ACT.Exp).then_inc(*n.up("rows_exp"))
                        elif kind in ("g_norm", "mn", "rn"):
                            k, w, src, dst = {"g_norm": (NC, GW, ms_, mrs), "mn": (MH, MD, ms_, mrs),
                                              "rn": (RH, RD, rss_, rrs)}[kind]
                            act.wait_ge(*n.at("ss_ready", numbered["ss", step] + 1))
                            inv_rms(dst[:, 0:k], src[:, 0:k], w, "rs_ready")
                        elif kind == "rqk":
                            take(step, rqk[:, c, :], ACT.Copy)
                        elif kind == "rv":
                            take(step, rv[:, c, :], ACT.Copy, cols=slice(0, RW))
                        elif kind == "mq":
                            for j, (dst, scale) in enumerate(((qT, 1.0), (kT, MD ** -0.5))):
                                take(step, dst[:, :, :], ACT.Copy, j=j + 1, rows=slice(0, MD),
                                     shape=("p (h l) -> p h l", {"h": MH}), scale=scale)
                            take(step, vx[:, :, 0:MD], ACT.Copy, j=3, cols=slice(0, MW),
                                 shape=("p (h d) -> p h d", {"h": MH}))
                        elif kind == "ms":
                            if c == 0:
                                act.preload_act_table_set("natural_log_exp_and_others")
                            act.wait_ge(*n.at("pv_taken", nth("pv", step)))
                            act.activation(et[:, :, :], et[:, :, :], ACT.Exp).then_inc(*n.up("e_ready"))
                        if kind == "g_mix":
                            for t in range(GT):
                                act.wait_ge(*n.at("y_ready", numbered["y", step] + t + 1))
                                act.activation(oh[:, 2 * MT + t, :], gy[:, t, :], ACT.Copy).then_inc(*n.up("oh_done"))
                        elif kind == "mt":
                            act.wait_ge(*n.at("y_ready", numbered["y", step] + 1))
                            act.activation(oh[:, 0:MT, tk], my[:, :, :], ACT.Copy).then_inc(*n.up("oh_done"))
                        elif kind == "rt":
                            act.wait_ge(*n.at("pv_taken", nth("pv", step)))
                            act.activation(oh[:, MT:2 * MT, tk], ry[:, :, :], ACT.Copy).then_inc(*n.up("oh_done"))
                    n.leave()
                n.enter("norm", layer)
                inv_norm(1, 1, 3)
                for k in range(KT):
                    round_h(k, slice(T, S))
                n.leave()
                with act.Fori(0, GROUPS) as group:
                    n.enter("group", layer, group)
                    round_unit(GROUP_UNITS, group_ends, 1)

                    def round_square(e):
                        act.wait_ge(*n.at("sq_done", e + 1))
                        h = e % HALVES
                        act.activation(hidh[:, e // HALVES, T * h:T * h + T], sqh[:, e % 2, :], ACT.Copy
                                       ).then_inc(*n.up("dh_done"))

                    for u in range(FG):
                        round_unit(GROUP_UNITS, group_ends, u + 2)
                        for e in (2 * u, 2 * u + 1):
                            act.wait_ge(*n.at("pa_full", e + 1))
                            act.activation(relu[:, e % 2, :], pa[e % 4][:, :], ACT.Relu).then_inc(*n.up("pa_taken"))
                            if e:
                                round_square(e - 1)
                    round_square(2 * FG - 1)
                    for u in (FG + 2, FG + 3):
                        round_unit(GROUP_UNITS, group_ends, u)
                    round_next(GROUP_UNITS, group_ends)
                    n.leave()
            n.enter("end")
            act.wait_ge(*n.at("pv_taken", 0))
            for h in range(HALVES):
                for k in range(KT):
                    square(n, k, h, slice(T * h, T * h + T), h)
                if h:
                    inv_norm(h, h - 1)
            inv_norm(HALVES, 1)

        @block.vector
        def _(dve):
            n = Count(sems, "w_ready")
            later = Count(sems)

            def rest_unit(order, u):
                i = order.index(u)
                dve.wait_ge(*n.at("hi_done", u + 1))
                dve.tensor_tensor(wl[:, u % RING, :, :].rearrange("p k n -> p (k n)"), raw[:, i % RAW, :],
                                  wh[:, u % RING, :, :].bitcast(F32).rearrange("p k n -> p (k n)"), ALU.subtract
                                  ).then_inc(*n.up("w_ready", 1 if u + 1 in order else 2))

            def rest_next(order):
                dve.wait_ge(*n.at("hi_done", order[-1] + 3))
                dve.tensor_tensor(wl[:, 0, :, :].rearrange("p k n -> p (k n)"), raw[:, 0, :],
                                  wh[:, 0, :, :].bitcast(F32).rearrange("p k n -> p (k n)"), ALU.subtract
                                  ).then_inc(*n.up("w_ready"))

            def add_square(n, k, b, first=0, names=("sq_ready", "sq_added")):
                if k == 0:
                    return
                dve.wait_ge(*n.at(names[0], first * KT + k + 1))
                if k > 1:
                    dve.wait_ge(*n.at(names[1], first * (KT - 1) + k - 1))
                dve.tensor_tensor(rstd[b][:, :], rstd[b][:, :], sq[b][:, k % 2, :], ALU.add
                                  ).then_inc(*n.up(names[1]))

            def make_h(k, b, cols, th, g):
                if k == 0:
                    dve.wait_ge(*n.at("rstd_ready", 1))
                go()
                dve.scalar_tensor_tensor(hf[:, k % 2, :], xT[:, k, cols], g[:, k:k + 1], rstd[b][:, :],
                                         ALU.mult, ALU.mult).then_inc(*n.up("h_ready"))
                for j in range(max(k - 1, 0), k + (k == KT - 1)):
                    dve.wait_ge(*n.at("hh_done", j + 1))
                    dve.tensor_tensor(hl[:, j, th], hf[:, j % 2, :], hh[:, j, th].bitcast(F32), ALU.subtract
                                      ).then_inc(*n.up("hl_ready"))

            def step_done(ins):
                ins.then_inc(*n.up("dve_step"))
                dve.wait_ge(*n.own())

            def go():
                dve.wait_ge(*n.own())

            def full(step, j=1):
                k = nth("pv", step, j)
                dve.wait_ge(*n.at("pv_full", k))
                return pv[(k - 1) % 4]

            def rest_output(step, dst, src, j=0):
                dve.wait_ge(*n.at("oh_done", numbered["o", step] + j + 1))
                dve.tensor_tensor(ol[:, dst[0], dst[1]], src, oh[:, dst[0], dst[1]].bitcast(F32), ALU.subtract
                                  ).then_inc(*n.up("o_ready"))

            for name in ("w_ready", "pv_taken", "hl_ready", "hid_ready"):
                dve.sem_inc(sems[name], RAISED[name][0])
            rest_unit(HALF_UNITS, 0)
            with dve.Fori(0, DEPTH) as layer:
                n.enter("pre", layer)
                for k in range(KT):
                    add_square(n, k, 0)
                dve.wait_ge(*n.at("small_loaded", 16))
                for k in range(KT):
                    make_h(k, 0, slice(0, T), slice(0, T), sm("g_mix"))
                dve.wait_ge(sems["const_loaded"], 16)
                for bd in (bdq, bdk):
                    dve.memset(bd[:, :, :], 0.0)
                for buf in (bdv, cst, rst, hist):
                    dve.memset(buf[:, :, :], 0.0)
                dve.memset(mp[:, :], 0.0)
                step_done(dve.memset(vx[:, :, MD:MD + 1], 1.0))
                blocks = cn("blocks")
                for bd, name in ((bdq, "wq"), (bdk, "wk")):
                    w = sm(name).rearrange("p (t j) -> p t j", j=4)
                    for i, (h, t) in enumerate(PIECES):
                        lo, hi = max(MD * h, P * t), min(MD * h + MD, P * t + P)
                        nb = (hi - lo) // 4
                        dve.tensor_tensor(
                            bd[:, i, lo - MD * h:hi - MD * h].rearrange("p (n j) -> p n j", j=4),
                            blocks[:, lo - P * t:hi - P * t].rearrange("p (n j) -> p n j", j=4),
                            w[:, t:t + 1, :].broadcast_to([P, nb, 4]), ALU.mult).then_inc(*n.up("dve_step"))
                w = sm("wv").rearrange("p (t j) -> p t j", j=4)
                for t in range(MT):
                    dve.tensor_tensor(bdv[:, t, :].rearrange("p (n j) -> p n j", j=4),
                                      blocks.rearrange("p (n j) -> p n j", j=4),
                                      w[:, t:t + 1, :].broadcast_to([P, P // 4, 4]), ALU.mult
                                      ).then_inc(*n.up("dve_step"))
                dve.tensor_tensor(ws, ws, cn("causal").rearrange("p (a l) -> p a l", a=1).broadcast_to([P, GG, L]),
                                  ALU.mult).then_inc(*n.up("layer_ready"))
                n.leave()
                for half in range(HALVES):
                    later.enter("norm", layer)
                    n.enter("half", layer, half)
                    dve.wait_ge(*n.at("pv_taken", 0))
                    for i, step in enumerate(steps):
                        for u in ahead[i]:
                            if u:
                                rest_unit(HALF_UNITS, u)
                        if step == ("out", KT - 1):
                            rest_next(HALF_UNITS)
                        kind, *a = step
                        c = a[0] if a else 0
                        tk = slice(L * c, L * c + L)
                        other = slice(T, S) if half == 0 else slice(0, T)
                        xcols = slice(half * T, half * T + T)
                        if kind == "na":
                            add_square(n, c, 0)
                        elif kind == "nh":
                            make_h(c, 0, other, slice(0, T), sm("g_ff" if half else "g_mix"))
                        elif kind == "mx":
                            dve.wait_ge(*n.at("pa_taken", nth("pa", step)))
                            go()
                            dve.tensor_copy(mxp[:, c, 0:3], hist[:, c, :]).then_inc(*n.up("dve_step"))
                            go()
                            step_done(dve.tensor_copy(hist[:, c, :], mxp[:, c, T:T + 3]))
                            w = sm("conv_w")
                            step_done(dve.tensor_scalar(xc[:, c, :], mxp[:, c, 0:T], w[:, 4 * c:4 * c + 1],
                                                        sm("conv_b", c), ALU.mult, ALU.add))
                            for j in range(1, 4):
                                ins = dve.scalar_tensor_tensor(xc[:, c, :], mxp[:, c, j:j + T],
                                                               w[:, 4 * c + j:4 * c + j + 1], xc[:, c, :],
                                                               ALU.mult, ALU.add)
                                if j < 3:
                                    step_done(ins)
                            ins.then_inc(*n.up("conv_done"))
                        elif kind == "gate_math":
                            go()
                            v3 = lambda r: r[:, :].rearrange("h (c l) -> h c l", c=NC)
                            dve.wait_ge(*n.at("softplus_ready", 1))
                            step_done(dve.scalar_tensor_tensor(rtmp[:, :], rxf[:, :], 0.0, rtmp[:, :],
                                                               ALU.min, ALU.subtract))
                            for cc in range(NC):
                                t = slice(L * cc, L * cc + L)
                                ins = dve.tensor_tensor_scan(rbc[:, t], rtmp[:, t], cn("zero")[0:MH, :], 0.0,
                                                             ALU.add, ALU.add)
                            step_done(ins)
                            dve.tensor_copy(mp[:, 0:1], mp[:, NC:NC + 1]).then_inc(*n.up("dve_step"))
                            step_done(dve.tensor_tensor(ra[:, :], rig[:, :], rbc[:, :], ALU.subtract))
                            for cc in range(NC):
                                t, e = slice(L * cc, L * cc + L), L * cc + L - 1
                                step_done(dve.tensor_tensor_scan(mrow[:, t], ra[:, t], ra[:, t], mp[:, cc:cc + 1],
                                                                 ALU.max, ALU.max))
                                step_done(dve.tensor_tensor(mp[:, cc + 1:cc + 2], mrow[:, e:e + 1], rbc[:, e:e + 1],
                                                            ALU.add))
                            ends_m = v3(mrow)[:, :, L - 1:L]
                            dve.tensor_tensor(v3(rsint), mp[:, 0:NC].rearrange("h (c a) -> h c a", a=1).broadcast_to(
                                [MH, NC, L]), v3(mrow), ALU.subtract)
                            dve.tensor_tensor(v3(reend), v3(ra), ends_m.broadcast_to([MH, NC, L]), ALU.subtract)
                            dve.scalar_tensor_tensor(rem[:, :], rbc[:, :], -1.0, mrow[:, :], ALU.mult, ALU.subtract)
                            dve.tensor_tensor(sold[:, :], mp[:, 0:NC], ends_m.rearrange("h c a -> h (c a)"),
                                              ALU.subtract).then_inc(*n.up("rows_ready"))
                        elif kind == "gate_tok":
                            dve.wait_ge(*n.at("rows_exp", 1))
                            dve.tensor_tensor(
                                soldd[:, :, :], sold[:, :].rearrange("h (a c) -> h a c", a=1).broadcast_to([MH, MH, NC]),
                                cn("eye4")[0:MH, :].rearrange("h (g a) -> h g a", a=1).broadcast_to([MH, MH, NC]),
                                ALU.mult).then_inc(*n.up("sold_ready"))
                            ps = full(step)
                            go()
                            dve.tensor_copy(tok[:, :], ps[:, 0:80]).then_inc(*n.up("pv_taken"))
                        elif kind == "g_norm":
                            dve.wait_ge(*n.at("pa_taken", nth("pa", ("gv",), NC)))
                            for b in range(2):
                                s2 = gsq[:, :].rearrange("p (c n) -> p c n", c=2)
                                go()
                                step_done(dve.tensor_tensor(s2, gv[:, 2 * b:2 * b + 2, :], gv[:, 2 * b:2 * b + 2, :],
                                                            ALU.mult))
                                dve.tensor_reduce(ms_[:, 2 * b:2 * b + 2], s2, AX_X, ALU.add
                                                  ).then_inc(*n.up("ss_ready" if b else "dve_step"))
                            dve.wait_ge(*n.at("rs_ready", numbered["ss", step] + 1))
                            for cc in range(NC):
                                ins = dve.scalar_tensor_tensor(gv[:, cc, :], gv[:, cc, :], mrs[:, cc:cc + 1],
                                                               sm("g_norm"), ALU.mult, ALU.mult)
                            ins.then_inc(*n.up("gvn_ready"))
                        elif kind == "rot":
                            if c == 0:
                                dve.wait_ge(*n.at("rope_loaded", 32))
                            ps = full(step)
                            go()
                            dve.tensor_tensor(rot[:, :], ps[:, :], sin[:, :], ALU.mult).then_inc(*n.up("pv_taken"))
                            step_done(dve.tensor_tensor(rqk[:, c, :], rqk[:, c, :], cos[:, :], ALU.mult))
                            dve.tensor_tensor(rqk[:, c, :], rqk[:, c, :], rot[:, :], ALU.add
                                              ).then_inc(*n.up("rqk_ready"))
                        elif kind == "g_mix":
                            bs = sm("bs").rearrange("p (t a l) -> p t a l", t=GT, a=1)
                            go()
                            for t in range(GT):
                                ps = full(step, t + 1)
                                y = gy[:, t, :].rearrange("p (c l) -> p c l", c=NC)
                                dve.tensor_tensor(y, ps[:, :].rearrange("p (c l) -> p c l", c=NC),
                                                  bs[:, t, :, :].broadcast_to([P, NC, L]), ALU.add
                                                  ).then_inc(*n.up("pv_taken"))
                                dve.wait_ge(*n.own())
                                dve.tensor_tensor(gy[:, t, :], gy[:, t, :], gu[:, t, :], ALU.mult
                                                  ).then_inc(*n.up("y_ready"))
                            for t in range(GT):
                                rest_output(step, (2 * MT + t, slice(0, T)), gy[:, t, :], t)
                        elif kind == "mq":
                            ps = full(step)
                            heads = lambda ap: ap.rearrange("p (h d) -> p h d", h=MH)
                            go()
                            dve.scalar_tensor_tensor(
                                heads(ktok[:, :]), heads(ps[:, 0:MW]), MD ** -0.5,
                                atok[:, c, 2, :].rearrange("p (h a) -> p h a", a=1).broadcast_to([P, MH, MD]),
                                ALU.mult, ALU.mult).then_inc(*n.up("pv_taken"))
                        elif kind == "ms":
                            ps = full(step)
                            go()
                            for h in range(MH):
                                ins = dve.scalar_tensor_tensor(et[:, h, :], ps[:, L * h:L * h + L],
                                                               atok[:, c, 0, h:h + 1], cn("upper"), ALU.add, ALU.min)
                            ins.then_inc(*n.up("pv_taken"))
                            dve.wait_ge(*n.at("e_ready", c + 1))
                            ps = full(step, 2)
                            dve.tensor_tensor(et[:, :, :], ps[:, :].rearrange("p (h l) -> p h l", h=MH), et[:, :, :],
                                              ALU.mult).then_inc(*n.up("pv_taken"))
                        elif kind == "mn":
                            w = MH * (MD + 1)
                            heads = lambda ap: ap.rearrange("p (h d) -> p h d", h=MH)
                            wide = lambda ap, m=P, d=MD + 1: ap.rearrange("p (h a) -> p h a", a=1).broadcast_to([m, MH, d])
                            ps = full(step)
                            go()
                            dve.tensor_tensor(num[:, :, :], heads(ps[:, 0:w]), wide(atok[:, c, 1, :]), ALU.mult
                                              ).then_inc(*n.up("pv_taken"))
                            ps = full(step, 2)
                            dve.wait_ge(*n.own())
                            dve.tensor_tensor(num[:, :, :], heads(ps[:, 0:w]), num[:, :, :], ALU.add
                                              ).then_inc(*n.up("pv_taken"))
                            step_done(dve.tensor_tensor(cst[:, :, :], cst[:, :, :], soldb[0:MD, :, c:c + 1].broadcast_to(
                                [MD, MH, MD + 1]), ALU.mult))
                            ps = full(step, 3)
                            dve.tensor_tensor(cst[:, :, :], heads(ps[0:MD, 0:w]), cst[:, :, :], ALU.add
                                              ).then_inc(*n.up("pv_taken"))
                            step_done(dve.scalar_tensor_tensor(dn[:, 0:MH], num[:, :, MD], -1.0, num[:, :, MD],
                                                               ALU.mult, ALU.max))
                            step_done(dve.tensor_tensor(dn[:, 0:MH], dn[:, 0:MH], atok[:, c, 3, :], ALU.max))
                            step_done(dve.reciprocal(dn[:, 4:4 + MH], dn[:, 0:MH]))
                            step_done(dve.tensor_tensor(num[:, :, 0:MD], num[:, :, 0:MD], wide(dn[:, 4:4 + MH], d=MD),
                                                        ALU.mult))
                            step_done(dve.tensor_tensor(heads(mn[:, :]), num[:, :, 0:MD], num[:, :, 0:MD], ALU.mult))
                            dve.tensor_reduce(ms_[:, 0:MH], heads(mn[:, :]), AX_X, ALU.add
                                              ).then_inc(*n.up("ss_ready"))
                            dve.wait_ge(*n.at("rs_ready", numbered["ss", step] + 1))
                            dve.tensor_tensor(heads(mn[:, :]), num[:, :, 0:MD], wide(mrs[:, 0:MH], d=MD), ALU.mult
                                              ).then_inc(*n.up("mn_ready"))
                        elif kind == "mt":
                            ps = full(step)
                            go()
                            for t in range(MT):
                                ins = dve.tensor_scalar(my[:, t, :], ps[:, P * t:P * t + P], sm("m_norm", t), None,
                                                        ALU.mult)
                            ins.then_inc(*n.up("pv_taken"))
                            dve.wait_ge(*n.own())
                            for t in range(MT):
                                ins = dve.scalar_tensor_tensor(my[:, t, :], xc[:, t, tk], sm("skip", t), my[:, t, :],
                                                               ALU.mult, ALU.add)
                            step_done(ins)
                            dve.tensor_tensor(my[:, :, :], my[:, :, :], zt[:, :, tk], ALU.mult
                                              ).then_inc(*n.up("y_ready"))
                            rest_output(step, (slice(0, MT), tk), my[:, :, :])
                        elif kind == "rs":
                            for p in range(2):
                                ps = full(step, p + 1)
                                if p == 0:
                                    go()
                                    dve.tensor_tensor(rqx[:, :, :], rqk[:, 0:MT, tk], xi, ALU.mult)
                                dve.tensor_tensor(rsc[p][:, :, :], ps[:, 0:MT * L].rearrange("p (t l) -> p t l", t=MT),
                                                  decay[:, p, :, :], ALU.mult).then_inc(*n.up("pv_taken"))
                            ps = full(step, 3)
                            dve.tensor_tensor(
                                rkt[:, :].rearrange("p (h d) -> p h d", h=RH),
                                ps[:, 0:RW].rearrange("p (h d) -> p h d", h=RH),
                                cn("zeta").rearrange("p (h a) -> p h a", a=1).broadcast_to([P, RH, RD]), ALU.mult
                                ).then_inc(*n.up("pv_taken"))
                        elif kind == "rn":
                            heads = lambda ap: ap.rearrange("p (h d) -> p h d", h=RH)
                            ps = full(step)
                            go()
                            dve.tensor_copy(ro[:, :], ps[:, 0:RW]).then_inc(*n.up("pv_taken"))
                            step_done(dve.tensor_tensor(rst[:, :, :], rst[:, :, :], cn("gl").rearrange(
                                "p (t a) -> p t a", a=1).broadcast_to([P, MT, P]), ALU.mult))
                            ps = full(step, 2)[:, 0:RW].rearrange("p (t n) -> p t n", t=MT)
                            for p in range(2):
                                q = slice(RD * p, RD * p + RD)
                                ins = dve.tensor_tensor(rst[q, :, q], ps[q, :, q], rst[q, :, q], ALU.add)
                            ins.then_inc(*n.up("pv_taken"))
                            step_done(dve.tensor_tensor(rn[:, :], ro[:, :], ro[:, :], ALU.mult))
                            dve.tensor_reduce(rss_[:, 0:RH], heads(rn[:, :]), AX_X, ALU.add).then_inc(*n.up("ss_ready"))
                            dve.wait_ge(*n.at("rs_ready", numbered["ss", step] + 1))
                            dve.tensor_tensor(heads(rn[:, :]), heads(ro[:, :]), rrs[:, 0:RH].rearrange(
                                "p (h a) -> p h a", a=1).broadcast_to([P, RH, RD]), ALU.mult
                                ).then_inc(*n.up("rn_ready"))
                        elif kind == "rt":
                            if c == 0:
                                dve.wait_ge(*n.at("rg_ready", 1))
                            ps = full(step)
                            go()
                            for t in range(MT):
                                ins = dve.scalar_tensor_tensor(ry[:, t, :], ps[:, P * t:P * t + P], sm("r_norm", t),
                                                               rg[:, t, tk], ALU.mult, ALU.mult)
                            ins.then_inc(*n.up("pv_taken"))
                            rest_output(step, (slice(MT, 2 * MT), tk), ry[:, :, :])
                        elif kind == "out":
                            ps = full(step)
                            go()
                            dve.tensor_tensor(xT[:, c, xcols], ps[:, :], xT[:, c, xcols], ALU.add
                                              ).then_inc(*n.up("pv_taken", 1 + PV_PADS * (c == KT - 1)))
                            if half == HALVES - 1:
                                for k in [c - 1] if c < KT - 1 else [c - 1, c]:
                                    if k > 0:
                                        add_square(later, k, 1, names=("sqb_ready", "sqb_added"))
                    n.leave()
                n.enter("norm", layer)
                for k in range(KT):
                    make_h(k, 1, slice(T, S), slice(T, S), sm("g_ff"))
                n.leave()
                with dve.Fori(0, GROUPS) as group:
                    n.enter("group", layer, group)
                    rest_unit(GROUP_UNITS, 1)

                    def rest_square(e):
                        dve.wait_ge(*n.at("dh_done", e + 1))
                        th = slice(T * (e % HALVES), T * (e % HALVES) + T)
                        dve.tensor_tensor(hidl[:, e // HALVES, th], sqh[:, e % 2, :],
                                          hidh[:, e // HALVES, th].bitcast(F32), ALU.subtract
                                          ).then_inc(*n.up("hid_ready"))

                    for u in range(FG):
                        rest_unit(GROUP_UNITS, u + 2)
                        for e in (2 * u, 2 * u + 1):
                            dve.wait_ge(*n.at("pa_taken", e + 1))
                            dve.wait_ge(*n.at("hid_ready", e - 1))
                            dve.tensor_tensor(sqh[:, e % 2, :], relu[:, e % 2, :], relu[:, e % 2, :], ALU.mult
                                              ).then_inc(*n.up("sq_done"))
                            if e:
                                rest_square(e - 1)
                    rest_square(2 * FG - 1)
                    for q in range(KT // 2):
                        if q < 2:
                            rest_unit(GROUP_UNITS, FG + 2 + q)
                        for j in range(4):
                            m, th = 2 * q + j // 2, slice(T * (j % 2), T * (j % 2) + T)
                            if q == KT // 2 - 1 and j == 1:
                                rest_next(GROUP_UNITS)
                            k = 4 * q + j
                            dve.wait_ge(*n.at("pv_full", k + 1))
                            dve.tensor_tensor(xT[:, m, th], pv[k % 4][:, :], xT[:, m, th], ALU.add
                                              ).then_inc(*n.up("pv_taken"))
                    n.leave()
            n.enter("end")

            def scale(h):
                th = slice(T * h, T * h + T)
                dve.wait_ge(*n.at("rstd_ready", h + 1))
                for k in range(KT):
                    dve.scalar_tensor_tensor(xT[:, k, th], xT[:, k, th], cn("final_g")[:, k:k + 1], rstd[h][:, :],
                                             ALU.mult, ALU.mult).then_inc(*n.up("out_ready"))

            for h in range(HALVES):
                for k in range(KT):
                    add_square(n, k, h, h)
            for h in range(HALVES):
                scale(h)


def _unit(w):
    return w.reshape(KT, P, P).transpose(1, 0, 2).reshape(P, KT * P)


def _constants(np):
    c = np.zeros((P, N_CONST), np.float32)

    def put(name, v):
        a, b = CONST[name]
        v = np.asarray(v, np.float32)
        v = v.reshape(v.shape[0], -1)
        c[:v.shape[0], a:b] = v

    i = np.arange(P)
    put("upper", np.where(i[:, None] <= i[None, :], 0.0, -BIG))
    put("causal", i[:, None] <= i[None, :])
    put("blocks", i[:, None] // 4 == i[None, :] // 4)
    put("eye", np.eye(P))
    put("ones", np.ones((P, P)))
    put("swap", i[:, None] == (i[None, :] ^ 32))
    lg = np.log(1.0 - 2.0 ** (-5.0 - np.arange(RH)))
    heads = np.stack([2 * np.arange(MT) + p for p in range(2)])
    rel = np.maximum(i[None, :] - i[:, None], 0)
    put("decay", np.stack([[np.where(i[:, None] <= i[None, :], np.exp(rel * lg[h]), 0.0) * RD ** -0.5 for h in r]
                           for r in heads]).transpose(2, 0, 1, 3))
    mine = heads[i // RD]
    put("xi", np.exp(lg[mine][:, :, None] * (i + 1.0)))
    put("gl", np.exp(L * lg[mine]))
    put("zeta", np.exp((L - 1.0 - i)[:, None] * lg[None, :]) * RD ** -0.5)
    put("sel", -np.repeat(np.eye(MH)[:, :, None], P, 2))
    put("eye4", np.eye(MH))
    put("eps", np.full((P, 1), EPS))
    put("one", np.ones((P, 1)))
    return c


def _rope(np):
    half = RD // 2
    pos = np.arange(S, dtype=np.float32)
    freq = np.float32(10000.0) ** (-np.arange(half, dtype=np.float32) / np.float32(half))
    ang = (pos[:, None] * freq[None, :].astype(np.float32)).astype(np.float32)
    i = np.arange(P) % RD
    cos, sin = np.cos(ang)[:, i % half].T, np.sin(ang)[:, i % half].T
    sin = np.where(i[:, None] < half, -sin, sin)
    return np.stack([cos, sin]).reshape(2, P, HALVES, T).transpose(2, 0, 1, 3).astype(np.float32)


def kernel(**inputs):
    import numpy as np
    import concourse.bacc as bacc
    from concourse.bass_utils import run_bass_kernel_spmd

    a = {k: np.asarray(v) for k, v in inputs.items()}
    w_in, w_out = a["w_in"], a["w_out"]
    at = np.cumsum([0, MW, MW, MH, MH, RW, RW, RW, RW, GW, GW])
    o_mx, o_z, o_i, o_f, o_rq, o_rk, o_rv, o_rg, o_gu, o_gv = at[:-1]
    units = np.zeros((DEPTH * LAYER_UNITS + 1, P, KT * P), np.float32)
    for l in range(DEPTH):
        gates = np.zeros((D, P), np.float32)
        gates[:, 0:MH] = w_in[l][:, o_i:o_i + MH]
        gates[:, 32:32 + MH] = w_in[l][:, o_f:o_f + MH]
        tiles = [gates]
        for o, nt in ((o_mx, MT), (o_gv, GT), (o_gu, GT), (o_z, MT), (o_rq, MT), (o_rk, MT), (o_rg, MT), (o_rv, MT)):
            tiles += [w_in[l][:, o + P * t:o + P * t + P] for t in range(nt)]
        tiles += [w_out[l][:, P * t:P * t + P] for t in range(KT)]
        for i, w in enumerate(tiles):
            units[l * LAYER_UNITS + i] = _unit(w)
    for l in range(DEPTH):
        for g in range(GROUPS):
            at = l * LAYER_UNITS + len(HALF_UNITS) + len(GROUP_UNITS) * g
            for j in range(FG):
                f = (g * FG + j) * P
                units[at + j] = _unit(a["w_ff1"][l][:, f:f + P])
            rows = a["w_ff2"][l][g * FG * P:(g + 1) * FG * P].reshape(FG, P, 4, 2 * P)
            units[at + FG:at + 2 * FG] = rows.transpose(2, 1, 0, 3).reshape(4, P, KT * P)
    small = np.zeros((DEPTH, P, N_SMALL), np.float32)

    def put(name, v, r0=0):
        c0, c1 = SMALL[name]
        v = v.reshape(DEPTH, v.shape[1], -1)
        small[:, r0:r0 + v.shape[1], c0:c1] = v

    def tiles_of(v):
        return v.reshape(DEPTH, -1, P).transpose(0, 2, 1)

    put("g_mix", tiles_of(a["norm_mix_g"]))
    put("g_ff", tiles_of(a["norm_ff_g"]))
    put("conv_w", a["m_conv_w"].reshape(DEPTH, 4, MT, P).transpose(0, 3, 2, 1))
    put("conv_b", tiles_of(a["m_conv_b"]))
    put("skip", tiles_of(a["m_skip"]))
    put("m_norm", tiles_of(a["m_norm_g"]))
    put("r_norm", tiles_of(a["r_norm_g"]))
    put("i_bias", a["m_i_bias"][:, :, None])
    put("f_bias", a["m_f_bias"][:, :, None], 32)
    for name, key in (("wq", "m_wq"), ("wk", "m_wk"), ("wv", "m_wv")):
        put(name, a[key].reshape(DEPTH, MT, P, 4).transpose(0, 2, 1, 3))
    bs = a["g_bs"].reshape(DEPTH, GT, 2, 1, L)
    put("bs", np.broadcast_to(bs, (DEPTH, GT, 2, GD, L)).transpose(0, 2, 3, 1, 4).reshape(DEPTH, P, -1))
    put("g_norm", np.broadcast_to(a["g_norm_g"][:, None, :], (DEPTH, P, GW)))
    put("ws", a["g_ws"].transpose(0, 3, 1, 2))
    const = _constants(np)
    const[:, CONST["final_g"][0]:CONST["final_g"][1]] = a["final_norm_g"].reshape(KT, P).T
    x_t = a["x"][0].T.reshape(KT, P, S).transpose(1, 0, 2)

    nc = bacc.Bacc("TRN2", target_bir_lowering=False, num_devices=1,
                   dynamic_dma_scratch_size=1024)
    arrays, args = {}, []
    for name, v in (("x_t", x_t), ("units", units), ("small", small), ("const", const),
                    ("rope", _rope(np))):
        v = np.ascontiguousarray(v)
        arrays[name] = v
        args.append(nc.dram_tensor(name, v.shape, mybir.dt.from_np(v.dtype), kind="ExternalInput").ap())
    args.append(nc.dram_tensor("y_t", (P, KT, S), F32, kind="ExternalOutput").ap())
    trunk(nc, *args)
    r = run_bass_kernel_spmd(nc, [arrays], core_ids=[0])
    y = r.results[0]["y_t"]
    return np.ascontiguousarray(y.transpose(2, 1, 0).reshape(1, S, D))
```

```python
from contextlib import ExitStack

import concourse.bass as bass
from concourse import mybir
from concourse.alu_op_type import AluOpType as ALU

F32 = mybir.dt.float32
F32R = mybir.dt.float32r
ACT = mybir.ActivationFunctionType
AX_X = mybir.AxisListType.X

P = 128
D = 1024
S = 1024
DEPTH = 2
KT = D // P
T = 512
HALVES = S // T
L = 128
NC = T // L
MW = RW = 384
MT = MW // P
MH, MD = 4, 96
RH, RD = 6, 64
GW, GG, GD = 256, 4, 64
GT = GW // P
FF = 4096
FG = 4
GROUPS = FF // P // FG
EPS = 1e-6
BIG = 1.0e30

RING = 3
RAW = 2
U_GATE, U_MX, U_Z, U_RQ, U_RG, U_GU, U_RV, U_GV, U_OUT = 0, 1, 4, 7, 13, 16, 18, 21, 24
PADS = (23, 32)
HALF_UNITS = [u for u in range(33) if u not in PADS]
LAYER_UNITS = len(HALF_UNITS) + 8 * (FF // P // FG)
GROUP_UNITS = list(range(8))

PIECES = [(h, t) for h in range(MH) for t in range(MT) if max(MD * h, P * t) < min(MD * h + MD, P * t + P)]

SMALL = {}
_n = 0
for _name, _w in (("g_mix", KT), ("g_ff", KT), ("conv_w", 4 * MT), ("conv_b", MT), ("skip", MT), ("m_norm", MT),
                  ("r_norm", MT), ("i_bias", 1), ("f_bias", 1), ("wq", 4 * MT), ("wk", 4 * MT), ("wv", 4 * MT),
                  ("bs", GT * L), ("g_norm", GW), ("ws", GG * L)):
    SMALL[_name] = (_n, _n + _w)
    _n += _w
N_SMALL = _n

CONST = {}
_n = 0
for _name, _w in (("ones", P), ("eps", 1), ("one", 1), ("final_g", KT), ("upper", L), ("causal", L), ("blocks", L),
                  ("eye", P), ("decay", 2 * MT * L), ("xi", MT * L), ("gl", MT), ("zeta", RH),
                  ("sel", MH * P), ("eye4", 4), ("zero", L)):
    CONST[_name] = (_n, _n + _w)
    _n += _w
N_CONST = _n
N_NORM = CONST["upper"][0]

SECTIONS = ("pre", "half", "norm", "group")
TIMES = {"pre": 1, "half": HALVES, "norm": 1, "group": GROUPS}
RAISED = {
    "x0_loaded": (0, 0, 0, 0, 0),
    "x1_loaded": (0, 0, 0, 0, 0),
    "x2_loaded": (0, 0, 0, 0, 0),
    "ones_loaded": (0, 0, 0, 0, 0),
    "const_loaded": (0, 0, 0, 0, 0),
    "small_loaded": (0, 16, 0, 0, 0),
    "rope_loaded": (0, 0, 32, 0, 0),
    "raw0_full": (0, 0, 16 * 16, 0, 16 * 4),
    "raw1_full": (0, 0, 16 * 15, 0, 16 * 4),
    "hi_done": (0, 0, 33, 0, 9),
    "w_ready": (3, 0, 33, 0, 9),
    "pa_full": (0, 4, 44, 0, 8),
    "pa_taken": (4, 4, 44, 0, 8),
    "pv_full": (8, 0, 60, 4, 16),
    "pv_taken": (16, 0, 60, 4, 16),
    "sq_ready": (0, 8, 8, 0, 0),
    "sq_added": (0, 7, 7, 0, 0),
    "sqb_ready": (0, 0, 0, 8, 0),
    "sqb_added": (0, 0, 0, 7, 0),
    "rstd_ready": (0, 1, 1, 1, 0),
    "h_ready": (0, 8, 8, 8, 0),
    "hh_done": (0, 8, 8, 8, 0),
    "hl_ready": (1, 8, 8, 8, 0),
    "layer_ready": (0, 1, 0, 0, 0),
    "block_step": (0, 15, 0, 0, 0),
    "conv_done": (0, 0, 3, 0, 0),
    "xc_ready": (0, 0, 3, 0, 0),
    "rg_ready": (0, 0, 1, 0, 0),
    "x_added": (0, 0, 3, 0, 0),
    "gvu_ready": (0, 0, 1, 0, 0),
    "gu_ready": (0, 0, 2, 0, 0),
    "softplus_ready": (0, 0, 1, 0, 0),
    "rows_ready": (0, 0, 1, 0, 0),
    "rows_exp": (0, 0, 1, 0, 0),
    "sold_ready": (0, 0, 1, 0, 0),
    "gvn_ready": (0, 0, 1, 0, 0),
    "rot0_loaded": (0, 0, 64 * 3, 0, 0),
    "rot1_loaded": (0, 0, 64 * 3, 0, 0),
    "rqk_ready": (0, 0, 6, 0, 0),
    "e_ready": (0, 0, 4, 0, 0),
    "ss_ready": (0, 0, 9, 0, 0),
    "rs_ready": (0, 0, 9, 0, 0),
    "mn_ready": (0, 0, 4, 0, 0),
    "rn_ready": (0, 0, 4, 0, 0),
    "y_ready": (0, 0, 6, 0, 0),
    "oh_done": (0, 0, 10, 0, 0),
    "o_ready": (0, 0, 10, 0, 0),
    "sq_done": (0, 0, 0, 0, 8),
    "dh_done": (0, 0, 0, 0, 8),
    "hid_ready": (2, 0, 0, 0, 8),
    "dve_step": (0, 1, 82, 0, 0),
    "act_step": (0, 0, 11, 1, 0),
    "out_ready": (0, 0, 0, 0, 0),
    "stored": (0, 0, 0, 0, 0),
}


class Count:

    def __init__(self, sems, carried=None):
        self.carried = carried
        self.sems, self.mine, self.last = sems, {}, None
        self.section, self.base = None, None

    def enter(self, section, *regs):
        self.section, self.regs = section, regs
        self.last = ("pv_taken", 0)
        self.mine = {self.carried: 1} if self.carried and section in ("half", "group") else {}

    def value(self, name, k):
        start, *per = RAISED[name]
        if self.section is None:
            return k
        if self.section == "end":
            return start + DEPTH * sum(n * TIMES[s] for s, n in zip(SECTIONS, per)) + k
        whole = sum(n * TIMES[s] for s, n in zip(SECTIONS, per))
        at = SECTIONS.index(self.section)
        fixed = start + sum(n * TIMES[s] for s, n in zip(SECTIONS[:at], per[:at])) + k
        v = self.regs[0] * whole + fixed if whole else fixed
        if len(self.regs) > 1 and per[at]:
            v = self.regs[1] * per[at] + v
        return v

    def at(self, name, k):
        return self.sems[name], self.value(name, k)

    def up(self, name, n=1):
        self.mine[name] = self.mine.get(name, 0) + n
        self.last = (name, self.mine[name])
        return self.sems[name], n

    def own(self):
        return self.at(*self.last)

    def leave(self):
        at = 1 + SECTIONS.index(self.section)
        for name, n in self.mine.items():
            n -= name == self.carried
            assert RAISED[name][at] == n, f"{name} is raised {n} times in {self.section}"


def schedule():
    order = """gates0 gate_math mx0 mx1 mx2 gate_exp z0 xs0 z1 gate_tok xs1 xs2 z2 mq0 rqk0 ms0 rqk1 rot0 mn0
        rqk2 rot1 mt0 mq1 rqk3 rot2 ms1 rqk4 rot3 mn1 rqk5 rot4 mt1 mq2 rg0 rot5 ms2 rg1 mn2 rg2 rgs mt2 mq3
        gu0 ms3 gu1 mn3 rv0 rs0 mt3 rv1 rn0 rv2 rs1 rt0 rv3 rn1 gv0 rs2 rt1 gv1 rn2 gv2 rs3 rt2 gv3 gvs rn3 op0
        op1 rt3 g_sq op2 g_norm om0 g_mix om1 na0 na1 om2 na2 na3 oq0 na4 na5 oq1 na6 na7 oq2 out3 nsum nh0 nh1 out4
        nh2 nh3 out5 nh4 nh5 out6 nh6 out7 nh7"""
    steps = [(s[:-1], int(s[-1])) if s[-1].isdigit() else (s,) for s in order.split()]
    return steps


def units_of(step):
    kind, *a = step
    if kind == "gates":
        return [U_GATE]
    if kind == "gv":
        return [U_GV, U_GV + 1] if a[0] == 0 else []
    if kind == "rqk":
        return [U_RQ + a[0]]
    if kind == "rv":
        return [U_RV, U_RV + 1, U_RV + 2] if a[0] == 0 else []
    first = {"gu": U_GU, "mx": U_MX, "z": U_Z, "rg": U_RG, "out": U_OUT, "op": U_OUT}
    return [first[kind] + a[0]] if kind in first else []


def groups_of(step):
    return {"nsum": (1, 0), "na": (0, 0), "nh": (0, 0), "op": (1, 0), "om": (0, 0), "oq": (0, 0), "g_sq": (0, 0),
            "gate_math": (0, 0), "gate_exp": (0, 0), "gvs": (0, 0), "g_norm": (0, 0), "gate_tok": (0, 1), "rot": (0, 0),
            "g_mix": (0, GT), "mq": (3, 0), "ms": (0, 3), "mn": (0, 3), "mt": (0, 1), "rt": (0, 1), "rs": (0, 3),
            "rn": (0, 2), "out": (0, 1), "xs": (0, 0), "rgs": (0, 0)}.get(step[0], (1, 0))


def places(steps):
    at, out = [0, 0], {}
    for s in steps:
        out[s] = tuple(at)
        at = [x + y for x, y in zip(at, groups_of(s))]
    return out


PA_PADS, PV_PADS = 2, 0
AHEAD = 2


def splits_before(steps):
    after = lambda st: steps.index(st) + 1
    free = {U_RV + 1: after(("gu", GT - 1)), U_RV + 2: after(("gu", GT - 1)), U_GV: after(("rv", NC - 1)),
            U_GV + 1: after(("rv", NC - 1)), U_OUT: after(("gv", NC - 1)), U_OUT + 1: after(("gv", NC - 1)),
            U_OUT + 3: after(("oq", 0)), U_OUT + 4: after(("oq", 1))}
    order = [(i, u) for i, s in enumerate(steps) for u in units_of(s)]
    out = [[] for _ in steps]
    for n, (i, u) in enumerate(order):
        at = order[max(n - AHEAD, 0)][0] if n >= AHEAD else 0
        if u in (U_RV + 1, U_RV + 2):
            at = free[u]
        at = max(at, free.get(u, 0))
        out[at].append(u)
    return out


TILES = [(u, h) for u in range(FG) for h in range(HALVES)]
FIRST_TILES = [(u, h) for h in range(HALVES) for u in range(RING)] + [(u, h) for u in range(RING, FG)
                                                                     for h in range(HALVES)]


def group_splits(tiles):
    first = {u: min(e for e, (v, _) in enumerate(tiles) if v == u) for u in range(FG)}
    last = {u: max(e for e, (v, _) in enumerate(tiles) if v == u) for u in range(FG)}
    out = [[] for _ in tiles]
    for u in range(2, FG + 2):
        e = first[u - 2] if u - 2 in first else 0
        if u >= RING:
            e = max(e, last[u - RING] + 1)
        out[min(e, len(tiles) - 1)].append(u)
    return out


def trunk(nc, x_t, units_d, small_d, const_d, rope_d, out):
    ctx = ExitStack()
    with ctx:
        base = nc.sbuf_base
        ctx.enter_context(nc.sbuf_tensor("arena", [P, (nc.sbuf_bytes_remaining - 512) // 4], F32))
        origin = [base + (-base) % 32]

        def place(name, shape, dt=F32, at=None):
            size = 4
            for n in shape[1:]:
                size *= n
            size += (-size) % 32
            off = origin[0] if at is None else at
            if at is None:
                origin[0] += size
            return nc.alloc_sbuf_tensor_at(name, shape, dt, offset=off), off

        xT, _ = place("xT", [P, KT, S])
        hh, hh_at = place("hh", [P, KT, S], F32R)
        hl, hl_at = place("hl", [P, KT, S], F32R)
        raw, _ = place("raw", [P, RAW, KT * P])
        wh, _ = place("wh", [P, RING, KT, P], F32R)
        wl, _ = place("wl", [P, RING, KT, P], F32R)
        small, _ = place("small", [P, N_SMALL])
        const, _ = place("const", [P, N_CONST])
        bdq, _ = place("bdq", [P, len(PIECES), MD])
        bdk, _ = place("bdk", [P, len(PIECES), MD])
        bdv, _ = place("bdv", [P, MT, P])
        cst, _ = place("cst", [MD, MH, MD + 1])
        rst, _ = place("rst", [P, MT, P])
        hist, _ = place("hist", [P, MT, 3])
        mrow, _ = place("mrow", [MH, T])
        tok, _ = place("tok", [P, 80])
        mp, _ = place("mp", [MH, NC + 1])
        sold, _ = place("sold", [MH, NC])
        soldd, _ = place("soldd", [MH, MH, NC])
        dn, _ = place("dn", [P, 8])
        ms_, _ = place("msum", [P, 8])
        mrs, _ = place("mrs", [P, 8])
        rss_, _ = place("rsum", [P, 8])
        rrs, _ = place("rrs", [P, 8])
        pool_at = origin[0]
        rv, _ = place("rv", [P, NC, RW])
        xc, xc_at = place("xc", [P, MT, T])
        zt, zt_at = place("zt", [P, MT, T])
        rg, _ = place("rg", [P, MT, T])
        mxp, mxp_at = place("mxp", [P, MT, T + 3])
        gv, _ = place("gv", [P, NC, GW], at=mxp_at)
        gy, _ = place("gy", [P, GT, T], at=xc_at)
        gsq, _ = place("gsq", [P, T], at=zt_at)
        rqk, rqk_at = place("rqk", [P, 2 * MT, T])
        hidh, _ = place("hidh", [P, FG, S], F32R, at=pool_at)
        hidl, _ = place("hidl", [P, FG, S], F32R, at=pool_at + 4 * FG * S)
        assert pool_at + 8 * FG * S <= rqk_at + 16 * T
        sq = [place(f"sq{b}", [P, 2, T], at=rqk_at + 8 * T * (1 - b))[0] for b in range(2)]
        rstd = [place(f"rstd{b}", [P, T], at=rqk_at + 16 * T + 4 * T * b)[0] for b in range(2)]
        chunk_at = origin[0]
        qT, q_at = place("qT", [MD, MH, L])
        kT, k_at = place("kT", [MD, MH, L])
        et, _ = place("et", [P, MH, L])
        ktok, _ = place("ktok", [P, MW])
        vx, _ = place("vx", [P, MH, MD + 1])
        num, _ = place("num", [P, MH, MD + 1])
        mn, _ = place("mn", [P, MW])
        my, _ = place("my", [P, MT, L])
        hf, _ = place("hf", [P, 2, T], at=origin[0])
        rsc = [place(f"rsc{p}", [P, MT, L])[0] for p in range(2)]
        rqx, _ = place("rqx", [P, MT, L])
        rkt, _ = place("rkt", [P, RW])
        ro, _ = place("ro", [P, RW])
        rn, _ = place("rn", [P, RW])
        ry, _ = place("ry", [P, MT, L])
        relu, _ = place("relu", [P, 2, T], at=chunk_at)
        sqh, _ = place("sqh", [P, 2, T], at=chunk_at + 8 * T)
        assert chunk_at + 16 * T <= origin[0]
        assert origin[0] <= nc.sbuf_usable_end, (origin[0], nc.sbuf_usable_end)
        oh, ol = hh[:, :, T:S], hl[:, :, T:S]

        def slot(name, shape, at, k, half):
            return place(name, shape, at=at + 4 * (k * S + half * T))[0]

        ra = slot("ra", [MH, T], hh_at, 0, 1)
        rsint = slot("rsint", [MH, T], hh_at, 1, 1)
        reend = slot("reend", [MH, T], hh_at, 2, 1)
        rem = slot("rem", [MH, T], hl_at, 0, 1)
        rbc = slot("rbc", [MH, T], hl_at, 1, 1)
        rtmp = slot("rtmp", [MH, T], hl_at, 2, 1)
        cos = slot("cos", [P, T], hh_at, 3, 1)
        sin = slot("sin", [P, T], hh_at, 4, 1)
        rot = [slot(f"rot{b}", [P, T], at, 5, 1) for b, at in enumerate((hh_at, hl_at))]
        gu = [slot(f"gu{t}", [P, T], hl_at, 2 * MT + t, 1) for t in range(GT)]
        rig = slot("rig", [MH, T], hl_at, 3, 1)
        rxf = slot("rxf", [MH, T], hl_at, 4, 1)
        pa = [ctx.enter_context(nc.psum_tensor(f"pa{i}", [P, 512], F32)) for i in range(4)]
        pv = [ctx.enter_context(nc.psum_tensor(f"pv{i}", [P, 512], F32)) for i in range(4)]

        sems = {n: ctx.enter_context(nc.semaphore(n)) for n in RAISED}

        def sm(name, k=None):
            a, b = SMALL[name]
            return small[:, a:b] if k is None else small[:, a + k:a + k + 1]

        def cn(name):
            a, b = CONST[name]
            return const[:, a:b]

        eye, ones = cn("eye"), cn("ones")
        decay = cn("decay").rearrange("p (e t l) -> p e t l", e=2, t=MT)
        xi = cn("xi").rearrange("p (t l) -> p t l", t=MT)
        sel = cn("sel").rearrange("p (h l) -> p h l", h=MH)
        ws = sm("ws").rearrange("p (g t) -> p g t", g=GG)
        atok = tok[:, 0:64].rearrange("p (c q h) -> p c q h", c=NC, q=4)
        soldb = tok[:, 64:80].rearrange("p (h c) -> p h c", h=MH)
        steps = schedule()
        ahead = splits_before(steps)
        before = places(steps)

        def nth(ring, step, j=1):
            return before[step]["pa pv".split().index(ring)] + j

        numbered = {}
        for names, kinds in (("ss", ("g_norm", "mn", "rn")), ("o", ("g_mix", "mt", "rt")), ("y", ("g_mix", "mt")),):
            k = 0
            for st in steps:
                if st[0] in kinds:
                    numbered[names, st] = k
                    k += GT if st[0] == "g_mix" else 1
        ends = {}
        for st in steps:
            for u in units_of(st):
                if st[0] in ("rv", "gv"):
                    ends[u] = ("pa_full", nth("pa", (st[0], NC - 1)))
                elif st[0] == "op":
                    ends[u] = ("pa_full", nth("pa", st))
                elif st[0] == "out":
                    ends[u] = ("pv_full", nth("pv", st))
                else:
                    ends[u] = ("pa_full", nth("pa", st, groups_of(st)[0]))
        def group_ends(tiles):
            return {u: ("pa_full", 1 + max(e for e, (v, _) in enumerate(tiles) if v == u)) if u < FG
                    else ("pv_full", 4 * (u - FG + 1)) for u in GROUP_UNITS}

        block = ctx.enter_context(nc.Block())

        def unit_at(index):
            return units_d[bass.ds(index, 1), :, :].rearrange("a p n -> (a p) n")

        @block.sync
        def _(sp):
            n = Count(sems)

            def load_unit(n, order, i, index):
                sp.wait_ge(*n.at("w_ready", 0 if i < RAW else order[i - RAW] + 1))
                sp.dma_start(raw[:, i % RAW, :], unit_at(index)).then_inc(*n.up(f"raw{i % RAW}_full", 16))

            def load_next(n, order, index):
                last = max(i for i in range(len(order)) if i % RAW == 0)
                sp.wait_ge(*n.at("w_ready", order[last] + 1))
                sp.dma_start(raw[:, 0, :], unit_at(index)).then_inc(*n.up("raw0_full", 16))

            sp.dma_start(const[:, 0:N_NORM], const_d[:, 0:N_NORM]).then_inc(*n.up("ones_loaded", 16))
            for j in range(2):
                q = slice(KT // 2 * j, KT // 2 * (j + 1))
                sp.dma_start(xT[:, q, 0:T], x_t[:, q, 0:T]).then_inc(*n.up(f"x{j}_loaded", 16))
            sp.dma_start(raw[:, 0, :], units_d[0, :, :]).then_inc(*n.up("raw0_full", 16))
            with sp.Fori(0, DEPTH) as layer:
                n.enter("pre", layer)
                sp.wait_ge(*n.at("hl_ready", 0))
                sp.dma_start(small[:, :], small_d[bass.ds(layer, 1), :, :].rearrange("a p n -> (a p) n")
                             ).then_inc(*n.up("small_loaded", 16))
                n.leave()
                for half in range(HALVES):
                    n.enter("half", layer, half)
                    for i, u in enumerate(HALF_UNITS):
                        if i:
                            load_unit(n, HALF_UNITS, i, layer * LAYER_UNITS + i)
                        if u == U_MX:
                            sp.wait_ge(*n.at("pv_full", 0))
                            for j, dst in enumerate((cos, sin)):
                                sp.dma_start(dst[:, :], rope_d[half, j, :, :]).then_inc(*n.up("rope_loaded", 16))
                    load_next(n, HALF_UNITS, layer * LAYER_UNITS + half * len(HALF_UNITS))
                    n.leave()
                def group_loads(group):
                    n.enter("group", layer, group)
                    first = group * len(GROUP_UNITS) + (layer * LAYER_UNITS + len(HALF_UNITS))
                    for i in GROUP_UNITS[1:]:
                        load_unit(n, GROUP_UNITS, i, first + i)
                    load_next(n, GROUP_UNITS, first + len(GROUP_UNITS))
                    n.leave()

                group_loads(0)
                with sp.Fori(1, GROUPS) as group:
                    group_loads(group)
            n.enter("end")
            for h in range(HALVES):
                for j in range(0, KT, 2):
                    sp.wait_ge(*n.at("out_ready", KT * h + j + 2))
                    sp.dma_start(out[:, j:j + 2, T * h:T * h + T], xT[:, j:j + 2, T * h:T * h + T]
                                 ).then_inc(*n.up("stored", 16))
            sp.wait_ge(*n.at("stored", 16 * KT // 2 * HALVES))

        @block.tensor
        def _(pe):
            n = Count(sems)
            rings, parts = {}, {}

            def bank(ring, taken=-4):
                k = rings[ring] = rings.get(ring, 0) + 1
                pe.wait_ge(*n.at(f"{ring}_taken", max(k - 4, taken)))
                return (pa if ring == "pa" else pv)[(k - 1) % 4]

            def norm_sum(name, k, b, pads=0):
                ps = bank("pa")
                pe.wait_ge(*n.at(name, k))
                pe.matmul(ps[:, :], ones, rstd[b][:, :], start=True, stop=True).then_inc(*n.up("pa_full", 1 + pads))

            def feature_tile(u, ring, hready=False):
                ps = bank(ring)
                pe.wait_ge(*n.at("w_ready", u + 1))
                for k in range(KT):
                    if hready:
                        pe.wait_ge(*n.at("hl_ready", k + 1 - KT))
                    pe.matmul(ps[:, :], wh[:, u % RING, k, :], hh[:, k, 0:T], start=(k == 0), stop=False)
                    pe.matmul(ps[:, :], wh[:, u % RING, k, :], hl[:, k, 0:T], start=False, stop=False)
                    ins = pe.matmul(ps[:, :], wl[:, u % RING, k, :], hh[:, k, 0:T], start=False, stop=(k == KT - 1))
                ins.then_inc(*n.up(f"{ring}_full"))
                return ins

            pe.sem_inc(sems["pv_full"], RAISED["pv_full"][0])
            pe.wait_ge(sems["ones_loaded"], 16)
            with pe.Fori(0, DEPTH) as layer:
                n.enter("pre", layer)
                rings.clear()
                norm_sum("sq_added", KT - 1, 0, 3)
                n.leave()
                for half in range(HALVES):
                    n.enter("half", layer, half)
                    rings.clear()
                    for step in steps:
                        kind, *a = step
                        c = a[0] if a else 0
                        tk = slice(L * c, L * c + L)
                        if kind == "nsum":
                            norm_sum("sq_added", KT - 1, 0, PA_PADS)
                        elif kind in ("gates", "gu", "mx", "z", "rg", "rqk"):
                            feature_tile(units_of(step)[0], "pa", kind == "gates")
                        elif kind in ("gv", "rv"):
                            u, cols = (U_GV, GT) if kind == "gv" else (U_RV, MT)
                            ps = bank("pa")
                            pe.wait_ge(*n.at("w_ready", u + cols))
                            s0 = u % RING
                            o = ps[:, 0:cols * P].rearrange("p (u n) -> p u n", u=cols)
                            for k in range(KT):
                                pe.matmul(o, hh[:, k, tk], wh[:, s0:s0 + cols, k, :], start=(k == 0), stop=False)
                                pe.matmul(o, hh[:, k, tk], wl[:, s0:s0 + cols, k, :], start=False, stop=False)
                                ins = pe.matmul(o, hl[:, k, tk], wh[:, s0:s0 + cols, k, :], start=False,
                                                stop=(k == KT - 1))
                            ins.then_inc(*n.up("pa_full"))
                        elif kind == "gate_tok":
                            ps = bank("pv")
                            pe.wait_ge(sems["const_loaded"], 16)
                            pe.wait_ge(*n.at("sold_ready", 1))
                            pe.matmul(ps[:, 64:80], ones[0:MH, :], soldd[:, :, :], start=True, stop=True)
                            for cc in range(NC):
                                for q, row in enumerate((ra, rsint, reend, rem)):
                                    at = 4 * (4 * cc + q)
                                    ins = pe.transpose(ps[:, at:at + 4], row[:, L * cc:L * cc + L], eye[0:MH, 0:MH])
                            ins.then_inc(*n.up("pv_full"))
                        elif kind == "g_mix":
                            for t in range(GT):
                                ps = bank("pv")
                                pe.wait_ge(*n.at("gvn_ready", 1))
                                for cc in range(NC):
                                    for g in (2 * t, 2 * t + 1):
                                        q = GD * (g % 2)
                                        ins = pe.matmul(ps[q:q + GD, L * cc:L * cc + L],
                                                        gv[:, cc, GD * g:GD * g + GD], ws[:, g, :],
                                                        start=True, stop=True)
                                ins.then_inc(*n.up("pv_full"))
                        elif kind == "mq":
                            if c == 0:
                                pe.wait_ge(*n.at("xc_ready", MT))
                                pe.wait_ge(*n.at("layer_ready", 0))
                            for bd in (bdq, bdk):
                                ps = bank("pa")
                                for h in range(MH):
                                    ts = [i for i, (hd, _) in enumerate(PIECES) if hd == h]
                                    for i in ts:
                                        ins = pe.matmul(ps[0:MD, L * h:L * h + L], bd[:, i, :],
                                                        xc[:, PIECES[i][1], tk],
                                                        start=(i == ts[0]), stop=(i == ts[-1]))
                                ins.then_inc(*n.up("pa_full"))
                            ps = bank("pa")
                            for t in range(MT):
                                ins = pe.matmul(ps[:, P * t:P * t + P], mxp[:, t, 3 + L * c:3 + L * c + L],
                                                bdv[:, t, :], start=True, stop=True)
                            ins.then_inc(*n.up("pa_full"))
                        elif kind == "ms":
                            ps = bank("pv")
                            for h in range(MH):
                                ins = pe.matmul(ps[:, L * h:L * h + L], sel[0:MH, h, :], mrow[:, tk],
                                                start=True, stop=True)
                            ins.then_inc(*n.up("pv_full"))
                            ps = bank("pv")
                            pe.wait_ge(*n.at("pa_taken", nth("pa", ("mq", c), 3)))
                            for h in range(MH):
                                ins = pe.matmul(ps[:, L * h:L * h + L], kT[:, h, :], qT[:, h, :],
                                                start=True, stop=True)
                            ins.then_inc(*n.up("pv_full"))
                            ps = bank("pv")
                            for h in range(MH):
                                ins = pe.transpose(ps[:, MD * h:MD * h + MD], kT[:, h, :], eye[0:MD, 0:MD])
                            ins.then_inc(*n.up("pv_full"))
                        elif kind == "mn":
                            w = MD + 1
                            ps = bank("pv", nth("pv", ("mn", c - 1), 3) if c else -4)
                            for h in range(MH):
                                ins = pe.matmul(ps[:, w * h:w * h + w], qT[:, h, :], cst[:, h, :],
                                                start=True, stop=True)
                            ins.then_inc(*n.up("pv_full"))
                            ps = bank("pv", nth("pv", ("ms", c), 2))
                            for h in range(MH):
                                ins = pe.matmul(ps[:, w * h:w * h + w], et[:, h, :], vx[:, h, :],
                                                start=True, stop=True)
                            ins.then_inc(*n.up("pv_full"))
                            ps = bank("pv", nth("pv", ("ms", c), 3))
                            for h in range(MH):
                                ins = pe.matmul(ps[0:MD, w * h:w * h + w], ktok[:, MD * h:MD * h + MD], vx[:, h, :],
                                                start=True, stop=True)
                            ins.then_inc(*n.up("pv_full"))
                        elif kind in ("mt", "rt"):
                            ps = bank("pv")
                            src, name = (mn, "mn_ready") if kind == "mt" else (rn, "rn_ready")
                            pe.wait_ge(*n.at(name, c + 1))
                            for t in range(MT):
                                ins = pe.transpose(ps[:, P * t:P * t + P], src[:, P * t:P * t + P], eye)
                            ins.then_inc(*n.up("pv_full"))
                        elif kind == "rs":
                            if c == 0:
                                pe.wait_ge(*n.at("rqk_ready", 2 * MT))
                            for p in range(2):
                                ps = bank("pv")
                                for t in range(MT):
                                    ins = pe.matmul(ps[:, L * t:L * t + L], rqk[RD * p:RD * p + RD, MT + t, tk],
                                                    rqk[RD * p:RD * p + RD, t, tk], start=True, stop=True)
                                ins.then_inc(*n.up("pv_full"))
                            ps = bank("pv")
                            for t in range(MT):
                                ins = pe.transpose(ps[:, P * t:P * t + P], rqk[:, MT + t, tk], eye)
                            ins.then_inc(*n.up("pv_full"))
                        elif kind == "rn":
                            ps = bank("pv", max(nth("pv", ("rs", c), 3), nth("pv", ("rn", c - 1), 2) if c else 0))
                            pe.wait_ge(*n.at("pa_taken", nth("pa", ("rv", c))))
                            for t in range(MT):
                                pe.matmul(ps[:, P * t:P * t + P], rqx[:, t, :], rst[:, t, :], start=True, stop=False)
                                for p in range(2):
                                    q = P * t + RD * p
                                    ins = pe.matmul(ps[:, q:q + RD], rsc[p][:, t, :], rv[:, c, q:q + RD],
                                                    start=False, stop=(p == 1))
                            ins.then_inc(*n.up("pv_full"))
                            ps = bank("pv")
                            for t in range(MT):
                                ins = pe.matmul(ps[:, P * t:P * t + P], rkt[:, P * t:P * t + P],
                                                rv[:, c, P * t:P * t + P], start=True, stop=True)
                            ins.then_inc(*n.up("pv_full"))
                        elif kind in ("out", "op", "om", "oq"):
                            u = U_OUT + c
                            if kind in ("om", "oq"):
                                ps = parts[c]
                                pe.wait_ge(*n.at("o_ready", 10 if kind == "oq" else 10 - GT))
                            else:
                                ps = bank("pv" if kind == "out" else "pa")
                                pe.wait_ge(*n.at("w_ready", u + 1))
                            if kind == "op":
                                parts[c] = ps
                                pe.wait_ge(*n.at("o_ready", 1 + max(numbered["o", ("mt", cc)] for cc in range(NC))))
                            for k in {"out": range(KT), "op": range(MT), "om": range(MT, 2 * MT),
                                      "oq": range(2 * MT, KT)}[kind]:
                                pe.matmul(ps[:, :], wh[:, u % RING, k, :], oh[:, k, :], start=(k == 0), stop=False)
                                pe.matmul(ps[:, :], wh[:, u % RING, k, :], ol[:, k, :], start=False, stop=False)
                                ins = pe.matmul(ps[:, :], wl[:, u % RING, k, :], oh[:, k, :], start=False,
                                                stop=(k == KT - 1))
                            if kind == "out":
                                ins.then_inc(*n.up("pv_full", 1 + PV_PADS * (c == KT - 1)))
                            elif kind == "oq":
                                ins.then_inc(*n.up("pa_full"))
                    n.leave()

                def group_products(group, tiles):
                    n.enter("group", layer, group)
                    rings.clear()
                    for e, (u, h) in enumerate(tiles):
                        s0, th = u % RING, slice(T * h, T * h + T)
                        first = u == min(v for v, g in tiles if g == h)
                        ps = bank("pa")
                        pe.wait_ge(*n.at("w_ready", u + 1))
                        for k in range(KT):
                            if first and tiles is FIRST_TILES:
                                pe.wait_ge(*n.at("hl_ready", k + 1 - KT * (HALVES - h)))
                            a, b = wh[:, s0, k, :], wl[:, s0, k, :]
                            pe.matmul(ps[:, :], a, hh[:, k, th], start=(k == 0), stop=False)
                            pe.matmul(ps[:, :], a, hl[:, k, th], start=False, stop=False)
                            ins = pe.matmul(ps[:, :], b, hh[:, k, th], start=False, stop=(k == KT - 1))
                        ins.then_inc(*n.up("pa_full"))
                        if e == 0 and tiles is FIRST_TILES:
                            later = Count(sems)
                            later.enter("norm", layer)
                            pe.wait_ge(*later.at("pv_taken", -3))
                            pe.wait_ge(*later.at("sqb_added", KT - 1))
                            pe.matmul(pv[0][:, :], ones, rstd[1][:, :], start=True, stop=True
                                      ).then_inc(*later.up("pv_full", 4))
                            later.leave()
                    for u in range(FG, 2 * FG):
                        s0 = u % RING
                        pe.wait_ge(*n.at("w_ready", u + 1))
                        for m in range(2):
                            for h in range(HALVES):
                                th = slice(T * h, T * h + T)
                                ps = bank("pv")
                                for k in range(FG):
                                    if u == FG and m == 0:
                                        pe.wait_ge(*n.at("hid_ready", tiles.index((k, h)) + 1))
                                    a, b = (w[:, s0, 2 * k + m, :] for w in (wh, wl))
                                    pe.matmul(ps[:, :], a, hidh[:, k, th], start=(k == 0), stop=False)
                                    pe.matmul(ps[:, :], a, hidl[:, k, th], start=False, stop=False)
                                    ins = pe.matmul(ps[:, :], b, hidh[:, k, th], start=False, stop=(k == FG - 1))
                                ins.then_inc(*n.up("pv_full"))
                    n.leave()

                group_products(0, FIRST_TILES)
                with pe.Fori(1, GROUPS) as group:
                    group_products(group, TILES)
            n.enter("end")
            rings.clear()
            norm_sum("sq_added", KT - 1, 0)
            ps = bank("pa")
            for k in range(KT):
                pe.wait_ge(*n.at("sqb_ready", k + 1))
                ins = pe.matmul(ps[:, :], ones, sq[1][:, k % 2, :] if k else rstd[1][:, :], start=(k == 0),
                                stop=(k == KT - 1))
                if 0 < k < KT - 1:
                    ins.then_inc(*n.up("sqb_added"))
            ins.then_inc(*n.up("pa_full"))

        @block.scalar
        def _(act):
            n = Count(sems, "hi_done")
            later = Count(sems)
            eps, one = cn("eps"), cn("one")

            def round_unit(order, slot_ends, u, after_norm=0):
                i = order.index(u)
                act.wait_ge(*n.at(f"raw{i % RAW}_full", 16 * (i // RAW + 1)))
                if u >= RING:
                    act.wait_ge(*n.at(*slot_ends[u - RING if u - RING in order else u - 2 * RING]))
                elif u:
                    act.wait_ge(*n.at("pv_full", (0, -PV_PADS - 2)[u - 1] - after_norm))
                act.activation(wh[:, u % RING, :, :].rearrange("p k n -> p (k n)"), raw[:, i % RAW, :], ACT.Copy
                               ).then_inc(*n.up("hi_done", 1 if u + 1 in order else 2))

            def round_next(order, slot_ends):
                act.wait_ge(*n.at("raw0_full", 16 * (1 + (len(order) + 1) // RAW)))
                act.wait_ge(*n.at(*slot_ends[max(u for u in order if u % RING == 0)]))
                act.activation(wh[:, 0, :, :].rearrange("p k n -> p (k n)"), raw[:, 0, :], ACT.Copy
                               ).then_inc(*n.up("hi_done"))

            def inv_rms(dst, src, width, name, wait_own=True):
                act.activation(dst, src, ACT.Ln, bias=eps, scale=1.0 / width).then_inc(*n.up("act_step"))
                act.wait_ge(*n.own())
                act.activation(dst, dst, ACT.Exp, scale=-0.5).then_inc(*n.up(name))

            def square(n, k, b, cols, names=("sq_ready", "sq_added")):
                if k >= 3:
                    act.wait_ge(*n.at(names[1], k - 2))
                act.activation(sq[b][:, k % 2, :] if k else rstd[b][:, :], xT[:, k, cols], ACT.Square
                               ).then_inc(*n.up(names[0]))

            def x_done(k, h):
                return HALVES * k + h + 1 - HALVES * KT

            def inv_norm(k, b, pads=0):
                act.wait_ge(*n.at("pa_full", k))
                act.activation(rstd[b][:, :], pa[(k - 1) % 4][:, :], ACT.Ln, bias=eps, scale=1.0 / D
                               ).then_inc(*n.up("pa_taken", 1 + pads))
                act.wait_ge(*n.own())
                act.activation(rstd[b][:, :], rstd[b][:, :], ACT.Exp, scale=-0.5).then_inc(*n.up("rstd_ready"))

            def round_h(n, k, th):
                act.wait_ge(*n.at("h_ready", k + 1))
                act.activation(hh[:, k, th], hf[:, k % 2, :], ACT.Copy).then_inc(*n.up("hh_done"))

            def take(step, dst, func, j=1, rows=slice(0, P), cols=slice(0, 512), shape=None, pads=0, **kw):
                k = nth("pa", step, j)
                act.wait_ge(*n.at("pa_full", k))
                src = pa[(k - 1) % 4][rows, cols]
                if shape:
                    src = src.rearrange(shape[0], **shape[1])
                act.activation(dst, src, func, **kw).then_inc(*n.up("pa_taken", 1 + pads))

            act.sem_inc(sems["pa_taken"], RAISED["pa_taken"][0])
            act.wait_ge(sems["x1_loaded"], 16)
            act.dma_start(const[:, N_NORM:], const_d[:, N_NORM:]).then_inc(sems["const_loaded"], 16)
            act.dma_start(xT[:, :, T:S], x_t[:, :, T:S]).then_inc(sems["x2_loaded"], 16)
            round_unit(HALF_UNITS, ends, 0)
            act.preload_act_table_set("natural_log_exp_and_others")
            with act.Fori(0, DEPTH) as layer:
                n.enter("pre", layer)
                for k in range(KT):
                    act.wait_ge(*n.at("pv_taken", x_done(k, 0)))
                    if k % (KT // 2) == 0:
                        act.wait_ge(sems[f"x{k // (KT // 2)}_loaded"], 16)
                    square(n, k, 0, slice(0, T))
                act.wait_ge(sems["ones_loaded"], 16)
                inv_norm(1, 0, 3)
                for k in range(KT):
                    round_h(n, k, slice(0, T))
                n.leave()
                for half in range(HALVES):
                    later.enter("norm", layer)
                    n.enter("half", layer, half)
                    for i, step in enumerate(steps):
                        for u in ahead[i]:
                            if u:
                                round_unit(HALF_UNITS, ends, u)
                        if step == ("out", KT - 1):
                            round_next(HALF_UNITS, ends)
                        kind, *a = step
                        c = a[0] if a else 0
                        tk = slice(L * c, L * c + L)
                        other = slice(T, S) if half == 0 else slice(0, T)
                        if kind == "na":
                            if c == 0:
                                act.wait_ge(*n.at("pv_taken", nth("pv", ("rs", NC - 1), 3)))
                                act.wait_ge(sems["x2_loaded"], 16)
                            square(n, c, 0, other)
                        elif kind == "nsum":
                            inv_norm(nth("pa", step), 0, PA_PADS)
                        elif kind == "nh":
                            round_h(n, c, slice(0, T))
                        elif kind in ("out", "oq"):
                            if kind == "oq":
                                take(("op", c), zt[:, c, :], ACT.Copy)
                            if half == HALVES - 1:
                                act.wait_ge(*(n.at("pv_taken", nth("pv", step)) if kind == "out" else
                                              n.at("x_added", c + 1)))
                                square(later, c, 1, slice(T, S), names=("sqb_ready", "sqb_added"))
                        elif kind == "gates":
                            k = nth("pa", step)
                            act.wait_ge(*n.at("small_loaded", 0))
                            act.wait_ge(*n.at("pa_full", k))
                            ps = pa[(k - 1) % 4]
                            act.activation(rig[:, :], ps[0:MH, :], ACT.Identity, bias=sm("i_bias")[0:MH, :])
                            act.activation(rxf[:, :], ps[32:32 + MH, :], ACT.Identity, bias=sm("f_bias")[32:32 + MH, :]
                                           ).then_inc(*n.up("pa_taken"))
                        elif kind == "gv":
                            take(step, gv[:, c, :], ACT.Copy, cols=slice(0, GW))
                        elif kind == "gu":
                            take(step, gu[c][:, :], ACT.Copy)
                        elif kind == "gvs":
                            act.wait_ge(*n.at("pa_taken", nth("pa", ("gv", NC - 1))))
                            act.activation(gv[:, :, :], gv[:, :, :], ACT.Gelu_apprx_tanh).then_inc(*n.up("gvu_ready"))
                            for t in range(GT):
                                act.activation(gu[t][:, :], gu[t][:, :], ACT.Gelu_apprx_tanh
                                               ).then_inc(*n.up("gu_ready"))
                            act.preload_act_table_set("natural_log_exp_and_others")
                        elif kind == "mx":
                            take(step, mxp[:, c, 3:3 + T], ACT.Copy)
                        elif kind == "z":
                            take(step, zt[:, c, :], ACT.Silu)
                        elif kind == "rg":
                            take(step, rg[:, c, :], ACT.Copy)
                        elif kind == "xs":
                            act.wait_ge(*n.at("conv_done", c + 1))
                            act.activation(xc[:, c, :], xc[:, c, :], ACT.Silu).then_inc(*n.up("xc_ready"))
                        elif kind == "rgs":
                            act.wait_ge(*n.at("pa_taken", nth("pa", ("rg", MT - 1))))
                            act.activation(rg[:, :, :], rg[:, :, :], ACT.Silu).then_inc(*n.up("rg_ready"))
                            act.preload_act_table_set("natural_log_exp_and_others")
                        elif kind == "gate_math":
                            act.wait_ge(*n.at("pa_taken", nth("pa", ("gates", 0))))
                            act.activation(rtmp[:, :], rxf[:, :], ACT.Abs).then_inc(*n.up("act_step"))
                            act.wait_ge(*n.own())
                            act.activation(rtmp[:, :], rtmp[:, :], ACT.Exp, scale=-1.0).then_inc(*n.up("act_step"))
                            act.wait_ge(*n.own())
                            act.activation(rtmp[:, :], rtmp[:, :], ACT.Ln, bias=one[0:MH, :]
                                           ).then_inc(*n.up("softplus_ready"))
                        elif kind == "gate_exp":
                            act.wait_ge(*n.at("rows_ready", 1))
                            for row in (rsint, reend, rem):
                                act.activation(row[:, :], row[:, :], ACT.Exp)
                            act.activation(sold[:, :], sold[:, :], ACT.Exp).then_inc(*n.up("rows_exp"))
                        elif kind in ("g_norm", "mn", "rn"):
                            k, w, src, dst = {"g_norm": (NC, GW, ms_, mrs), "mn": (MH, MD, ms_, mrs),
                                              "rn": (RH, RD, rss_, rrs)}[kind]
                            act.wait_ge(*n.at("ss_ready", numbered["ss", step] + 1))
                            inv_rms(dst[:, 0:k], src[:, 0:k], w, "rs_ready")
                        elif kind == "rqk":
                            take(step, rqk[:, c, :], ACT.Copy)
                            act.wait_ge(*n.at("pa_taken", nth("pa", step)))
                            if c >= 2:
                                act.wait_ge(*n.at("rqk_ready", c - 1))
                            for b in range(P // 32):
                                to, of = slice(32 * b, 32 * b + 32), slice(32 * (b ^ 1), 32 * (b ^ 1) + 32)
                                act.dma_start(rot[c % 2][to, :], rqk[of, c, :]
                                              ).then_inc(*n.up(f"rot{c % 2}_loaded", 16))
                        elif kind == "rv":
                            take(step, rv[:, c, :], ACT.Copy, cols=slice(0, RW))
                        elif kind == "mq":
                            for j, (dst, scale) in enumerate(((qT, 1.0), (kT, MD ** -0.5))):
                                take(step, dst[:, :, :], ACT.Copy, j=j + 1, rows=slice(0, MD),
                                     shape=("p (h l) -> p h l", {"h": MH}), scale=scale)
                            take(step, vx[:, :, 0:MD], ACT.Copy, j=3, cols=slice(0, MW),
                                 shape=("p (h d) -> p h d", {"h": MH}))
                        elif kind == "ms":
                            if c == 0:
                                act.preload_act_table_set("natural_log_exp_and_others")
                            act.wait_ge(*n.at("pv_taken", nth("pv", step)))
                            act.activation(et[:, :, :], et[:, :, :], ACT.Exp).then_inc(*n.up("e_ready"))
                        if kind == "g_mix":
                            for t in range(GT):
                                act.wait_ge(*n.at("y_ready", numbered["y", step] + t + 1))
                                act.activation(oh[:, 2 * MT + t, :], gy[:, t, :], ACT.Copy).then_inc(*n.up("oh_done"))
                        elif kind == "mt":
                            act.wait_ge(*n.at("y_ready", numbered["y", step] + 1))
                            act.activation(oh[:, 0:MT, tk], my[:, :, :], ACT.Copy).then_inc(*n.up("oh_done"))
                        elif kind == "rt":
                            act.wait_ge(*n.at("pv_taken", nth("pv", step)))
                            act.activation(oh[:, MT:2 * MT, tk], ry[:, :, :], ACT.Copy).then_inc(*n.up("oh_done"))
                    n.leave()

                def group_rounds(group, tiles):
                    n.enter("group", layer, group)
                    slot_ends, ahead = group_ends(tiles), group_splits(tiles)
                    norm_banks = 4 if tiles is FIRST_TILES else 0
                    round_unit(GROUP_UNITS, slot_ends, 1, norm_banks)
                    if tiles is FIRST_TILES:
                        act.wait_ge(*later.at("pv_full", 4))
                        act.activation(rstd[1][:, :], pv[0][:, :], ACT.Ln, bias=eps, scale=1.0 / D
                                       ).then_inc(*later.up("act_step"))
                        act.wait_ge(*later.own())
                        act.activation(rstd[1][:, :], rstd[1][:, :], ACT.Exp, scale=-0.5
                                       ).then_inc(*later.up("rstd_ready"))
                        for k in range(KT):
                            round_h(later, k, slice(T, S))
                            if k == 2:
                                round_unit(GROUP_UNITS, slot_ends, 2, norm_banks)

                    def round_square(e):
                        u, h = tiles[e]
                        act.wait_ge(*n.at("sq_done", e + 1))
                        act.activation(hidh[:, u, T * h:T * h + T], sqh[:, e % 2, :], ACT.Copy
                                       ).then_inc(*n.up("dh_done"))

                    for e, (u, h) in enumerate(tiles):
                        for u in ahead[e]:
                            if u != 2 or tiles is TILES:
                                round_unit(GROUP_UNITS, slot_ends, u)
                        act.wait_ge(*n.at("pa_full", e + 1))
                        act.activation(relu[:, e % 2, :], pa[e % 4][:, :], ACT.Relu).then_inc(*n.up("pa_taken"))
                        if e:
                            round_square(e - 1)
                    round_square(2 * FG - 1)
                    for u in (FG + 2, FG + 3):
                        round_unit(GROUP_UNITS, slot_ends, u)
                    round_next(GROUP_UNITS, slot_ends)
                    n.leave()

                group_rounds(0, FIRST_TILES)
                later.leave()
                with act.Fori(1, GROUPS) as group:
                    group_rounds(group, TILES)
            n.enter("end")
            for h in range(HALVES):
                for k in range(KT):
                    act.wait_ge(*n.at("pv_taken", 0 if h else x_done(k, 0)))
                    square(n, k, h, slice(T * h, T * h + T), names=("sqb_ready", "sqb_added") if h else
                           ("sq_ready", "sq_added"))
                inv_norm(h + 1, h)

        @block.vector
        def _(dve):
            n = Count(sems, "w_ready")
            later = Count(sems)

            def rest_unit(order, u):
                i = order.index(u)
                dve.wait_ge(*n.at("hi_done", u + 1))
                dve.tensor_tensor(wl[:, u % RING, :, :].rearrange("p k n -> p (k n)"), raw[:, i % RAW, :],
                                  wh[:, u % RING, :, :].bitcast(F32).rearrange("p k n -> p (k n)"), ALU.subtract
                                  ).then_inc(*n.up("w_ready", 1 if u + 1 in order else 2))

            def rest_next(order):
                dve.wait_ge(*n.at("hi_done", order[-1] + 3))
                dve.tensor_tensor(wl[:, 0, :, :].rearrange("p k n -> p (k n)"), raw[:, 0, :],
                                  wh[:, 0, :, :].bitcast(F32).rearrange("p k n -> p (k n)"), ALU.subtract
                                  ).then_inc(*n.up("w_ready"))

            def add_square(n, k, b, names=("sq_ready", "sq_added")):
                if k == 0:
                    return
                dve.wait_ge(*n.at(names[0], k + 1))
                if k > 1:
                    dve.wait_ge(*n.at(names[1], k - 1))
                dve.tensor_tensor(rstd[b][:, :], rstd[b][:, :], sq[b][:, k % 2, :], ALU.add
                                  ).then_inc(*n.up(names[1]))

            def make_h(n, k, b, cols, th, g):
                if k == 0:
                    dve.wait_ge(*n.at("rstd_ready", 1))
                dve.wait_ge(*n.own())
                dve.scalar_tensor_tensor(hf[:, k % 2, :], xT[:, k, cols], g[:, k:k + 1], rstd[b][:, :],
                                         ALU.mult, ALU.mult).then_inc(*n.up("h_ready"))
                for j in range(max(k - 1, 0), k + (k == KT - 1)):
                    dve.wait_ge(*n.at("hh_done", j + 1))
                    dve.tensor_tensor(hl[:, j, th], hf[:, j % 2, :], hh[:, j, th].bitcast(F32), ALU.subtract
                                      ).then_inc(*n.up("hl_ready"))

            def step_done(ins):
                ins.then_inc(*n.up("dve_step"))
                dve.wait_ge(*n.own())

            def go():
                dve.wait_ge(*n.own())

            def full(step, j=1):
                k = nth("pv", step, j)
                dve.wait_ge(*n.at("pv_full", k))
                return pv[(k - 1) % 4]

            def rest_output(step, dst, src, j=0):
                dve.wait_ge(*n.at("oh_done", numbered["o", step] + j + 1))
                dve.tensor_tensor(ol[:, dst[0], dst[1]], src, oh[:, dst[0], dst[1]].bitcast(F32), ALU.subtract
                                  ).then_inc(*n.up("o_ready"))

            for name in ("w_ready", "pv_taken", "hl_ready", "hid_ready"):
                dve.sem_inc(sems[name], RAISED[name][0])
            rest_unit(HALF_UNITS, 0)
            with dve.Fori(0, DEPTH) as layer:
                n.enter("pre", layer)
                for k in range(KT):
                    add_square(n, k, 0)
                for bd in (bdq, bdk):
                    dve.memset(bd[:, :, :], 0.0)
                for buf in (bdv, cst, rst, hist):
                    dve.memset(buf[:, :, :], 0.0)
                dve.memset(mp[:, :], 0.0)
                step_done(dve.memset(vx[:, :, MD:MD + 1], 1.0))
                dve.wait_ge(*n.at("small_loaded", 16))
                for k in range(KT):
                    make_h(n, k, 0, slice(0, T), slice(0, T), sm("g_mix"))
                dve.wait_ge(sems["const_loaded"], 16)
                n.leave()
                for half in range(HALVES):
                    later.enter("norm", layer)
                    n.enter("half", layer, half)
                    dve.wait_ge(*n.at("pv_taken", 0))
                    for i, step in enumerate(steps):
                        for u in ahead[i]:
                            if u:
                                rest_unit(HALF_UNITS, u)
                        if step == ("out", KT - 1):
                            rest_next(HALF_UNITS)
                        kind, *a = step
                        c = a[0] if a else 0
                        tk = slice(L * c, L * c + L)
                        other = slice(T, S) if half == 0 else slice(0, T)
                        xcols = slice(half * T, half * T + T)
                        if step == ("z", 0) and half == 0:
                            layer_count = Count(sems)
                            layer_count.enter("pre", layer)
                            blocks = cn("blocks")
                            for bd, name in ((bdq, "wq"), (bdk, "wk")):
                                w = sm(name).rearrange("p (t j) -> p t j", j=4)
                                for i, (h, t) in enumerate(PIECES):
                                    lo, hi = max(MD * h, P * t), min(MD * h + MD, P * t + P)
                                    nb = (hi - lo) // 4
                                    dve.tensor_tensor(
                                        bd[:, i, lo - MD * h:hi - MD * h].rearrange("p (n j) -> p n j", j=4),
                                        blocks[:, lo - P * t:hi - P * t].rearrange("p (n j) -> p n j", j=4),
                                        w[:, t:t + 1, :].broadcast_to([P, nb, 4]), ALU.mult).then_inc(*layer_count.up("block_step"))
                            w = sm("wv").rearrange("p (t j) -> p t j", j=4)
                            for t in range(MT):
                                dve.tensor_tensor(bdv[:, t, :].rearrange("p (n j) -> p n j", j=4),
                                                  blocks.rearrange("p (n j) -> p n j", j=4),
                                                  w[:, t:t + 1, :].broadcast_to([P, P // 4, 4]), ALU.mult
                                                  ).then_inc(*layer_count.up("block_step"))
                            dve.tensor_tensor(ws, ws, cn("causal").rearrange("p (a l) -> p a l", a=1).broadcast_to([P, GG, L]),
                                              ALU.mult).then_inc(*layer_count.up("layer_ready"))
                            layer_count.leave()
                        if kind == "na":
                            add_square(n, c, 0)
                        elif kind == "nh":
                            make_h(n, c, 0, other, slice(0, T), sm("g_ff" if half else "g_mix"))
                        elif kind == "mx":
                            dve.wait_ge(*n.at("pa_taken", nth("pa", step)))
                            go()
                            dve.tensor_copy(mxp[:, c, 0:3], hist[:, c, :]).then_inc(*n.up("dve_step"))
                            go()
                            step_done(dve.tensor_copy(hist[:, c, :], mxp[:, c, T:T + 3]))
                            w = sm("conv_w")
                            step_done(dve.tensor_scalar(xc[:, c, :], mxp[:, c, 0:T], w[:, 4 * c:4 * c + 1],
                                                        sm("conv_b", c), ALU.mult, ALU.add))
                            for j in range(1, 4):
                                ins = dve.scalar_tensor_tensor(xc[:, c, :], mxp[:, c, j:j + T],
                                                               w[:, 4 * c + j:4 * c + j + 1], xc[:, c, :],
                                                               ALU.mult, ALU.add)
                                if j < 3:
                                    step_done(ins)
                            ins.then_inc(*n.up("conv_done"))
                        elif kind == "gate_math":
                            go()
                            v3 = lambda r: r[:, :].rearrange("h (c l) -> h c l", c=NC)
                            dve.wait_ge(*n.at("softplus_ready", 1))
                            step_done(dve.scalar_tensor_tensor(rtmp[:, :], rxf[:, :], 0.0, rtmp[:, :],
                                                               ALU.min, ALU.subtract))
                            for cc in range(NC):
                                t = slice(L * cc, L * cc + L)
                                ins = dve.tensor_tensor_scan(rbc[:, t], rtmp[:, t], cn("zero")[0:MH, :], 0.0,
                                                             ALU.add, ALU.add)
                            step_done(ins)
                            dve.tensor_copy(mp[:, 0:1], mp[:, NC:NC + 1]).then_inc(*n.up("dve_step"))
                            step_done(dve.tensor_tensor(ra[:, :], rig[:, :], rbc[:, :], ALU.subtract))
                            for cc in range(NC):
                                t, e = slice(L * cc, L * cc + L), L * cc + L - 1
                                step_done(dve.tensor_tensor_scan(mrow[:, t], ra[:, t], ra[:, t], mp[:, cc:cc + 1],
                                                                 ALU.max, ALU.max))
                                step_done(dve.tensor_tensor(mp[:, cc + 1:cc + 2], mrow[:, e:e + 1], rbc[:, e:e + 1],
                                                            ALU.add))
                            ends_m = v3(mrow)[:, :, L - 1:L]
                            dve.tensor_tensor(v3(rsint), mp[:, 0:NC].rearrange("h (c a) -> h c a", a=1).broadcast_to(
                                [MH, NC, L]), v3(mrow), ALU.subtract)
                            dve.tensor_tensor(v3(reend), v3(ra), ends_m.broadcast_to([MH, NC, L]), ALU.subtract)
                            dve.scalar_tensor_tensor(rem[:, :], rbc[:, :], -1.0, mrow[:, :], ALU.mult, ALU.subtract)
                            dve.tensor_tensor(sold[:, :], mp[:, 0:NC], ends_m.rearrange("h c a -> h (c a)"),
                                              ALU.subtract).then_inc(*n.up("rows_ready"))
                        elif kind == "gate_tok":
                            dve.wait_ge(*n.at("rows_exp", 1))
                            dve.tensor_tensor(
                                soldd[:, :, :], sold[:, :].rearrange("h (a c) -> h a c", a=1).broadcast_to([MH, MH, NC]),
                                cn("eye4")[0:MH, :].rearrange("h (g a) -> h g a", a=1).broadcast_to([MH, MH, NC]),
                                ALU.mult).then_inc(*n.up("sold_ready"))
                            ps = full(step)
                            go()
                            dve.tensor_copy(tok[:, :], ps[:, 0:80]).then_inc(*n.up("pv_taken"))
                        elif kind == "g_sq":
                            dve.wait_ge(*n.at("gvu_ready", 1))
                            for b in range(2):
                                s2 = gsq[:, :].rearrange("p (c n) -> p c n", c=2)
                                go()
                                step_done(dve.tensor_tensor(s2, gv[:, 2 * b:2 * b + 2, :], gv[:, 2 * b:2 * b + 2, :],
                                                            ALU.mult))
                                dve.tensor_reduce(ms_[:, 2 * b:2 * b + 2], s2, AX_X, ALU.add
                                                  ).then_inc(*n.up("ss_ready" if b else "dve_step"))
                        elif kind == "g_norm":
                            dve.wait_ge(*n.at("rs_ready", numbered["ss", step] + 1))
                            for cc in range(NC):
                                ins = dve.scalar_tensor_tensor(gv[:, cc, :], gv[:, cc, :], mrs[:, cc:cc + 1],
                                                               sm("g_norm"), ALU.mult, ALU.mult)
                            ins.then_inc(*n.up("gvn_ready"))
                        elif kind == "rot":
                            if c == 0:
                                dve.wait_ge(*n.at("rope_loaded", 32))
                            dve.wait_ge(*n.at(f"rot{c % 2}_loaded", 64 * (c // 2 + 1)))
                            dve.tensor_tensor(rot[c % 2][:, :], rot[c % 2][:, :], sin[:, :], ALU.mult
                                              ).then_inc(*n.up("dve_step"))
                            step_done(dve.tensor_tensor(rqk[:, c, :], rqk[:, c, :], cos[:, :], ALU.mult))
                            dve.tensor_tensor(rqk[:, c, :], rqk[:, c, :], rot[c % 2][:, :], ALU.add
                                              ).then_inc(*n.up("rqk_ready"))
                        elif kind == "g_mix":
                            bs = sm("bs").rearrange("p (t a l) -> p t a l", t=GT, a=1)
                            go()
                            for t in range(GT):
                                ps = full(step, t + 1)
                                y = gy[:, t, :].rearrange("p (c l) -> p c l", c=NC)
                                dve.tensor_tensor(y, ps[:, :].rearrange("p (c l) -> p c l", c=NC),
                                                  bs[:, t, :, :].broadcast_to([P, NC, L]), ALU.add
                                                  ).then_inc(*n.up("pv_taken"))
                                dve.wait_ge(*n.own())
                                dve.wait_ge(*n.at("gu_ready", GT))
                                dve.tensor_tensor(gy[:, t, :], gy[:, t, :], gu[t][:, :], ALU.mult
                                                  ).then_inc(*n.up("y_ready"))
                            for t in range(GT):
                                rest_output(step, (2 * MT + t, slice(0, T)), gy[:, t, :], t)
                        elif kind == "ms":
                            ps = full(step)
                            go()
                            for h in range(MH):
                                ins = dve.scalar_tensor_tensor(et[:, h, :], ps[:, L * h:L * h + L],
                                                               atok[:, c, 0, h:h + 1], cn("upper"), ALU.add, ALU.min)
                            ins.then_inc(*n.up("pv_taken"))
                            dve.wait_ge(*n.at("e_ready", c + 1))
                            ps = full(step, 2)
                            dve.tensor_tensor(et[:, :, :], ps[:, :].rearrange("p (h l) -> p h l", h=MH), et[:, :, :],
                                              ALU.mult).then_inc(*n.up("pv_taken"))
                            ps = full(step, 3)
                            dve.tensor_tensor(
                                ktok[:, :].rearrange("p (h d) -> p h d", h=MH),
                                ps[:, 0:MW].rearrange("p (h d) -> p h d", h=MH),
                                atok[:, c, 2, :].rearrange("p (h a) -> p h a", a=1).broadcast_to([P, MH, MD]),
                                ALU.mult).then_inc(*n.up("pv_taken"))
                        elif kind == "mn":
                            w = MH * (MD + 1)
                            heads = lambda ap: ap.rearrange("p (h d) -> p h d", h=MH)
                            wide = lambda ap, m=P, d=MD + 1: ap.rearrange("p (h a) -> p h a", a=1).broadcast_to([m, MH, d])
                            ps = full(step)
                            go()
                            dve.tensor_tensor(num[:, :, :], heads(ps[:, 0:w]), wide(atok[:, c, 1, :]), ALU.mult
                                              ).then_inc(*n.up("pv_taken"))
                            ps = full(step, 2)
                            dve.wait_ge(*n.own())
                            dve.tensor_tensor(num[:, :, :], heads(ps[:, 0:w]), num[:, :, :], ALU.add
                                              ).then_inc(*n.up("pv_taken"))
                            dve.wait_ge(*n.own())
                            step_done(dve.scalar_tensor_tensor(dn[:, 0:MH], num[:, :, MD], -1.0, num[:, :, MD],
                                                               ALU.mult, ALU.max))
                            step_done(dve.tensor_tensor(dn[:, 0:MH], dn[:, 0:MH], atok[:, c, 3, :], ALU.max))
                            step_done(dve.reciprocal(dn[:, 4:4 + MH], dn[:, 0:MH]))
                            step_done(dve.tensor_tensor(num[:, :, 0:MD], num[:, :, 0:MD], wide(dn[:, 4:4 + MH], d=MD),
                                                        ALU.mult))
                            step_done(dve.tensor_tensor(heads(mn[:, :]), num[:, :, 0:MD], num[:, :, 0:MD], ALU.mult))
                            dve.tensor_reduce(ms_[:, 0:MH], heads(mn[:, :]), AX_X, ALU.add
                                              ).then_inc(*n.up("ss_ready"))
                            step_done(dve.tensor_tensor(cst[:, :, :], cst[:, :, :], soldb[0:MD, :, c:c + 1].broadcast_to(
                                [MD, MH, MD + 1]), ALU.mult))
                            ps = full(step, 3)
                            dve.tensor_tensor(cst[:, :, :], heads(ps[0:MD, 0:w]), cst[:, :, :], ALU.add
                                              ).then_inc(*n.up("pv_taken"))
                            dve.wait_ge(*n.at("rs_ready", numbered["ss", step] + 1))
                            dve.tensor_tensor(heads(mn[:, :]), num[:, :, 0:MD], wide(mrs[:, 0:MH], d=MD), ALU.mult
                                              ).then_inc(*n.up("mn_ready"))
                        elif kind == "mt":
                            ps = full(step)
                            go()
                            for t in range(MT):
                                ins = dve.tensor_scalar(my[:, t, :], ps[:, P * t:P * t + P], sm("m_norm", t), None,
                                                        ALU.mult)
                            ins.then_inc(*n.up("pv_taken"))
                            dve.wait_ge(*n.own())
                            for t in range(MT):
                                ins = dve.scalar_tensor_tensor(my[:, t, :], xc[:, t, tk], sm("skip", t), my[:, t, :],
                                                               ALU.mult, ALU.add)
                            step_done(ins)
                            dve.tensor_tensor(my[:, :, :], my[:, :, :], zt[:, :, tk], ALU.mult
                                              ).then_inc(*n.up("y_ready"))
                            rest_output(step, (slice(0, MT), tk), my[:, :, :])
                        elif kind == "rs":
                            for p in range(2):
                                ps = full(step, p + 1)
                                if p == 0:
                                    go()
                                    dve.tensor_tensor(rqx[:, :, :], rqk[:, 0:MT, tk], xi, ALU.mult)
                                dve.tensor_tensor(rsc[p][:, :, :], ps[:, 0:MT * L].rearrange("p (t l) -> p t l", t=MT),
                                                  decay[:, p, :, :], ALU.mult).then_inc(*n.up("pv_taken"))
                            ps = full(step, 3)
                            dve.tensor_tensor(
                                rkt[:, :].rearrange("p (h d) -> p h d", h=RH),
                                ps[:, 0:RW].rearrange("p (h d) -> p h d", h=RH),
                                cn("zeta").rearrange("p (h a) -> p h a", a=1).broadcast_to([P, RH, RD]), ALU.mult
                                ).then_inc(*n.up("pv_taken"))
                        elif kind == "rn":
                            heads = lambda ap: ap.rearrange("p (h d) -> p h d", h=RH)
                            ps = full(step)
                            go()
                            step_done(dve.tensor_copy(ro[:, :], ps[:, 0:RW]))
                            step_done(dve.tensor_tensor(rn[:, :], ro[:, :], ro[:, :], ALU.mult))
                            dve.tensor_reduce(rss_[:, 0:RH], heads(rn[:, :]), AX_X, ALU.add).then_inc(*n.up("ss_ready"))
                            step_done(dve.tensor_tensor(rst[:, :, :], rst[:, :, :], cn("gl").rearrange(
                                "p (t a) -> p t a", a=1).broadcast_to([P, MT, P]), ALU.mult))
                            ps = full(step, 2)[:, 0:RW].rearrange("p (t n) -> p t n", t=MT)
                            for p in range(2):
                                q = slice(RD * p, RD * p + RD)
                                ins = dve.tensor_tensor(rst[q, :, q], ps[q, :, q], rst[q, :, q], ALU.add)
                            ins.then_inc(*n.up("pv_taken", 2))
                            dve.wait_ge(*n.at("rs_ready", numbered["ss", step] + 1))
                            dve.tensor_tensor(heads(rn[:, :]), heads(ro[:, :]), rrs[:, 0:RH].rearrange(
                                "p (h a) -> p h a", a=1).broadcast_to([P, RH, RD]), ALU.mult
                                ).then_inc(*n.up("rn_ready"))
                        elif kind == "rt":
                            if c == 0:
                                dve.wait_ge(*n.at("rg_ready", 1))
                            ps = full(step)
                            go()
                            for t in range(MT):
                                ins = dve.scalar_tensor_tensor(ry[:, t, :], ps[:, P * t:P * t + P], sm("r_norm", t),
                                                               rg[:, t, tk], ALU.mult, ALU.mult)
                            ins.then_inc(*n.up("pv_taken"))
                            rest_output(step, (slice(MT, 2 * MT), tk), ry[:, :, :])
                        elif kind in ("out", "oq"):
                            if kind == "out":
                                ps = full(step)
                                go()
                                dve.tensor_tensor(xT[:, c, xcols], ps[:, :], xT[:, c, xcols], ALU.add
                                                  ).then_inc(*n.up("pv_taken", 1 + PV_PADS * (c == KT - 1)))
                            else:
                                dve.wait_ge(*n.at("pa_taken", nth("pa", ("op", c))))
                                dve.tensor_tensor(xT[:, c, xcols], zt[:, c, :], xT[:, c, xcols], ALU.add
                                                  ).then_inc(*n.up("x_added"))
                            if half == HALVES - 1:
                                for k in [c - 1] if c < KT - 1 else [c - 1, c]:
                                    if k > 0:
                                        add_square(later, k, 1, names=("sqb_ready", "sqb_added"))
                    n.leave()

                def group_rests(group, tiles):
                    n.enter("group", layer, group)
                    ahead = group_splits(tiles)
                    rest_unit(GROUP_UNITS, 1)
                    if tiles is FIRST_TILES:
                        for k in range(KT):
                            make_h(later, k, 1, slice(T, S), slice(T, S), sm("g_ff"))
                            if k == 0:
                                dve.sem_inc(*later.up("pv_taken", 4))
                                later.last = ("h_ready", 1)
                            if k == 2:
                                rest_unit(GROUP_UNITS, 2)

                    def rest_square(e):
                        u, h = tiles[e]
                        dve.wait_ge(*n.at("dh_done", e + 1))
                        th = slice(T * h, T * h + T)
                        dve.tensor_tensor(hidl[:, u, th], sqh[:, e % 2, :], hidh[:, u, th].bitcast(F32), ALU.subtract
                                          ).then_inc(*n.up("hid_ready"))

                    for e in range(len(tiles)):
                        for u in ahead[e]:
                            if u != 2 or tiles is TILES:
                                rest_unit(GROUP_UNITS, u)
                        dve.wait_ge(*n.at("pa_taken", e + 1))
                        dve.wait_ge(*n.at("hid_ready", e - 1))
                        dve.tensor_tensor(sqh[:, e % 2, :], relu[:, e % 2, :], relu[:, e % 2, :], ALU.mult
                                          ).then_inc(*n.up("sq_done"))
                        if e:
                            rest_square(e - 1)
                    rest_square(2 * FG - 1)
                    for q in range(KT // 2):
                        if q < 2:
                            rest_unit(GROUP_UNITS, FG + 2 + q)
                        for j in range(4):
                            m, th = 2 * q + j // 2, slice(T * (j % 2), T * (j % 2) + T)
                            if q == KT // 2 - 1 and j == 1:
                                rest_next(GROUP_UNITS)
                            k = 4 * q + j
                            dve.wait_ge(*n.at("pv_full", k + 1))
                            dve.tensor_tensor(xT[:, m, th], pv[k % 4][:, :], xT[:, m, th], ALU.add
                                              ).then_inc(*n.up("pv_taken"))
                    n.leave()

                group_rests(0, FIRST_TILES)
                later.leave()
                with dve.Fori(1, GROUPS) as group:
                    group_rests(group, TILES)
            n.enter("end")

            def scale(h):
                th = slice(T * h, T * h + T)
                dve.wait_ge(*n.at("rstd_ready", h + 1))
                for k in range(KT):
                    dve.scalar_tensor_tensor(xT[:, k, th], xT[:, k, th], cn("final_g")[:, k:k + 1], rstd[h][:, :],
                                             ALU.mult, ALU.mult).then_inc(*n.up("out_ready"))

            for h in range(HALVES):
                if h == 0:
                    for k in range(KT):
                        add_square(n, k, 0)
                scale(h)


def _unit(w):
    return w.reshape(KT, P, P).transpose(1, 0, 2).reshape(P, KT * P)


def _constants(np):
    c = np.zeros((P, N_CONST), np.float32)

    def put(name, v):
        a, b = CONST[name]
        v = np.asarray(v, np.float32)
        v = v.reshape(v.shape[0], -1)
        c[:v.shape[0], a:b] = v

    i = np.arange(P)
    put("upper", np.where(i[:, None] <= i[None, :], 0.0, -BIG))
    put("causal", i[:, None] <= i[None, :])
    put("blocks", i[:, None] // 4 == i[None, :] // 4)
    put("eye", np.eye(P))
    put("ones", np.ones((P, P)))
    lg = np.log(1.0 - 2.0 ** (-5.0 - np.arange(RH)))
    heads = np.stack([2 * np.arange(MT) + p for p in range(2)])
    rel = np.maximum(i[None, :] - i[:, None], 0)
    put("decay", np.stack([[np.where(i[:, None] <= i[None, :], np.exp(rel * lg[h]), 0.0) * RD ** -0.5 for h in r]
                           for r in heads]).transpose(2, 0, 1, 3))
    mine = heads[i // RD]
    put("xi", np.exp(lg[mine][:, :, None] * (i + 1.0)))
    put("gl", np.exp(L * lg[mine]))
    put("zeta", np.exp((L - 1.0 - i)[:, None] * lg[None, :]) * RD ** -0.5)
    put("sel", -np.repeat(np.eye(MH)[:, :, None], P, 2))
    put("eye4", np.eye(MH))
    put("eps", np.full((P, 1), EPS))
    put("one", np.ones((P, 1)))
    return c


def _rope(np):
    half = RD // 2
    pos = np.arange(S, dtype=np.float32)
    freq = np.float32(10000.0) ** (-np.arange(half, dtype=np.float32) / np.float32(half))
    ang = (pos[:, None] * freq[None, :].astype(np.float32)).astype(np.float32)
    i = np.arange(P) % RD
    cos, sin = np.cos(ang)[:, i % half].T, np.sin(ang)[:, i % half].T
    sin = np.where(i[:, None] < half, -sin, sin)
    return np.stack([cos, sin]).reshape(2, P, HALVES, T).transpose(2, 0, 1, 3).astype(np.float32)


def kernel(**inputs):
    import numpy as np
    import concourse.bacc as bacc
    from concourse.bass_utils import run_bass_kernel_spmd

    a = {k: np.asarray(v) for k, v in inputs.items()}
    w_in, w_out = a["w_in"], a["w_out"]
    at = np.cumsum([0, MW, MW, MH, MH, RW, RW, RW, RW, GW, GW])
    o_mx, o_z, o_i, o_f, o_rq, o_rk, o_rv, o_rg, o_gu, o_gv = at[:-1]
    units = np.zeros((DEPTH * LAYER_UNITS + 1, P, KT * P), np.float32)
    for l in range(DEPTH):
        gates = np.zeros((D, P), np.float32)
        gates[:, 0:MH] = w_in[l][:, o_i:o_i + MH]
        gates[:, 32:32 + MH] = w_in[l][:, o_f:o_f + MH]
        tiles = [gates]
        for o, nt in ((o_mx, MT), (o_z, MT), (o_rq, MT), (o_rk, MT), (o_rg, MT), (o_gu, GT), (o_rv, MT),
                      (o_gv, GT)):
            tiles += [w_in[l][:, o + P * t:o + P * t + P] for t in range(nt)]
        tiles += [w_out[l][:, P * t:P * t + P] for t in range(KT)]
        for i, w in enumerate(tiles):
            units[l * LAYER_UNITS + i] = _unit(w)
    for l in range(DEPTH):
        for g in range(GROUPS):
            at = l * LAYER_UNITS + len(HALF_UNITS) + len(GROUP_UNITS) * g
            for j in range(FG):
                f = (g * FG + j) * P
                units[at + j] = _unit(a["w_ff1"][l][:, f:f + P])
            rows = a["w_ff2"][l][g * FG * P:(g + 1) * FG * P].reshape(FG, P, 4, 2 * P)
            units[at + FG:at + 2 * FG] = rows.transpose(2, 1, 0, 3).reshape(4, P, KT * P)
    small = np.zeros((DEPTH, P, N_SMALL), np.float32)

    def put(name, v, r0=0):
        c0, c1 = SMALL[name]
        v = v.reshape(DEPTH, v.shape[1], -1)
        small[:, r0:r0 + v.shape[1], c0:c1] = v

    def tiles_of(v):
        return v.reshape(DEPTH, -1, P).transpose(0, 2, 1)

    put("g_mix", tiles_of(a["norm_mix_g"]))
    put("g_ff", tiles_of(a["norm_ff_g"]))
    put("conv_w", a["m_conv_w"].reshape(DEPTH, 4, MT, P).transpose(0, 3, 2, 1))
    put("conv_b", tiles_of(a["m_conv_b"]))
    put("skip", tiles_of(a["m_skip"]))
    put("m_norm", tiles_of(a["m_norm_g"]))
    put("r_norm", tiles_of(a["r_norm_g"]))
    put("i_bias", a["m_i_bias"][:, :, None])
    put("f_bias", a["m_f_bias"][:, :, None], 32)
    for name, key in (("wq", "m_wq"), ("wk", "m_wk"), ("wv", "m_wv")):
        put(name, a[key].reshape(DEPTH, MT, P, 4).transpose(0, 2, 1, 3))
    bs = a["g_bs"].reshape(DEPTH, GT, 2, 1, L)
    put("bs", np.broadcast_to(bs, (DEPTH, GT, 2, GD, L)).transpose(0, 2, 3, 1, 4).reshape(DEPTH, P, -1))
    put("g_norm", np.broadcast_to(a["g_norm_g"][:, None, :], (DEPTH, P, GW)))
    put("ws", a["g_ws"].transpose(0, 3, 1, 2))
    const = _constants(np)
    const[:, CONST["final_g"][0]:CONST["final_g"][1]] = a["final_norm_g"].reshape(KT, P).T
    x_t = a["x"][0].T.reshape(KT, P, S).transpose(1, 0, 2)

    nc = bacc.Bacc("TRN2", target_bir_lowering=False, num_devices=1,
                   dynamic_dma_scratch_size=1024)
    arrays, args = {}, []
    for name, v in (("x_t", x_t), ("units", units), ("small", small), ("const", const),
                    ("rope", _rope(np))):
        v = np.ascontiguousarray(v)
        arrays[name] = v
        args.append(nc.dram_tensor(name, v.shape, mybir.dt.from_np(v.dtype), kind="ExternalInput").ap())
    args.append(nc.dram_tensor("y_t", (P, KT, S), F32, kind="ExternalOutput").ap())
    trunk(nc, *args)
    r = run_bass_kernel_spmd(nc, [arrays], core_ids=[0])
    y = r.results[0]["y_t"]
    return np.ascontiguousarray(y.transpose(2, 1, 0).reshape(1, S, D))
```
